# Optimizing a Trainium2 kernel written in Bass

```python
import math
import jax, jax.numpy as jnp
from jax import lax
import numpy as np

D_MODEL = 1024
BATCH = 1
SEQ = 512
DEPTH = 1

GRID_W = 64
NA_HEADS = 8
NA_HEAD_DIM = 64
NA_WIDTH = NA_HEADS * NA_HEAD_DIM
NA_KH_MAX = 8
NA_KW = 16
HY_WIDTH = 512
HY_ORDER = 2
HY_SHORT_K = 3
HY_EMB_DIM = 33
HY_FILTER_HIDDEN = 64
HY_FAST_DECAY_PCT = 0.3
HY_SLOW_DECAY_PCT = 1.5
HY_DECAY_TARGET = 1e-2
N_DIR = 2
N_BRANCH = 2
D_FF = 2816
QKV_COLS = 3 * NA_WIDTH
HY_COLS = (HY_ORDER + 1) * HY_WIDTH
GATE_COLS = N_BRANCH * D_MODEL
IN_COLS = QKV_COLS + HY_COLS + GATE_COLS
DN_ALPHA = (2 * DEPTH) ** 0.25
DN_BETA = (8 * DEPTH) ** -0.25
LN_EPS = 1e-5

kernel_name = 'hybrid_na2d_hyena_macaron_deepnorm'

def layer_norm(x, g, b):
    xf = x.astype(jnp.float32)
    mu = jnp.mean(xf, axis=-1, keepdims=True)
    var = jnp.mean(jnp.square(xf - mu), axis=-1, keepdims=True)
    return ((xf - mu) * lax.rsqrt(var + LN_EPS)).astype(x.dtype) * g + b

def swiglu(x, w1, w3, w2):
    return (jax.nn.silu(x @ w1) * (x @ w3)) @ w2

def _window_starts(n, k):
    return np.clip(np.arange(n) - k // 2, 0, n - k)

def neighbourhood_attention_2d(q, k, v, rpb):
    b, L, h, dh = q.shape
    rows = L // GRID_W
    kh = min(NA_KH_MAX, rows)
    kw = NA_KW
    grid = lambda t: t.reshape(b, rows, GRID_W, h, dh).transpose(0, 3, 1, 2, 4)
    qg, kg, vg = grid(q), grid(k), grid(v)
    row_idx = _window_starts(rows, kh)[:, None] + np.arange(kh)[None, :]
    col_idx = _window_starts(GRID_W, kw)[:, None] + np.arange(kw)[None, :]
    k_band = kg[:, :, row_idx]
    v_band = vg[:, :, row_idx]
    col_sel = jax.nn.one_hot(col_idx, GRID_W, dtype=q.dtype)
    s_band = jnp.einsum('bhrqd,bhrakd->bhrqak', qg, k_band)
    s = jnp.einsum('bhrqak,qjk->bhrqaj', s_band, col_sel)
    dr = row_idx - np.arange(rows)[:, None] + (NA_KH_MAX - 1)
    dc = col_idx - np.arange(GRID_W)[:, None] + (NA_KW - 1)
    bias = rpb[:, dr[:, None, :, None], dc[None, :, None, :]]
    s = s.astype(jnp.float32) * (dh ** -0.5) + bias[None].astype(jnp.float32)
    p = jax.nn.softmax(s.reshape(b, h, rows, GRID_W, kh * kw), axis=-1)
    p = p.reshape(b, h, rows, GRID_W, kh, kw).astype(v.dtype)
    p_band = jnp.einsum('bhrqaj,qjk->bhrqak', p, col_sel)
    o = jnp.einsum('bhrqak,bhrakd->bhrqd', p_band, v_band)
    return o.transpose(0, 2, 3, 1, 4).reshape(b, L, h * dh)

def _short_conv(u, w, bias):
    L = u.shape[1]
    pad = HY_SHORT_K // 2
    up = jnp.pad(u, ((0, 0), (pad, pad), (0, 0)))
    out = bias
    for j in range(HY_SHORT_K):
        out = out + w[j] * up[:, j:j + L]
    return out

def _hyena_filters(L, fw1, fb1, fw2, fb2, fw3, fb3, freq):
    f32 = jnp.float32
    t = jnp.linspace(0.0, 1.0, L, dtype=f32)[:, None]
    bands = (HY_EMB_DIM - 1) // 2
    w = (2.0 * math.pi / L) * jnp.arange(L, dtype=f32)[:, None]
    f = jnp.linspace(1e-4, bands - 1, bands, dtype=f32)[None, :]
    z = jnp.concatenate([t, jnp.cos(f * w), -jnp.sin(f * w)], axis=-1)
    fr = freq.astype(f32)
    hdn = jnp.sin(fr * (z @ fw1.astype(f32) + fb1.astype(f32)))
    hdn = jnp.sin(fr * (hdn @ fw2.astype(f32) + fb2.astype(f32)))
    hf = hdn @ fw3.astype(f32) + fb3.astype(f32)
    hf = hf.reshape(L, N_DIR, HY_ORDER, HY_WIDTH)
    max_decay = math.log(HY_DECAY_TARGET) / HY_FAST_DECAY_PCT
    min_decay = math.log(HY_DECAY_TARGET) / HY_SLOW_DECAY_PCT
    deltas = jnp.abs(jnp.linspace(min_decay, max_decay, HY_WIDTH, dtype=f32))
    decay = jnp.exp(-t[:, :, None, None] * deltas)
    return hf * decay

def _two_sided_kernels(h):
    fwd, bwd = h[:, 0], h[:, 1]
    k = jnp.concatenate([fwd, jnp.zeros_like(fwd[:1]), bwd[1:][::-1]], axis=0)
    return k * lax.rsqrt(jnp.sum(jnp.square(k), axis=0, keepdims=True) + 1e-12)

def _fft_conv(z, k):
    L = z.shape[1]
    Z = jnp.fft.rfft(z.astype(jnp.float32), n=2 * L, axis=1)
    K = jnp.fft.rfft(k.astype(jnp.float32), n=2 * L, axis=0)
    return jnp.fft.irfft(Z * K[None], n=2 * L, axis=1)[:, :L].astype(z.dtype)

def hyena_mixer(u, short_w, short_b, fw1, fb1, fw2, fb2, fw3, fb3, freq, hy_bias):
    L = u.shape[1]
    parts = jnp.split(_short_conv(u, short_w, short_b), HY_ORDER + 1, axis=-1)
    kern = _two_sided_kernels(_hyena_filters(L, fw1, fb1, fw2, fb2, fw3, fb3, freq))
    z = parts[0]
    for n in range(HY_ORDER):
        z = parts[n + 1] * (_fft_conv(z, kern[:, n]) + hy_bias[n] * z)
    return z

def _layer(x, ln1_g, ln1_b, ffn1_w1, ffn1_w3, ffn1_w2, w_in, b_gate, na_rpb,
           hy_short_w, hy_short_b, hy_filt_w1, hy_filt_b1, hy_filt_w2, hy_filt_b2,
           hy_filt_w3, hy_filt_b3, hy_filt_freq, hy_bias, w_pa, w_pb, w_out,
           ln2_g, ln2_b, ffn2_w1, ffn2_w3, ffn2_w2, ln3_g, ln3_b):
    x = layer_norm(DN_ALPHA * x + 0.5 * swiglu(x, ffn1_w1, ffn1_w3, ffn1_w2), ln1_g, ln1_b)
    b, L, _ = x.shape
    proj = x @ w_in
    qkv, hy_u, gate_logits = jnp.split(proj, [QKV_COLS, QKV_COLS + HY_COLS], axis=-1)
    q, k, v = [t.reshape(b, L, NA_HEADS, NA_HEAD_DIM) for t in jnp.split(qkv, 3, axis=-1)]
    y_a = neighbourhood_attention_2d(q, k, v, na_rpb)
    y_b = hyena_mixer(hy_u, hy_short_w, hy_short_b, hy_filt_w1, hy_filt_b1, hy_filt_w2,
                      hy_filt_b2, hy_filt_w3, hy_filt_b3, hy_filt_freq, hy_bias)
    g_a, g_b = jnp.split(jax.nn.sigmoid(gate_logits + b_gate), N_BRANCH, axis=-1)
    mix = (g_a * (y_a @ w_pa) + g_b * (y_b @ w_pb)) @ w_out
    x = layer_norm(DN_ALPHA * x + mix, ln2_g, ln2_b)
    x = layer_norm(DN_ALPHA * x + 0.5 * swiglu(x, ffn2_w1, ffn2_w3, ffn2_w2), ln3_g, ln3_b)
    return x

def setup_inputs(seed: int = 0) -> dict:
    key = jax.random.key(seed)
    ks = jax.random.split(key, 32)
    f32 = jnp.float32

    def nrm(k, shape, scale):
        return jax.random.normal(k, shape, f32) * scale

    Dp = DEPTH
    return {
        'x': jax.random.normal(ks[0], (BATCH, SEQ, D_MODEL), f32),
        'ln1_g': 1.0 + nrm(ks[1], (Dp, D_MODEL), 0.02),
        'ln1_b': nrm(ks[2], (Dp, D_MODEL), 0.02),
        'ffn1_w1': nrm(ks[3], (Dp, D_MODEL, D_FF), D_MODEL ** -0.5),
        'ffn1_w3': nrm(ks[4], (Dp, D_MODEL, D_FF), D_MODEL ** -0.5),
        'ffn1_w2': nrm(ks[5], (Dp, D_FF, D_MODEL), DN_BETA * D_FF ** -0.5),
        'w_in': nrm(ks[6], (Dp, D_MODEL, IN_COLS), D_MODEL ** -0.5),
        'b_gate': nrm(ks[7], (Dp, GATE_COLS), 0.02),
        'na_rpb': nrm(ks[8], (Dp, NA_HEADS, 2 * NA_KH_MAX - 1, 2 * NA_KW - 1), 0.02),
        'hy_short_w': nrm(ks[9], (Dp, HY_SHORT_K, HY_COLS), HY_SHORT_K ** -0.5),
        'hy_short_b': nrm(ks[10], (Dp, HY_COLS), 0.02),
        'hy_filt_w1': nrm(ks[11], (Dp, HY_EMB_DIM, HY_FILTER_HIDDEN), HY_EMB_DIM ** -0.5),
        'hy_filt_b1': nrm(ks[12], (Dp, HY_FILTER_HIDDEN), 0.02),
        'hy_filt_w2': nrm(ks[13], (Dp, HY_FILTER_HIDDEN, HY_FILTER_HIDDEN), HY_FILTER_HIDDEN ** -0.5),
        'hy_filt_b2': nrm(ks[14], (Dp, HY_FILTER_HIDDEN), 0.02),
        'hy_filt_w3': nrm(ks[15], (Dp, HY_FILTER_HIDDEN, N_DIR * HY_ORDER * HY_WIDTH), HY_FILTER_HIDDEN ** -0.5),
        'hy_filt_b3': nrm(ks[16], (Dp, N_DIR * HY_ORDER * HY_WIDTH), 0.02),
        'hy_filt_freq': 1.0 + nrm(ks[17], (Dp, HY_FILTER_HIDDEN), 0.02),
        'hy_bias': nrm(ks[18], (Dp, HY_ORDER, HY_WIDTH), 1.0),
        'w_pa': nrm(ks[19], (Dp, NA_WIDTH, D_MODEL), DN_BETA * NA_WIDTH ** -0.5),
        'w_pb': nrm(ks[20], (Dp, HY_WIDTH, D_MODEL), DN_BETA * HY_WIDTH ** -0.5),
        'w_out': nrm(ks[21], (Dp, D_MODEL, D_MODEL), DN_BETA * D_MODEL ** -0.5),
        'ln2_g': 1.0 + nrm(ks[22], (Dp, D_MODEL), 0.02),
        'ln2_b': nrm(ks[23], (Dp, D_MODEL), 0.02),
        'ffn2_w1': nrm(ks[24], (Dp, D_MODEL, D_FF), D_MODEL ** -0.5),
        'ffn2_w3': nrm(ks[25], (Dp, D_MODEL, D_FF), D_MODEL ** -0.5),
        'ffn2_w2': nrm(ks[26], (Dp, D_FF, D_MODEL), DN_BETA * D_FF ** -0.5),
        'ln3_g': 1.0 + nrm(ks[27], (Dp, D_MODEL), 0.02),
        'ln3_b': nrm(ks[28], (Dp, D_MODEL), 0.02),
    }

def reference(x, ln1_g, ln1_b, ffn1_w1, ffn1_w3, ffn1_w2, w_in, b_gate, na_rpb,
              hy_short_w, hy_short_b, hy_filt_w1, hy_filt_b1, hy_filt_w2, hy_filt_b2,
              hy_filt_w3, hy_filt_b3, hy_filt_freq, hy_bias, w_pa, w_pb, w_out,
              ln2_g, ln2_b, ffn2_w1, ffn2_w3, ffn2_w2, ln3_g, ln3_b):
    for i in range(DEPTH):
        x = _layer(x, ln1_g[i], ln1_b[i], ffn1_w1[i], ffn1_w3[i], ffn1_w2[i], w_in[i],
                   b_gate[i], na_rpb[i], hy_short_w[i], hy_short_b[i], hy_filt_w1[i],
                   hy_filt_b1[i], hy_filt_w2[i], hy_filt_b2[i], hy_filt_w3[i], hy_filt_b3[i],
                   hy_filt_freq[i], hy_bias[i], w_pa[i], w_pb[i], w_out[i], ln2_g[i],
                   ln2_b[i], ffn2_w1[i], ffn2_w3[i], ffn2_w2[i], ln3_g[i], ln3_b[i])
    return x


_drawn_inputs = setup_inputs


def setup_inputs(seed=0):
    import zlib

    import numpy as np

    out = dict(_drawn_inputs(seed))
    spreads = {}
    factors = {'b_gate': 23.418,
     'na_rpb': 64.0,
     'hy_filt_b1': 7.337,
     'hy_filt_b2': 5.131,
     'hy_filt_b3': 4.612,
     'hy_filt_freq': 8.0,
     'ln2_g': 2.798,
     'ln2_b': 2.88,
     'ln3_g': 9.739,
     'ln3_b': 8.546,
     'hy_short_b': 4.602}
    for name, (base, spread) in spreads.items():
        noise = np.random.default_rng([zlib.crc32(name.encode()), seed]).standard_normal(out[name].shape)
        drawn = base * np.exp(spread * noise) if base else spread * noise
        out[name] = __import__('jax').numpy.asarray(drawn.astype(out[name].dtype))
    for name, factor in factors.items():
        out[name] = (out[name] * factor).astype(out[name].dtype)
    return out
```

```python
from contextlib import ExitStack

import numpy as np

import concourse.bass as bass
from concourse import mybir

F32 = mybir.dt.float32
F32R = mybir.dt.float32r
ALU = mybir.AluOpType
ACT = mybir.ActivationFunctionType
AX = mybir.AxisListType

P = 128
D_MODEL, SEQ, D_FF = 1024, 512, 2816
GRID_W, KW, KH = 64, 16, 8
ROWS = SEQ // GRID_W
HEADS, HEAD_DIM = 8, 64
HY_WIDTH, HY_ORDER, EMB, HID = 512, 2, 33, 64
DEPTH = 1
ALPHA = (2 * DEPTH) ** 0.25
LN_EPS = 1e-5

DT = D_MODEL // P
FT = D_FF // P
CT = HY_WIDTH // P
TT = SEQ // P
HALF = SEQ // 2

UP_W = DT * P
DOWN_K = FT // 2
DOWN_W = DOWN_K * P
SLOTS = 4
UP_UNITS, DOWN_UNITS = 2 * FT, 2 * DT
FFN_UNITS = UP_UNITS + DOWN_UNITS
FFN_SLOTS = UP_UNITS + 2 * DOWN_UNITS
U_HYENA, U_Q, U_K, U_V, U_MIX, U_OUT = 0, 3 * CT, 4 * CT, 5 * CT, 6 * CT, 6 * CT + 3 * DT
MIX_UNITS = U_OUT + DT
RESIDUAL_TILES = DT

C_LN = 0
C_GATE = C_LN + 6 * DT
C_SW = C_GATE + 2 * DT
C_SB = C_SW + 9 * CT
C_HB = C_SB + 3 * CT
N_PARAM = C_HB + HY_ORDER * CT

SEG = (KH - 1) * (2 * KW - 1) + 2 * KW
W_EDGE, W_MID = 12 * KW, 16 * KW
MASKED = -1e30

MAGIC = 1.5 * 2 ** 23
TWO_PI_PARTS = (6.28125, 0.0019350051879882812, 3.019916050561733e-07)


class Steps:

    def __init__(self, eng, sem):
        self.eng, self.sem, self.n, self.turn, self.first = eng, sem, 0, None, 0

    def then(self, ins):
        ins.then_inc(self.sem, 1)
        self.n += 1
        self.eng.wait_ge(self.sem, self.n if self.turn is None else self.turn + self.n)

    def loop(self, i, per_turn):
        self.turn, self.first, self.per_turn = i * per_turn, self.n, per_turn

    def end(self, turns):
        assert self.n - self.first == self.per_turn, (self.n - self.first, self.per_turn)
        self.n = self.first + turns * self.per_turn
        self.turn = None


def build(nc, xT, params, up1, down1, mix_units, up2, down2, ident, dft, feat, filt1, filt2, filt_cols,
          filt3, decay, rpb_seg, na_mask, out):
    with ExitStack() as ctx:
        base = (nc.sbuf_base + 63) // 64 * 64
        KB = 1024

        def at(name, shape, dt, offset):
            return nc.alloc_sbuf_tensor_at(name, shape, dt, offset=base + offset)

        def sem(name):
            return ctx.enter_context(nc.semaphore(name))

        x_hi = at("x_hi", [P, DT, SEQ], F32R, 0)
        x_lo = at("x_lo", [P, DT, SEQ], F32R, 16 * KB)
        ring_hi = at("ring_hi", [P, SLOTS * UP_W], F32R, 32 * KB)
        ring_lo = at("ring_lo", [P, SLOTS * UP_W], F32R, 48 * KB)
        raw = at("raw", [P, 2, DOWN_W], F32, 64 * KB)
        fixed = 64 * KB + 2 * DOWN_W * 4
        par = at("par", [P, N_PARAM], F32, fixed)
        mean_of = at("mean_of", [P, P], F32, fixed + 512)
        eye = at("eye", [P, P], F32, fixed + 1024)
        u_pad = at("u_pad", [P, SEQ + 2], F32, fixed + 1536)
        kernel_scale = at("kernel_scale", [P, HY_ORDER, CT], F32, fixed + 1536 + 2112)
        R = fixed + 1536 + 2112 + 64
        y = at("y", [P, DT, SEQ], F32, R)
        act_gate = [y[:, p, :] for p in range(2)]
        h_prod = [y[:, 2 + p, :] for p in range(2)]
        h_hi = at("h_hi", [P, FT, SEQ], F32R, R + 16 * KB)
        h_lo = at("h_lo", [P, FT, SEQ], F32R, R + 60 * KB)
        squares = at("squares", [P, 2, SEQ], F32, R + 112 * KB)
        rstd = at("rstd", [P, SEQ], F32, R + 116 * KB)
        y_sum = at("y_sum", [P, SEQ], F32, R + 118 * KB)
        feat_sb = at("feat_sb", [EMB, SEQ], F32, R + 104 * KB)
        w_f1 = at("w_f1", [EMB, HID], F32, R + 106 * KB)
        w_f2 = at("w_f2", [HID, HID], F32, R + 106 * KB + 256)
        f_cols = at("f_cols", [HID, 3], F32, R + 106 * KB + 512)
        arg = at("arg", [HID, SEQ], F32, R + 108 * KB)
        turns = at("turns", [HID, SEQ], F32, R + 110 * KB)
        hid1 = at("hid1", [HID, SEQ], F32, R + 120 * KB)
        hid = at("hid", [HID + 1, SEQ], F32, R + 124 * KB)
        z0 = at("z0", [P, CT, SEQ], F32, R)
        z1 = at("z1", [P, CT, SEQ], F32, R + 8 * KB)
        part2 = at("part2", [P, CT, SEQ], F32, R + 16 * KB)
        parts = [z0, z1, part2]
        w_f3 = at("w_f3", [HID + 1, 2 * HY_ORDER * HY_WIDTH], F32, R + 16 * KB)
        dft_hi = at("dft_hi", [P, 6, 2, HALF], F32R, R + 24 * KB)
        dft_lo = at("dft_lo", [P, 6, 2, HALF], F32R, R + 36 * KB)
        spec_k = [at(f"spec_k{o}", [P, 2, 2, 2, HY_WIDTH], F32, R + (48 + 16 * o) * KB) for o in range(2)]
        decay_sb = at("decay_sb", [P, TT, HY_WIDTH], F32, R + 64 * KB)
        taps_hi = at("taps_hi", [P, 2, TT, HY_WIDTH], F32R, R + 80 * KB)
        taps_lo = at("taps_lo", [P, 2, TT, HY_WIDTH], F32R, R + 96 * KB)
        dft_raw = at("dft_raw", [P, 6, 2, HALF], F32, R + 80 * KB)
        zy_hi = at("zy_hi", [P, TT, HY_WIDTH], F32R, R + 80 * KB)
        zy_lo = at("zy_lo", [P, TT, HY_WIDTH], F32R, R + 88 * KB)
        spec_z = at("spec_z", [P, 2, 2, 2, HY_WIDTH], F32, R + 96 * KB)
        tap_f = at("tap_f", [P, HY_WIDTH], F32, R + 112 * KB)
        tap_b = at("tap_b", [P, HY_WIDTH], F32, R + 114 * KB)
        tap_pm = at("tap_pm", [P, 2, HY_WIDTH], F32, R + 116 * KB)
        tap_sq = at("tap_sq", [P, 2, HY_WIDTH], F32, R + 120 * KB)
        energy = at("energy", [P, HY_WIDTH], F32, R + 126 * KB)
        half_spec = at("half_spec", [P, HY_WIDTH], F32, R + 126 * KB)
        prod = [at(f"prod{n}", [P, 2, HY_WIDTH], F32, R + (112 + 4 * n) * KB) for n in range(3)]
        yb_hi = at("yb_hi", [P, CT, SEQ], F32R, R + 112 * KB)
        yb_lo = at("yb_lo", [P, CT, SEQ], F32R, R + 120 * KB)
        vT = at("vT", [P, CT, SEQ], F32, R + 88 * KB)
        qT = at("qT", [P, CT, SEQ], F32, R + 48 * KB)
        kT = at("kT", [P, CT, SEQ], F32, R + 56 * KB)
        seg_sb = at("seg_sb", [P, HEADS, SEG], F32, R + 64 * KB)
        mask_sb = at("mask_sb", [P, 2 * W_EDGE + W_MID], F32, R + 72 * KB)
        bias_sb = at("bias_sb", [P, 2, 2 * W_EDGE + W_MID], F32, R + 75 * KB)
        v_sb = at("v_sb", [P, 4, HEADS * HEAD_DIM], F32, R + 80 * KB)
        ya_hi = at("ya_hi", [P, CT, SEQ], F32R, R + 24 * KB)
        ya_lo = at("ya_lo", [P, CT, SEQ], F32R, R + 32 * KB)
        scores = at("scores", [P, 2, W_MID], F32, R + 96 * KB)
        probs = at("probs", [P, 2, W_MID], F32, R + 98 * KB)
        probsT = at("probsT", [P, 2, W_MID], F32, R + 100 * KB)
        neg_max = at("neg_max", [P, 32], F32, R + 102 * KB)
        row_sum = at("row_sum", [P, 32], F32, R + 102 * KB + 128)
        row_inv = at("row_inv", [P, 32], F32, R + 102 * KB + 256)
        m_hi = at("m_hi", [P, DT, SEQ], F32R, R + 48 * KB)
        m_lo = at("m_lo", [P, DT, SEQ], F32R, R + 64 * KB)
        gate_a = at("gate_a", [P, 2, SEQ], F32, R + 96 * KB)
        gate_b = at("gate_b", [P, 2, SEQ], F32, R + 100 * KB)

        ps = [ctx.enter_context(nc.psum_tensor(f"ps{n}", [P, SEQ], F32)) for n in range(8)]
        MEAN, VAR = ps[6], ps[7]

        raw_loaded = [sem("raw_loaded0"), sem("raw_loaded1")]
        x_loaded, small_loaded, filt_loaded = sem("x_loaded"), sem("small_loaded"), sem("filt_loaded")
        mixer_loaded, na_loaded, stored = sem("mixer_loaded"), sem("na_loaded"), sem("stored")
        slot_taken, unit_hi, unit_lo, ring_freed = sem("slot_taken"), sem("unit_hi"), sem("unit_lo"), sem("ring_freed")
        mean_set = sem("mean_set")
        x_hi_ready, x_ready = sem("x_hi_ready"), sem("x_ready")
        up_freed, gate_ready = sem("up_freed"), sem("gate_ready")
        h_hi_ready, h_ready = sem("h_hi_ready"), sem("h_ready")
        res_freed = sem("res_freed")
        y_summed, mean_ready, centred = sem("y_summed"), sem("mean_ready"), sem("centred")
        squared, var_step, var_eps, std_ready = sem("squared"), sem("var_step"), sem("var_eps"), sem("std_ready")
        scaled, final_ready = sem("scaled"), sem("final_ready")
        dve_step, pool_step, act_step = sem("dve_step"), sem("pool_step"), sem("act_step")
        hid_mm, arg_ready, hid_ready, ones_row = sem("hid_mm"), sem("arg_ready"), sem("hid_ready"), sem("ones_row")
        dft_ready = sem("dft_ready")
        proj_freed, pad_ready, conv_ready = sem("proj_freed"), sem("pad_ready"), sem("conv_ready")
        filt_mm, filt_freed, taps_made, taps_hi_ready, taps_ready = (
            sem("filt_mm"), sem("filt_freed"), sem("taps_made"), sem("taps_hi_ready"), sem("taps_ready"))
        energy_ready, energy_mm, energy_eps, energy_std, scale_ready = (
            sem("energy_ready"), sem("energy_mm"), sem("energy_eps"), sem("energy_std"), sem("scale_ready"))
        spec_mm, spec_half, spec_freed = sem("spec_mm"), sem("spec_half"), sem("spec_freed")
        zt_ready, z_hi_ready, z_ready = sem("zt_ready"), sem("z_hi_ready"), sem("z_ready")
        spec_made, spec_hi_ready, spec_ready = sem("spec_made"), sem("spec_hi_ready"), sem("spec_ready")
        inv_mm, inv_ready, gated = sem("inv_mm"), sem("inv_ready"), sem("gated")
        yb_hi_ready, yb_ready = sem("yb_hi_ready"), sem("yb_ready")
        qk_ready, vt_ready, v_mm, v_ready = sem("qk_ready"), sem("vt_ready"), sem("v_mm"), sem("v_ready")
        bias_ready, score_mm, scored, max_ready, exp_ready, prob_ready = (
            sem("bias_ready"), sem("score_mm"), sem("scored"), sem("max_ready"), sem("exp_ready"),
            sem("prob_ready"))
        pt_mm, pt_ready, pv_mm, ya_hi_ready, ya_ready = (
            sem("pt_mm"), sem("pt_ready"), sem("pv_mm"), sem("ya_hi_ready"), sem("ya_ready"))
        gates_ready, m_made, m_hi_ready, m_ready = (
            sem("gates_ready"), sem("m_made"), sem("m_hi_ready"), sem("m_ready"))

        UNIT0 = {"ffn1": 0, "mix": FFN_UNITS, "ffn2": FFN_UNITS + MIX_UNITS}
        SLOT0 = {"ffn1": 0, "mix": FFN_SLOTS, "ffn2": FFN_SLOTS + MIX_UNITS}

        def used(phase, slots):
            return SLOTS + SLOT0[phase] + slots

        block = ctx.enter_context(nc.Block())

        @block.sync
        def _(sp):
            sp.dma_start(feat_sb[:], feat).then_inc(filt_loaded, 16)
            sp.dma_start(w_f1[:], filt1).then_inc(filt_loaded, 16)
            sp.dma_start(w_f2[:], filt2).then_inc(filt_loaded, 16)
            sp.dma_start(f_cols[:], filt_cols).then_inc(filt_loaded, 16)
            sp.dma_start(par[:], params).then_inc(small_loaded, 16)
            sp.dma_start(eye[:], ident).then_inc(small_loaded, 16)
            for half in range(2):
                a = half * DT // 2
                sp.dma_start(y[:, a:a + DT // 2, :], xT[:, a:a + DT // 2, :]).then_inc(x_loaded, 16)

            def units(src, width, n, first):
                with sp.Fori(0, n // 2) as i:
                    for s in range(2):
                        sp.wait_ge(unit_lo, i * 2 + (first + s - 1))
                        sp.dma_start(raw[:, s, 0:width], src[i * 2 + s]).then_inc(raw_loaded[s], 16)

            def ffn(up, down, u0):
                skip = 2 if u0 == 0 else 0
                for u in range(skip):
                    sp.dma_start(raw[:, u, 0:UP_W], up[u]).then_inc(raw_loaded[u], 16)
                units(up[skip:], UP_W, UP_UNITS - skip, u0 + skip)
                units(down, DOWN_W, DOWN_UNITS, u0 + UP_UNITS)

            ffn(up1, down1, 0)
            u0 = UNIT0["mix"]
            units(mix_units[0:4], UP_W, 4, u0)
            sp.wait_ge(ring_freed, used("ffn1", FFN_SLOTS))
            sp.dma_start(dft_raw[:], dft).then_inc(mixer_loaded, 16)
            sp.dma_start(w_f3[:], filt3).then_inc(mixer_loaded, 16)
            sp.dma_start(decay_sb[:], decay).then_inc(mixer_loaded, 16)
            units(mix_units[4:U_MIX], UP_W, U_MIX - 4, u0 + 4)
            sp.wait_ge(spec_made, 4)
            sp.dma_start(seg_sb[:], rpb_seg).then_inc(na_loaded, 16)
            sp.dma_start(mask_sb[:], na_mask).then_inc(na_loaded, 16)
            units(mix_units[U_MIX:], UP_W, MIX_UNITS - U_MIX, u0 + U_MIX)
            ffn(up2, down2, UNIT0["ffn2"])
            for d in range(DT):
                sp.wait_ge(final_ready, d + 1)
                sp.dma_start(out[:, d, :], y[:, d, :]).then_inc(stored, 16)
            sp.wait_ge(stored, 16 * DT)

        @block.gpsimd
        def _(pool):
            pool.sem_inc(ring_freed, SLOTS)

            def split(slot, width, raw_slot, nth_load, slots_taken, unit):
                pool.wait_ge(raw_loaded[raw_slot], nth_load * 16)
                pool.wait_ge(ring_freed, slots_taken)
                pool.sem_inc(slot_taken, 1)
                hi = ring_hi[:, slot * UP_W:slot * UP_W + width]
                lo = ring_lo[:, slot * UP_W:slot * UP_W + width]
                pool.tensor_copy(hi, raw[:, raw_slot, 0:width]).then_inc(unit_hi, 1)
                pool.wait_ge(unit_hi, unit + 1)
                pool.tensor_tensor(lo, raw[:, raw_slot, 0:width], hi.bitcast(F32), ALU.subtract
                                   ).then_inc(unit_lo, 1)

            def up_units(n, unit0, slot0):
                with pool.Fori(0, n // SLOTS) as i:
                    for s in range(SLOTS):
                        split(s, UP_W, s % 2, i * 2 + (unit0 // 2 + s // 2 + 1),
                              i * SLOTS + (slot0 + s + 1), i * SLOTS + (unit0 + s))

            def down_units(unit0, slot0):
                with pool.Fori(0, DOWN_UNITS // 2) as i:
                    for s in range(2):
                        split(2 * s, DOWN_W, s, i + (unit0 // 2 + 1),
                              i * 4 + (slot0 + 2 * (s + 1)), i * 2 + (unit0 + s))

            up_units(UP_UNITS, 0, 0)
            down_units(UP_UNITS, UP_UNITS)
            u0, s0 = UNIT0["mix"], SLOT0["mix"]
            up_units(4, u0, s0)
            pool.wait_ge(mixer_loaded, 48)
            pool.tensor_copy(dft_hi[:], dft_raw[:]).then_inc(pool_step, 1)
            pool.wait_ge(pool_step, 1)
            pool.tensor_tensor(dft_lo[:], dft_raw[:], dft_hi[:].bitcast(F32), ALU.subtract).then_inc(dft_ready, 1)
            up_units(U_MIX - 4, u0 + 4, s0 + 4)
            up_units(4, u0 + U_MIX, s0 + U_MIX)
            pool.wait_ge(na_loaded, 32)
            for h in range(HEADS):
                if h >= 2:
                    pool.wait_ge(scored, 4 * (h - 1))
                pos = 0
                for c0, cols in ((8, 8), (16, 16), (0, 16), (16, 16), (0, 16), (16, 8)):
                    w = ROWS * cols
                    seg = bass.AP(seg_sb[:].tensor, seg_sb[:, h, c0:c0 + 1].offset,
                                  [list(seg_sb[:].ap[0]), [2 * KW - 1, ROWS], [1, cols]])
                    last = pool.tensor_tensor(
                        bias_sb[:, h % 2, pos:pos + w].rearrange("p (r c) -> p r c", r=ROWS), seg,
                        mask_sb[:, pos:pos + w].rearrange("p (r c) -> p r c", r=ROWS), ALU.add)
                    pos += w
                last.then_inc(bias_ready, 1)
            up_units(MIX_UNITS - U_MIX - 4, u0 + U_MIX + 4, s0 + U_MIX + 4)
            up_units(UP_UNITS, UNIT0["ffn2"], SLOT0["ffn2"])
            down_units(UNIT0["ffn2"] + UP_UNITS, SLOT0["ffn2"] + UP_UNITS)

        @block.tensor
        def _(pe):
            def mm3(out_ps, lhs_hi, lhs_lo, rhs_hi, rhs_lo, start, stop, **kw):
                pe.matmul(out_ps, lhs_hi, rhs_hi, start=start, stop=False, **kw)
                pe.matmul(out_ps, lhs_hi, rhs_lo, start=False, stop=False, **kw)
                return pe.matmul(out_ps, lhs_lo, rhs_hi, start=False, stop=stop, **kw)

            def tile_of(slot, k):
                a = slot * UP_W + k * P
                return ring_hi[:, a:a + P], ring_lo[:, a:a + P]

            def unit_times(slot, out_ps, mov_hi, mov_lo, tiles=DT, first=0, start=True, stop=True):
                for k in range(tiles):
                    w_hi, w_lo = tile_of(slot, k + first)
                    last = mm3(out_ps, w_hi, w_lo, mov_hi(k), mov_lo(k), start and k == 0,
                               stop and k == tiles - 1)
                return last

            x_tile = (lambda k: x_hi[:, k, :], lambda k: x_lo[:, k, :])

            def ffn_up(f, unit0, x_count):
                pe.wait_ge(x_ready, x_count)
                with pe.Fori(0, FT // 2) as i:
                    for p in range(2):
                        pe.wait_ge(up_freed, i * 2 + (f * FT + p + 1))
                        for m in range(2):
                            s = 2 * p + m
                            pe.wait_ge(unit_lo, i * SLOTS + (unit0 + s + 1))
                            unit_times(s, ps[s][:], *x_tile).then_inc(ring_freed, 1)

            def ffn_down(f, r0, unit0):
                pe.wait_ge(h_ready, (f + 1) * FT)
                with pe.Fori(0, DT // 2) as i:
                    for p in range(2):
                        pe.wait_ge(res_freed, i * 2 + (r0 + p + 1))
                        for half in range(2):
                            pe.wait_ge(unit_lo, i * 4 + (unit0 + 2 * p + half + 1))
                            k0 = half * DOWN_K
                            last = unit_times(2 * half, ps[4 + p][:], lambda k: h_hi[:, k0 + k, :],
                                              lambda k: h_lo[:, k0 + k, :], tiles=DOWN_K,
                                              start=half == 0, stop=half == 1)
                            last.then_inc(ring_freed, 2)

            def layer_norm(n):
                pe.wait_ge(y_summed, n + 1)
                pe.matmul(MEAN[:], mean_of[:], y_sum[:], start=True, stop=True).then_inc(mean_ready, 1)
                for d in range(DT):
                    pe.wait_ge(squared, n * DT + d + 1)
                    pe.matmul(VAR[:], mean_of[:], squares[:, d % 2, :], start=d == 0, stop=d == DT - 1
                              ).then_inc(var_step, 1)

            pe.wait_ge(filt_loaded, 64)
            pe.matmul(ps[7][0:HID, :], w_f1[:], feat_sb[:], start=True, stop=True).then_inc(hid_mm, 1)
            pe.wait_ge(hid_ready, 1)
            pe.matmul(ps[7][0:HID, :], w_f2[:], hid1[:], start=True, stop=True).then_inc(hid_mm, 1)

            pe.wait_ge(mean_set, 3)
            ffn_up(0, 0, DT)
            ffn_down(0, 0, UP_UNITS)
            layer_norm(0)

            u0 = UNIT0["mix"]
            pe.wait_ge(x_ready, 2 * DT)

            def project(n):
                pe.wait_ge(proj_freed, n + 1)
                pe.wait_ge(unit_lo, u0 + n + 1)
                unit_times(n % SLOTS, ps[n % 2][:], *x_tile).then_inc(ring_freed, 1)

            def filter_tile(n):
                o, t = n // TT, n % TT
                if n >= 2:
                    pe.wait_ge(filt_freed, n - 1)
                if n == TT:
                    pe.wait_ge(spec_freed, 4)
                tokens = hid[:, t * P:(t + 1) * P]
                for way in range(2):
                    col = (way * HY_ORDER + o) * HY_WIDTH
                    last = pe.matmul(ps[2 + 2 * (n % 2) + way][:], tokens, w_f3[:, col:col + HY_WIDTH],
                                     start=True, stop=True)
                last.then_inc(filt_mm, 1)

            def spectrum(v0, src, kinds):
                for kt in range(2):
                    for rs in range(2):
                        v = v0 + 2 * kt + rs
                        if v - v0 >= 2:
                            pe.wait_ge(spec_freed, v - 1)
                        for odd in range(2):
                            for t in range(2):
                                hi, lo = (w[:, 2 * rs + odd, t, kt * P:(kt + 1) * P] for w in (dft_hi, dft_lo))
                                s_hi, s_lo = src(rs, 2 * odd + t)
                                last = mm3(ps[2 + 2 * rs + odd][:], hi, lo, s_hi, s_lo, t == 0, t == 1)
                        last.then_inc(spec_mm, 1)

            taps = lambda rs, t: (taps_hi[:, rs, t, :], taps_lo[:, rs, t, :])
            z_of = lambda rs, t: (zy_hi[:, t, :], zy_lo[:, t, :])

            def energy_sum(o):
                pe.wait_ge(energy_ready, o + 1)
                for c in range(CT):
                    last = pe.matmul(ps[7][:, c:c + 1], energy[:, c * P:(c + 1) * P], mean_of[:, 0:1],
                                     start=True, stop=True)
                last.then_inc(energy_mm, 1)

            def turn_z(o):
                for t in range(TT):
                    if t >= 2:
                        pe.wait_ge(z_ready, o * TT + t - 1)
                    for c in range(CT):
                        last = pe.transpose(ps[6 + t % 2][:, c * P:(c + 1) * P],
                                            parts[o][:, c, t * P:(t + 1) * P], eye[:])
                    last.then_inc(zt_ready, 1)

            def inverse(o, kt):
                pe.wait_ge(spec_ready, 2 * o + kt + 1)
                for c in range(CT):
                    cols = slice(c * P, (c + 1) * P)
                    for odd, mats in ((0, (4, 5)), (1, (1, 3))):
                        for rs in range(2):
                            a = 2 * rs + odd
                            first = kt == 0 and odd == 0 and rs == 0
                            last = mm3(ps[2 + c][:, odd * HALF:(odd + 1) * HALF],
                                       zy_hi[:, a, cols], zy_lo[:, a, cols],
                                       dft_hi[:, mats[rs], kt, :], dft_lo[:, mats[rs], kt, :],
                                       first, kt == 1 and rs == 1, skip_group_check=True)
                    if kt == 1:
                        last.then_inc(inv_ready, 1)
                if kt == 0:
                    last.then_inc(inv_mm, 1)

            pe.wait_ge(mixer_loaded, 48)
            pe.wait_ge(ones_row, 1)
            pe.wait_ge(hid_ready, 2)
            pe.wait_ge(dft_ready, 1)
            for n in range(TT):
                project(n)
                filter_tile(n)
            project(TT)
            energy_sum(0)
            pe.wait_ge(taps_ready, TT)
            spectrum(0, taps, 2)
            filter_tile(TT)
            for n in range(TT + 1, 2 * TT):
                project(n)
                filter_tile(n)
            pe.wait_ge(conv_ready, CT)
            energy_sum(1)
            pe.wait_ge(taps_ready, 2 * TT)
            spectrum(4, taps, 2)
            for o in range(HY_ORDER):
                if o:
                    pe.wait_ge(gated, CT)
                turn_z(o)
                pe.wait_ge(z_ready, (o + 1) * TT)
                spectrum(8 + 4 * o, z_of, 1)
                for n in (range(2 * CT, 3 * CT) if o == 0 else range(3 * CT, 5 * CT)):
                    project(n)
                pe.wait_ge(spec_freed, 12 + 4 * o)
                inverse(o, 0)
                inverse(o, 1)

            for n in range(5 * CT, 6 * CT):
                project(n)
            for g in range(TT):
                pe.wait_ge(vt_ready, CT)
                if g >= 2:
                    pe.wait_ge(v_ready, g - 1)
                for c in range(CT):
                    last = pe.transpose(ps[6 + g % 2][:, c * P:(c + 1) * P], vT[:, c, g * P:(g + 1) * P], eye[:])
                last.then_inc(v_mm, 1)

            def keys(g):
                if g == 0:
                    return 0, 8, 0
                if g == 4:
                    return 56, 8, 64
                return KW * g - 8, KW, 0

            def score(a):
                h, b = a // 4, a % 4
                if a >= 2:
                    pe.wait_ge(scored, a - 1)
                row = slice((h % 2) * HEAD_DIM, (h % 2 + 1) * HEAD_DIM)
                q = qT[row, h // 2, b * P:(b + 1) * P]
                pos = 0
                for g in (b, b + 1):
                    c0, n, _ = keys(g)
                    k = kT[row, h // 2, :].rearrange("p (r w) -> p r w", w=GRID_W)[:, :, c0:c0 + n]
                    last = pe.matmul(ps[a % 2][:, pos:pos + ROWS * n], q, k, start=True, stop=True)
                    pos += ROWS * n
                last.then_inc(score_mm, 1)

            def turn_probs(a):
                b = a % 4
                pe.wait_ge(prob_ready, a + 1)
                if a >= 2:
                    pe.wait_ge(pt_ready, a - 1)
                bank = ps[2 + a % 2]
                if b == 0:
                    pe.transpose(bank[0:64, 0:P], probs[:, a % 2, 0:64], eye[:])
                    last = pe.transpose(bank[:, P:2 * P], probs[:, a % 2, 64:192], eye[:])
                else:
                    pe.transpose(bank[:, 0:P], probs[:, a % 2, 0:P], eye[:])
                    c = 64 if b == 3 else P
                    last = pe.transpose(bank[:, P:2 * P], probs[:, a % 2, c:c + P], eye[:])
                last.then_inc(pt_mm, 1)

            def values(a):
                h, b = a // 4, a % 4
                pe.wait_ge(pt_ready, a + 1)
                if a % 8 == 0 and a >= 16:
                    pe.wait_ge(ya_ready, a // 8 - 1)
                out_ps = ps[4 + (h // 2) % 2][(h % 2) * HEAD_DIM:(h % 2 + 1) * HEAD_DIM, b * P:(b + 1) * P]
                for n, g in enumerate((b, b + 1)):
                    _, cols, r0 = keys(g)
                    rows = slice(r0, r0 + ROWS * cols)
                    last = pe.matmul(out_ps, v_sb[rows, g % 4, h * HEAD_DIM:(h + 1) * HEAD_DIM],
                                     probsT[rows, a % 2, n * P:(n + 1) * P], start=n == 0, stop=n == 1)
                last.then_inc(pv_mm, 1)

            pe.wait_ge(v_ready, 4)
            pe.wait_ge(qk_ready, 2 * CT)
            pe.wait_ge(gated, 2 * CT)
            score(0)
            for a in range(32):
                if a + 1 < 32:
                    score(a + 1)
                turn_probs(a)
                if a >= 1:
                    values(a - 1)
            values(31)

            pe.wait_ge(ya_ready, CT)
            pe.wait_ge(yb_ready, CT)
            ya_t = (lambda k: ya_hi[:, k, :], lambda k: ya_lo[:, k, :])
            yb_t = (lambda k: yb_hi[:, k, :], lambda k: yb_lo[:, k, :])
            with pe.Fori(0, 2) as i:
                for d in range(4):
                    b0 = 4 * (d % 2)
                    pe.wait_ge(m_made, i * 4 + (d + 1))
                    for m in range(3):
                        n = 3 * d + m
                        pe.wait_ge(unit_lo, i * 12 + (u0 + U_MIX + n + 1))
                        if m < 2:
                            last = unit_times(n % SLOTS, ps[b0 + m][:], *x_tile)
                        else:
                            unit_times(n % SLOTS, ps[b0 + 2][:], *ya_t, tiles=CT)
                            last = unit_times(n % SLOTS, ps[b0 + 3][:], *yb_t, tiles=CT, first=CT)
                        last.then_inc(ring_freed, 1)
            pe.wait_ge(m_ready, DT)
            m_t = (lambda k: m_hi[:, k, :], lambda k: m_lo[:, k, :])
            with pe.Fori(0, DT // 4) as i:
                for s in range(4):
                    pe.wait_ge(res_freed, i * 4 + (RESIDUAL_TILES + s + 1))
                    pe.wait_ge(unit_lo, i * 4 + (u0 + U_OUT + s + 1))
                    unit_times(s, ps[4 + s % 2][:], *m_t).then_inc(ring_freed, 1)
            layer_norm(1)

            ffn_up(1, UNIT0["ffn2"], 3 * DT)
            ffn_down(1, 2 * RESIDUAL_TILES, UNIT0["ffn2"] + UP_UNITS)
            layer_norm(2)

        @block.scalar
        def _(act):
            def split_x():
                act.wait_ge(x_loaded, 32)
                for d in range(DT):
                    act.activation(x_hi[:, d, :], y[:, d, :], ACT.Copy).then_inc(x_hi_ready, 1)

            def ffn_up(f):
                with act.Fori(0, FT // 2) as i:
                    for p in range(2):
                        act.wait_ge(ring_freed, i * 4 + used(("ffn1", "ffn2")[f], 2 * p + 2))
                        act.activation(act_gate[p], ps[2 * p][:], ACT.Silu).then_inc(gate_ready, 1)
                        act.wait_ge(up_freed, i * 2 + (2 + f * FT + p + 1))
                        act.activation(h_hi[:, i * 2 + p, :], h_prod[p], ACT.Copy).then_inc(h_hi_ready, 1)

            def layer_norm(n, last):
                for d in range(DT):
                    act.wait_ge(centred, n * DT + d + 1)
                    if d >= 2:
                        act.wait_ge(var_step, n * DT + d - 1)
                    act.activation(squares[:, d % 2, :], y[:, d, :], ACT.Square).then_inc(squared, 1)
                act.wait_ge(var_eps, n + 1)
                act.activation(rstd[:], rstd[:], ACT.Sqrt).then_inc(std_ready, 1)
                for d in range(DT):
                    b = par[:, (2 * n + 1) * DT + d:(2 * n + 1) * DT + d + 1]
                    act.wait_ge(scaled, n * DT + d + 1)
                    if last:
                        act.activation(y[:, d, :], y[:, d, :], ACT.Identity, bias=b).then_inc(final_ready, 1)
                    else:
                        act.activation(x_hi[:, d, :], y[:, d, :], ACT.Identity, bias=b).then_inc(x_hi_ready, 1)

            act.wait_ge(small_loaded, 32)
            for n in range(2):
                act.wait_ge(arg_ready, n + 1)
                act.activation((hid1, hid)[n][0:HID, :], arg[:], ACT.Sin).then_inc(hid_ready, 1)
            split_x()
            ffn_up(0)
            layer_norm(0, False)

            act.sem_inc(proj_freed, 2)
            act.wait_ge(mean_set, 3)

            def pad_part(n):
                part, c = n // CT, n % CT
                if n >= 1:
                    act.wait_ge(conv_ready, n)
                act.wait_ge(ring_freed, used("mix", n + 1))
                act.activation(u_pad[:, 1:SEQ + 1], ps[n % 2][:], ACT.Copy).then_inc(pad_ready, 1)
                act.activation(parts[part][:, c, :].rearrange("p (two s) -> p s two", two=2),
                               ps[n % 2][:].rearrange("p (s two) -> p s two", two=2), ACT.Identity,
                               scale=par[:, C_SW + 3 * CT + n:C_SW + 3 * CT + n + 1],
                               bias=par[:, C_SB + n:C_SB + n + 1]).then_inc(pad_ready, 1)
                act.wait_ge(pad_ready, 2 * n + 2)
                act.sem_inc(proj_freed, 1)

            def tap_hi(n):
                act.wait_ge(taps_made, n + 1)
                if n == TT:
                    act.wait_ge(spec_mm, 4)
                t = n % TT
                act.activation(taps_hi[:, :, t, :], tap_pm[:], ACT.Copy).then_inc(taps_hi_ready, 1)
                act.activation(tap_sq[:], tap_pm[:], ACT.Square).then_inc(taps_hi_ready, 1)

            def spec_evac(v0):
                for v in range(v0, v0 + 4):
                    act.wait_ge(spec_mm, v + 1)
                    if v >= 1:
                        act.wait_ge(spec_freed, v)
                    act.activation(half_spec[:], ps[2 + 2 * (v % 2)][:], ACT.Copy).then_inc(spec_half, 1)

            def energy_sqrt(o):
                act.wait_ge(energy_eps, o + 1)
                act.activation(kernel_scale[:, o, :], kernel_scale[:, o, :], ACT.Sqrt).then_inc(energy_std, 1)

            for n in range(TT):
                pad_part(n)
                tap_hi(n)
            pad_part(TT)
            energy_sqrt(0)
            spec_evac(0)
            tap_hi(TT)
            for n in range(TT + 1, 2 * TT):
                pad_part(n)
                tap_hi(n)
            energy_sqrt(1)
            spec_evac(4)
            for o in range(HY_ORDER):
                for t in range(TT):
                    act.wait_ge(zt_ready, o * TT + t + 1)
                    act.activation(zy_hi[:, t, :], ps[6 + t % 2][:], ACT.Copy).then_inc(z_hi_ready, 1)
                spec_evac(8 + 4 * o)

                def product_hi(kt):
                    act.wait_ge(spec_made, 2 * o + kt + 1)
                    if kt:
                        act.wait_ge(inv_mm, o + 1)
                    act.activation(zy_hi[:], spec_z[:, kt].rearrange("p a b c -> p (a b) c"), ACT.Copy
                                   ).then_inc(spec_hi_ready, 1)

                if o == 0:
                    pad_part(2 * CT)
                    pad_part(2 * CT + 1)
                    product_hi(0)
                    pad_part(2 * CT + 2)
                    pad_part(2 * CT + 3)
                    product_hi(1)
                else:
                    for n in range(2 * CT):
                        if n == 4:
                            product_hi(0)
                        act.wait_ge(ring_freed, used("mix", 3 * CT + n + 1))
                        if n < CT:
                            act.activation(qT[:, n, :].rearrange("p (b r w) -> p b r w", r=ROWS, w=KW),
                                           ps[n % 2][:].rearrange("p (r b w) -> p b r w", r=ROWS, w=KW),
                                           ACT.Copy).then_inc(qk_ready, 1)
                        else:
                            act.activation(kT[:, n - CT, :], ps[n % 2][:], ACT.Copy).then_inc(qk_ready, 1)
                        act.wait_ge(qk_ready, n + 1)
                        act.sem_inc(proj_freed, 1)
                    product_hi(1)
            for c in range(CT):
                act.wait_ge(gated, CT + c + 1)
                act.activation(yb_hi[:, c, :], z0[:, c, :], ACT.Copy).then_inc(yb_hi_ready, 1)
            act.wait_ge(inv_ready, 2 * CT)
            for n in range(CT):
                bank, vt = ps[n % 2][:], vT[:, n, :]
                act.wait_ge(ring_freed, used("mix", U_V + n + 1))
                act.activation(vt[:, 0:P].rearrange("p (s r w) -> p s r w", s=2, w=8),
                               bank.rearrange("p (r s w) -> p s r w", s=8, w=8)[:, 0:8:7], ACT.Copy)
                act.activation(vt[:, P:].rearrange("p (g r w) -> p g r w", g=3, w=KW),
                               bank.rearrange("p (r w) -> p r w", w=GRID_W)[:, :, 8:56].rearrange(
                                   "p r (g w) -> p g r w", w=KW), ACT.Copy).then_inc(vt_ready, 1)
                act.wait_ge(vt_ready, n + 1)
                act.sem_inc(proj_freed, 1)
            for g in range(TT):
                act.wait_ge(v_mm, g + 1)
                act.activation(v_sb[:, g, :], ps[6 + g % 2][:], ACT.Copy).then_inc(v_ready, 1)

            def pt_evac(a):
                act.wait_ge(pt_mm, a + 1)
                if a >= 2:
                    act.wait_ge(pv_mm, a - 1)
                src, dst = ps[2 + a % 2], probsT[:, a % 2, :]
                if a % 4 == 0:
                    act.activation(dst[0:64, 0:P], src[0:64, 0:P], ACT.Copy)
                    act.activation(dst[:, P:2 * P], src[:, P:2 * P], ACT.Copy).then_inc(pt_ready, 1)
                else:
                    act.activation(dst, src[:, 0:2 * P], ACT.Copy).then_inc(pt_ready, 1)

            by_block = lambda t, c: t[:, c, :].rearrange("p (r b w) -> p b r w", b=4, w=KW)
            for a in range(32 + 1):
                if a < 32:
                    w = W_EDGE if a % 4 in (0, 3) else W_MID
                    act.wait_ge(max_ready, a + 1)
                    if a >= 2:
                        act.wait_ge(pt_mm, a - 1)
                    act.activation(probs[:, a % 2, 0:w], scores[:, a % 2, 0:w], ACT.Exp,
                                   bias=neg_max[:, a:a + 1], accum_out=row_sum[:, a:a + 1]).then_inc(exp_ready, 1)
                if a >= 1:
                    pt_evac(a - 1)
                if a >= 9 and (a - 1) % 8 == 0 or a == 32:
                    c = (a - 9) // 8 if a < 32 else 3
                    if c < 4 and a != 32 or a == 32:
                        act.wait_ge(pv_mm, 8 * (c + 1))
                        act.activation(by_block(ya_hi, c), ps[4 + c % 2][:].rearrange(
                            "p (b r w) -> p b r w", b=4, w=KW), ACT.Copy).then_inc(ya_hi_ready, 1)

            for d in range(DT):
                act.wait_ge(ring_freed, used("mix", U_MIX + 3 * (d + 1)))
                b0 = 4 * (d % 2)
                for br, dst in ((0, gate_a), (1, gate_b)):
                    col = C_GATE + br * DT + d
                    last = act.activation(dst[:, d % 2, :], ps[b0 + br][:], ACT.Sigmoid, bias=par[:, col:col + 1])
                last.then_inc(gates_ready, 1)
                act.wait_ge(m_made, 2 + d + 1)
                act.activation(m_hi[:, d, :], gate_a[:, d % 2, :], ACT.Copy).then_inc(m_hi_ready, 1)
            layer_norm(1, False)
            ffn_up(1)
            layer_norm(2, True)

        @block.vector
        def _(dve):
            step = Steps(dve, dve_step)
            dve.memset(mean_of[:], 1.0 / D_MODEL).then_inc(mean_set, 1)
            dve.memset(hid[HID:HID + 1, :], 1.0).then_inc(ones_row, 1)
            dve.memset(u_pad[:, 0:1], 0.0).then_inc(mean_set, 1)
            dve.memset(u_pad[:, SEQ + 1:SEQ + 2], 0.0).then_inc(mean_set, 1)
            dve.sem_inc(up_freed, 2)
            dve.sem_inc(res_freed, 2)
            dve.sem_inc(m_made, 2)

            def ffn_up(f):
                with dve.Fori(0, FT // 2) as i:
                    for p in range(2):
                        dve.wait_ge(gate_ready, i * 2 + (f * FT + p + 1))
                        dve.tensor_tensor(h_prod[p], act_gate[p], ps[2 * p + 1][:], ALU.mult
                                          ).then_inc(up_freed, 1)
                        dve.wait_ge(h_hi_ready, i * 2 + (f * FT + p + 1))
                        dve.tensor_tensor(h_lo[:, i * 2 + p, :], h_prod[p], h_hi[:, i * 2 + p, :].bitcast(F32),
                                          ALU.subtract).then_inc(h_ready, 1)

            def residual(r0, scale, phase, slot0, slots):
                for d in range(DT):
                    dve.wait_ge(ring_freed, used(phase, slot0 + (d + 1) * slots))
                    dve.scalar_tensor_tensor(y[:, d, :], x_hi[:, d, :].bitcast(F32), scale,
                                             ps[4 + d % 2][:], ALU.mult, ALU.add).then_inc(res_freed, 1)
                    dve.wait_ge(res_freed, 2 + r0 + d + 1)
                    step.then(dve.scalar_tensor_tensor(y[:, d, :], x_lo[:, d, :].bitcast(F32), scale,
                                                       y[:, d, :], ALU.mult, ALU.add))
                    if d == 0:
                        step.then(dve.tensor_copy(y_sum[:], y[:, 0, :]))
                    else:
                        last = dve.tensor_tensor(y_sum[:], y_sum[:], y[:, d, :], ALU.add)
                        if d == DT - 1:
                            last.then_inc(y_summed, 1)
                        else:
                            step.then(last)

            def layer_norm(n, eps, last):
                dve.wait_ge(mean_ready, n + 1)
                for d in range(DT):
                    dve.tensor_tensor(y[:, d, :], y[:, d, :], MEAN[:], ALU.subtract).then_inc(centred, 1)
                dve.wait_ge(var_step, (n + 1) * DT)
                dve.tensor_scalar(rstd[:], VAR[:], eps, None, ALU.add).then_inc(var_eps, 1)
                dve.wait_ge(std_ready, n + 1)
                step.then(dve.reciprocal(rstd[:], rstd[:]))

                def low(d):
                    dve.wait_ge(x_hi_ready, (n + 1) * DT + d + 1)
                    b = par[:, (2 * n + 1) * DT + d:(2 * n + 1) * DT + d + 1]
                    dve.scalar_tensor_tensor(x_lo[:, d, :], y[:, d, :], b, x_hi[:, d, :].bitcast(F32),
                                             ALU.add, ALU.subtract).then_inc(x_ready, 1)

                for d in range(DT):
                    g = par[:, 2 * n * DT + d:2 * n * DT + d + 1]
                    dve.scalar_tensor_tensor(y[:, d, :], y[:, d, :], g, rstd[:], ALU.mult, ALU.mult
                                             ).then_inc(scaled, 1)
                    if d >= 1 and not last:
                        low(d - 1)
                if not last:
                    low(DT - 1)

            dve.wait_ge(filt_loaded, 64)
            for n in range(2):
                dve.wait_ge(hid_mm, n + 1)
                step.then(dve.tensor_scalar(arg[:], ps[7][0:HID, :], f_cols[:, n:n + 1], f_cols[:, 2:3],
                                            ALU.add, ALU.mult))
                step.then(dve.tensor_scalar(turns[:], arg[:], float(1 / (2 * np.pi)), MAGIC, ALU.mult, ALU.add))
                step.then(dve.tensor_scalar(turns[:], turns[:], MAGIC, None, ALU.subtract))
                for part in TWO_PI_PARTS:
                    step.then(dve.scalar_tensor_tensor(arg[:], turns[:], -part, arg[:], ALU.mult, ALU.add))
                pi = 3.1415925
                dve.tensor_scalar(arg[:], arg[:], pi, -pi, ALU.min, ALU.max).then_inc(arg_ready, 1)
            for d in range(DT):
                dve.wait_ge(x_hi_ready, d + 1)
                dve.tensor_tensor(x_lo[:, d, :], y[:, d, :], x_hi[:, d, :].bitcast(F32), ALU.subtract
                                  ).then_inc(x_ready, 1)
            ffn_up(0)
            residual(0, 2 * ALPHA, "ffn1", UP_UNITS, 4)
            layer_norm(0, 4 * LN_EPS, False)

            def short_conv(n):
                part, c = n // CT, n % CT
                dst = parts[part][:, c, :].rearrange("p (two s) -> p s two", two=2)
                dve.wait_ge(pad_ready, 2 * n + 2)
                for tap in (0, 2):
                    col = C_SW + tap * 3 * CT + n
                    src = u_pad[:, tap:tap + SEQ].rearrange("p (s two) -> p s two", two=2)
                    last = dve.scalar_tensor_tensor(dst, src, par[:, col:col + 1], dst, ALU.mult, ALU.add)
                    if tap == 0:
                        step.then(last)
                last.then_inc(conv_ready, 1)

            def tap_tile(n):
                o, t = n // TT, n % TT
                dve.wait_ge(filt_mm, n + 1)
                b0 = 2 + 2 * (n % 2)
                if n >= 1:
                    dve.wait_ge(taps_hi_ready, 2 * n)
                step.then(dve.tensor_tensor(tap_f[:], decay_sb[:, t, :], ps[b0][:], ALU.mult))
                dve.tensor_tensor(tap_b[:], decay_sb[:, t, :], ps[b0 + 1][:], ALU.mult).then_inc(filt_freed, 1)
                dve.wait_ge(filt_freed, n + 1)
                if t == 0:
                    step.then(dve.memset(tap_b[0:1, :], 0.0))
                dve.tensor_tensor(tap_pm[:, 0, :], tap_f[:], tap_b[:], ALU.add)
                dve.tensor_tensor(tap_pm[:, 1, :], tap_f[:], tap_b[:], ALU.subtract).then_inc(taps_made, 1)
                dve.wait_ge(taps_hi_ready, 2 * n + 2)
                dve.tensor_tensor(taps_lo[:, :, t, :], tap_pm[:], taps_hi[:, :, t, :].bitcast(F32),
                                  ALU.subtract).then_inc(taps_ready, 1)
                if t == 0:
                    if o == 1:
                        dve.wait_ge(spec_half, 4)
                    step.then(dve.tensor_tensor(energy[:], tap_sq[:, 0, :], tap_sq[:, 1, :], ALU.add))
                else:
                    step.then(dve.tensor_tensor(energy[:], energy[:], tap_sq[:, 0, :], ALU.add))
                    last = dve.tensor_tensor(energy[:], energy[:], tap_sq[:, 1, :], ALU.add)
                    if t == TT - 1:
                        last.then_inc(energy_ready, 1)
                    else:
                        step.then(last)

            def kernel_norm(o):
                dve.wait_ge(energy_mm, o + 1)
                dve.tensor_scalar(kernel_scale[:, o, :], ps[7][:, 0:CT], float(D_MODEL / 2 * SEQ ** 2),
                                  1e-12 * SEQ ** 2, ALU.mult, ALU.add).then_inc(energy_eps, 1)
                dve.wait_ge(energy_std, o + 1)
                step.then(dve.reciprocal(kernel_scale[:, o, :], kernel_scale[:, o, :]))

            def spec_evac(v0, dst):
                for v in range(v0, v0 + 4):
                    kt, rs = (v - v0) // 2, v % 2
                    dve.wait_ge(spec_half, v + 1)
                    odd = ps[3 + 2 * rs][:]
                    dve.tensor_tensor(dst[:, kt, rs, 0, :], half_spec[:], odd, ALU.add)
                    if rs == 0:
                        last = dve.tensor_tensor(dst[:, kt, rs, 1, :], half_spec[:], odd, ALU.subtract)
                    else:
                        last = dve.tensor_tensor(dst[:, kt, rs, 1, :], odd, half_spec[:], ALU.subtract)
                    last.then_inc(spec_freed, 1)

            def product(o, kt):
                zr, zs = spec_z[:, kt, 0], spec_z[:, kt, 1]
                kr, ks = spec_k[o][:, kt, 0], spec_k[o][:, kt, 1]
                if kt == 0:
                    dve.wait_ge(spec_freed, 12 + 4 * o)
                dve.tensor_tensor(prod[0][:], zr, kr, ALU.mult)
                dve.tensor_tensor(prod[1][:], zs, ks, ALU.mult)
                step.then(dve.tensor_tensor(prod[2][:], zr, ks, ALU.mult))
                step.then(dve.tensor_tensor(zs, zs, kr, ALU.mult))
                dve.tensor_tensor(prod[0][:], prod[0][:], prod[1][:], ALU.subtract)
                step.then(dve.tensor_tensor(prod[2][:], prod[2][:], zs, ALU.add))
                for rs, src in ((0, prod[0]), (1, prod[2])):
                    for odd in range(2):
                        op = ALU.add if odd == rs else ALU.subtract
                        last = dve.tensor_tensor(spec_z[:, kt, rs, odd, :], src[:, 0, :], src[:, 1, :], op)
                last.then_inc(spec_made, 1)

            def product_lo(o, kt):
                dve.wait_ge(spec_hi_ready, 2 * o + kt + 1)
                dve.tensor_tensor(zy_lo[:], spec_z[:, kt].rearrange("p a b c -> p (a b) c"),
                                  zy_hi[:].bitcast(F32), ALU.subtract).then_inc(spec_ready, 1)

            def gate(o, c):
                z = parts[o][:, c, :]
                col = C_HB + o * CT + c
                step.then(dve.tensor_scalar(z, z, par[:, col:col + 1], None, ALU.mult))
                dve.wait_ge(inv_ready, o * CT + c + 1)
                step.then(dve.scalar_tensor_tensor(z, ps[2 + c][:], kernel_scale[:, o, c:c + 1], z,
                                                   ALU.mult, ALU.add))
                if o == 0:
                    dve.tensor_tensor(z1[:, c, :], z, z1[:, c, :], ALU.mult).then_inc(gated, 1)
                else:
                    last = dve.tensor_tensor(z0[:, c, :].rearrange("p (s two) -> p two s", two=2),
                                             z.rearrange("p (two s) -> p two s", two=2),
                                             part2[:, c, :].rearrange("p (two s) -> p two s", two=2), ALU.mult)
                    last.then_inc(gated, 1)

            for n in range(TT):
                short_conv(n)
                tap_tile(n)
            short_conv(TT)
            kernel_norm(0)
            spec_evac(0, spec_k[0])
            tap_tile(TT)
            for n in range(TT + 1, 2 * TT):
                short_conv(n)
                tap_tile(n)
            kernel_norm(1)
            spec_evac(4, spec_k[1])
            for o in range(HY_ORDER):
                for t in range(TT):
                    dve.wait_ge(z_hi_ready, o * TT + t + 1)
                    dve.tensor_tensor(zy_lo[:, t, :], ps[6 + t % 2][:], zy_hi[:, t, :].bitcast(F32),
                                      ALU.subtract).then_inc(z_ready, 1)
                spec_evac(8 + 4 * o, spec_z)
                product(o, 0)
                if o == 0:
                    short_conv(2 * CT)
                    short_conv(2 * CT + 1)
                product_lo(o, 0)
                product(o, 1)
                if o == 0:
                    short_conv(2 * CT + 2)
                    short_conv(2 * CT + 3)
                product_lo(o, 1)
                for c in range(CT):
                    gate(o, c)
            for c in range(CT):
                dve.wait_ge(yb_hi_ready, c + 1)
                dve.tensor_tensor(yb_lo[:, c, :], z0[:, c, :], yb_hi[:, c, :].bitcast(F32), ALU.subtract
                                  ).then_inc(yb_ready, 1)

            by_block = lambda t, c: t[:, c, :].rearrange("p (r b w) -> p b r w", b=4, w=KW)
            BIAS_AT = (0, W_EDGE, W_EDGE, W_EDGE + W_MID)

            def softmax_front(a):
                h, b = a // 4, a % 4
                w = W_EDGE if b in (0, 3) else W_MID
                if b == 0:
                    dve.wait_ge(bias_ready, h + 1)
                dve.wait_ge(score_mm, a + 1)
                if a >= 2:
                    dve.wait_ge(exp_ready, a - 1)
                last = dve.scalar_tensor_tensor(scores[:, a % 2, 0:w], ps[a % 2][:, 0:w], HEAD_DIM ** -0.5,
                                                bias_sb[:, h % 2, BIAS_AT[b]:BIAS_AT[b] + w], ALU.mult, ALU.add)
                last.then_inc(scored, 1)
                dve.wait_ge(scored, a + 1)
                dve.tensor_reduce(neg_max[:, a:a + 1], scores[:, a % 2, 0:w], AX.X, ALU.max, negate=True
                                  ).then_inc(max_ready, 1)

            def softmax_back(a):
                w = W_EDGE if a % 4 in (0, 3) else W_MID
                dve.wait_ge(exp_ready, a + 1)
                step.then(dve.reciprocal(row_inv[:, a:a + 1], row_sum[:, a:a + 1]))
                dve.tensor_scalar(probs[:, a % 2, 0:w], probs[:, a % 2, 0:w], row_inv[:, a:a + 1], None,
                                  ALU.mult).then_inc(prob_ready, 1)

            softmax_front(0)
            for a in range(32):
                if a + 1 < 32:
                    softmax_front(a + 1)
                softmax_back(a)
                if a >= 9 and (a - 9) % 8 == 0 or a == 31:
                    for c in ([(a - 9) // 8] if a < 31 else [3]):
                        dve.wait_ge(ya_hi_ready, c + 1)
                        dve.tensor_tensor(by_block(ya_lo, c), ps[4 + c % 2][:].rearrange(
                            "p (b r w) -> p b r w", b=4, w=KW), by_block(ya_hi, c).bitcast(F32),
                            ALU.subtract).then_inc(ya_ready, 1)

            for d in range(DT):
                s, b0 = d % 2, 4 * (d % 2)
                dve.wait_ge(gates_ready, d + 1)
                dve.tensor_tensor(gate_a[:, s, :], gate_a[:, s, :], ps[b0 + 2][:], ALU.mult)
                step.then(dve.tensor_tensor(gate_b[:, s, :], gate_b[:, s, :], ps[b0 + 3][:], ALU.mult))
                dve.tensor_tensor(gate_a[:, s, :], gate_a[:, s, :], gate_b[:, s, :], ALU.add).then_inc(m_made, 1)
                dve.wait_ge(m_hi_ready, d + 1)
                dve.tensor_tensor(m_lo[:, d, :], gate_a[:, s, :], m_hi[:, d, :].bitcast(F32), ALU.subtract
                                  ).then_inc(m_ready, 1)
            residual(RESIDUAL_TILES, ALPHA, "mix", U_OUT, 1)
            layer_norm(1, LN_EPS, False)
            ffn_up(1)
            residual(2 * RESIDUAL_TILES, 2 * ALPHA, "ffn2", UP_UNITS, 4)
            layer_norm(2, 4 * LN_EPS, True)


def _dft_tables():
    k = np.arange(HALF)[None, :]
    s = np.arange(HALF)[:, None]
    def angle(t):
        return np.pi * (((2 * k + 1) * t) % (4 * SEQ)) / (2 * SEQ)
    ce, se = np.cos(angle(2 * s)), np.sin(angle(2 * s))
    co, so = np.cos(angle(2 * s + 1)), np.sin(angle(2 * s + 1))
    tables = np.stack([ce, co, se, so, ce.T, se.T]).astype(np.float32)
    return np.ascontiguousarray(tables.reshape(6, 2, P, HALF).transpose(2, 0, 1, 3))


def _split_tokens():
    return np.concatenate([np.arange(0, SEQ, 2), np.arange(1, SEQ, 2)])


def _filter_features():
    t = np.linspace(0.0, 1.0, SEQ, dtype=np.float32)[:, None]
    bands = (EMB - 1) // 2
    w = (np.float32(2.0 * np.pi / SEQ) * np.arange(SEQ, dtype=np.float32))[:, None]
    f = np.linspace(1e-4, bands - 1, bands, dtype=np.float32)[None, :]
    z = np.concatenate([t, np.cos(f * w), -np.sin(f * w)], axis=-1).astype(np.float32)
    return np.ascontiguousarray(z[_split_tokens()].T)


def _decay():
    t = np.linspace(0.0, 1.0, SEQ, dtype=np.float32)[:, None]
    lo, hi = np.log(1e-2) / 1.5, np.log(1e-2) / 0.3
    deltas = np.abs(np.linspace(lo, hi, HY_WIDTH, dtype=np.float32))
    d = np.exp(-t * deltas).astype(np.float32)[_split_tokens()]
    return np.ascontiguousarray(d.reshape(TT, P, HY_WIDTH).transpose(1, 0, 2))


def _window_mask():
    cq = np.arange(P) % KW
    out = []
    for b, groups in ((0, ((0, 8), (8, 16))), (1, ((8, 16), (24, 16))), (3, ((40, 16), (56, 8)))):
        start = np.clip(KW * b + cq - KW // 2, 0, GRID_W - KW)[:, None, None]
        for c0, n in groups:
            col = (c0 + np.arange(n))[None, None, :]
            ok = (col >= start) & (col < start + KW)
            out.append(np.broadcast_to(np.where(ok, 0.0, MASKED), (P, ROWS, n)).reshape(P, -1))
    return np.concatenate(out, axis=1).astype(np.float32)


def _col_tiles(w, first, n):
    kt = w.shape[0] // P
    t = w[:, first:first + n * P].reshape(kt, P, n, P)
    return np.ascontiguousarray(t.transpose(2, 1, 0, 3)).reshape(n, P, kt * P)


def _up_units(w1, w3):
    return np.ascontiguousarray(np.stack([_col_tiles(w1, 0, FT), _col_tiles(w3, 0, FT)], axis=1)
                                ).reshape(UP_UNITS, P, UP_W)


def _down_units(w2):
    t = w2.reshape(2, DOWN_K, P, DT, P).transpose(3, 0, 2, 1, 4)
    return np.ascontiguousarray(t).reshape(DOWN_UNITS, P, DOWN_W)


def _mixer_units(w_in, w_pa, w_pb, w_out):
    a_w, h_w = 3 * HEADS * HEAD_DIM, 3 * HY_WIDTH
    ga, gb = _col_tiles(w_in, a_w + h_w, DT), _col_tiles(w_in, a_w + h_w + D_MODEL, DT)
    pab = np.concatenate([_col_tiles(w_pa, 0, DT), _col_tiles(w_pb, 0, DT)], axis=2)
    gates = np.stack([ga, gb, pab], axis=1).reshape(3 * DT, P, UP_W)
    return np.ascontiguousarray(np.concatenate([
        _col_tiles(w_in, a_w, 3 * CT), _col_tiles(w_in, 0, CT), _col_tiles(w_in, 512, CT),
        _col_tiles(w_in, 1024, CT), gates,
        _col_tiles(w_out, 0, DT)], axis=0))


def _bias_segments(rpb):
    flat = np.pad(rpb.reshape(HEADS, -1), ((0, 0), (8, 8)))
    out = np.empty((P, HEADS, SEG), np.float32)
    for rq in range(ROWS):
        for cq in range(KW):
            a = 8 + (KH - 1 - rq) * (2 * KW - 1) + (7 - cq)
            out[rq * KW + cq] = flat[:, a:a + SEG]
    return out


def _columns(v):
    return np.asarray(v).reshape(-1, P).T


def kernel(**inputs):
    import concourse.bacc as bacc
    from concourse.bass_utils import run_bass_kernel_spmd

    a = {k: np.asarray(v)[0] for k, v in inputs.items()}
    xT = np.ascontiguousarray(a["x"].T.reshape(DT, P, SEQ).transpose(1, 0, 2))
    arrays = {
        "in_xT": xT,
        "in_params": np.ascontiguousarray(np.concatenate(
            [_columns(a[n]) for n in ("ln1_g", "ln1_b", "ln2_g", "ln2_b", "ln3_g", "ln3_b", "b_gate",
                                      "hy_short_w", "hy_short_b", "hy_bias")], axis=1)),
        "in_up1": _up_units(a["ffn1_w1"], a["ffn1_w3"]),
        "in_down1": _down_units(a["ffn1_w2"]),
        "in_mix": _mixer_units(a["w_in"], a["w_pa"], a["w_pb"], a["w_out"]),
        "in_up2": _up_units(a["ffn2_w1"], a["ffn2_w3"]),
        "in_down2": _down_units(a["ffn2_w2"]),
        "in_eye": np.eye(P, dtype=np.float32),
        "in_dft": _dft_tables(),
        "in_feat": _filter_features(),
        "in_filt1": np.ascontiguousarray(a["hy_filt_w1"]),
        "in_filt2": np.ascontiguousarray(a["hy_filt_w2"]),
        "in_filt_cols": np.ascontiguousarray(np.stack([a["hy_filt_b1"], a["hy_filt_b2"], a["hy_filt_freq"]], 1)),
        "in_filt3": np.concatenate([a["hy_filt_w3"], a["hy_filt_b3"][None]], axis=0),
        "in_decay": _decay(),
        "in_seg": _bias_segments(a["na_rpb"]),
        "in_mask": _window_mask(),
    }
    nc = bacc.Bacc("TRN2", target_bir_lowering=False, num_devices=1)
    args = [nc.dram_tensor(n, v.shape, mybir.dt.from_np(v.dtype), kind="ExternalInput").ap()
            for n, v in arrays.items()]
    args.append(nc.dram_tensor("out_yT", (P, DT, SEQ), F32, kind="ExternalOutput").ap())
    build(nc, *args)
    got = run_bass_kernel_spmd(nc, [arrays], core_ids=[0]).results[0]["out_yT"]
    return np.ascontiguousarray(np.asarray(got).transpose(1, 0, 2).reshape(D_MODEL, SEQ).T)[None]
```

```python
from contextlib import ExitStack

import numpy as np

import concourse.bass as bass
from concourse import mybir

F32 = mybir.dt.float32
F32R = mybir.dt.float32r
ALU = mybir.AluOpType
ACT = mybir.ActivationFunctionType
AX = mybir.AxisListType

P = 128
D_MODEL, SEQ, D_FF = 1024, 512, 2816
GRID_W, KW, KH = 64, 16, 8
ROWS = SEQ // GRID_W
HEADS, HEAD_DIM = 8, 64
HY_WIDTH, HY_ORDER, EMB, HID = 512, 2, 33, 64
DEPTH = 1
ALPHA = (2 * DEPTH) ** 0.25
LN_EPS = 1e-5

DT = D_MODEL // P
FT = D_FF // P
CT = HY_WIDTH // P
TT = SEQ // P
HALF = SEQ // 2

UP_W = DT * P
DOWN_K = FT // 2
DOWN_W = DOWN_K * P
SLOTS = 4
UP_UNITS, DOWN_UNITS = 2 * FT, 2 * DT
FFN_UNITS = UP_UNITS + DOWN_UNITS
FFN_SLOTS = UP_UNITS + 2 * DOWN_UNITS
U_HYENA, U_Q, U_K, U_V, U_MIX, U_OUT = 0, 3 * CT, 4 * CT, 5 * CT, 6 * CT, 6 * CT + 3 * DT
MIX_UNITS = U_OUT + DT
RESIDUAL_TILES = DT

C_LN = 0
C_GATE = C_LN + 6 * DT
C_SW = C_GATE + 2 * DT
C_SB = C_SW + 9 * CT
C_HB = C_SB + 3 * CT
N_PARAM = C_HB + HY_ORDER * CT

SEG = (KH - 1) * (2 * KW - 1) + 2 * KW
BLOCKS = GRID_W // KW
KEYS = 2 * P
MASKED = -1e30

MAGIC = 1.5 * 2 ** 23
TWO_PI_PARTS = (6.28125, 0.0019350051879882812, 3.019916050561733e-07)


class Steps:

    def __init__(self, eng, sem):
        self.eng, self.sem, self.n, self.turn, self.first = eng, sem, 0, None, 0

    def then(self, ins):
        ins.then_inc(self.sem, 1)
        self.n += 1
        self.eng.wait_ge(self.sem, self.n if self.turn is None else self.turn + self.n)

    def loop(self, i, per_turn):
        self.turn, self.first, self.per_turn = i * per_turn, self.n, per_turn

    def end(self, turns):
        assert self.n - self.first == self.per_turn, (self.n - self.first, self.per_turn)
        self.n = self.first + turns * self.per_turn
        self.turn = None


def build(nc, xT, params, up1, down1, mix_units, up2, down2, ident, dft, feat, filt1, filt2, filt_cols,
          filt3, decay, rpb_seg, na_mask, out):
    with ExitStack() as ctx:
        base = (nc.sbuf_base + 63) // 64 * 64
        KB = 1024

        def at(name, shape, dt, offset):
            return nc.alloc_sbuf_tensor_at(name, shape, dt, offset=base + offset)

        def sem(name):
            return ctx.enter_context(nc.semaphore(name))

        x_hi = at("x_hi", [P, DT, SEQ], F32R, 0)
        x_lo = at("x_lo", [P, DT, SEQ], F32R, 16 * KB)
        ring_hi = at("ring_hi", [P, SLOTS * UP_W], F32R, 32 * KB)
        ring_lo = at("ring_lo", [P, SLOTS * UP_W], F32R, 48 * KB)
        raw = at("raw", [P, 2, DOWN_W], F32, 64 * KB)
        fixed = 64 * KB + 2 * DOWN_W * 4
        par = at("par", [P, N_PARAM], F32, fixed)
        mean_of = at("mean_of", [P, P], F32, fixed + 512)
        eye = at("eye", [P, P], F32, fixed + 1024)
        u_pad = at("u_pad", [P, SEQ + 2], F32, fixed + 1536)
        kernel_scale = at("kernel_scale", [P, HY_ORDER, CT], F32, fixed + 1536 + 2112)
        R = fixed + 1536 + 2112 + 64
        y = at("y", [P, DT, SEQ], F32, R)
        act_gate = [y[:, p, :] for p in range(2)]
        h_prod = [y[:, 2 + p, :] for p in range(2)]
        h_hi = at("h_hi", [P, FT, SEQ], F32R, R + 16 * KB)
        h_lo = at("h_lo", [P, FT, SEQ], F32R, R + 60 * KB)
        squares = at("squares", [P, 2, SEQ], F32, R + 112 * KB)
        rstd = at("rstd", [P, SEQ], F32, R + 116 * KB)
        y_sum = at("y_sum", [P, SEQ], F32, R + 118 * KB)
        feat_sb = at("feat_sb", [EMB, SEQ], F32, R + 104 * KB)
        w_f1 = at("w_f1", [EMB, HID], F32, R + 106 * KB)
        w_f2 = at("w_f2", [HID, HID], F32, R + 106 * KB + 256)
        f_cols = at("f_cols", [HID, 3], F32, R + 106 * KB + 512)
        arg = at("arg", [HID, SEQ], F32, R + 108 * KB)
        turns = at("turns", [HID, SEQ], F32, R + 110 * KB)
        hid1 = at("hid1", [HID, SEQ], F32, R + 120 * KB)
        hid = at("hid", [HID + 1, SEQ], F32, R + 124 * KB)
        z0 = at("z0", [P, CT, SEQ], F32, R)
        z1 = at("z1", [P, CT, SEQ], F32, R + 8 * KB)
        part2 = at("part2", [P, CT, SEQ], F32, R + 16 * KB)
        parts = [z0, z1, part2]
        w_f3 = at("w_f3", [HID + 1, 2 * HY_ORDER * HY_WIDTH], F32, R + 16 * KB)
        dft_hi = at("dft_hi", [P, 6, 2, HALF], F32R, R + 24 * KB)
        dft_lo = at("dft_lo", [P, 6, 2, HALF], F32R, R + 36 * KB)
        spec_k = [at(f"spec_k{o}", [P, 2, 2, 2, HY_WIDTH], F32, R + (48 + 16 * o) * KB) for o in range(2)]
        decay_sb = at("decay_sb", [P, TT, HY_WIDTH], F32, R + 64 * KB)
        taps_hi = at("taps_hi", [P, 2, TT, HY_WIDTH], F32R, R + 80 * KB)
        taps_lo = at("taps_lo", [P, 2, TT, HY_WIDTH], F32R, R + 96 * KB)
        dft_raw = at("dft_raw", [P, 6, 2, HALF], F32, R + 80 * KB)
        zy_hi = at("zy_hi", [P, TT, HY_WIDTH], F32R, R + 80 * KB)
        zy_lo = at("zy_lo", [P, TT, HY_WIDTH], F32R, R + 88 * KB)
        spec_z = at("spec_z", [P, 2, 2, 2, HY_WIDTH], F32, R + 96 * KB)
        tap_f = at("tap_f", [P, HY_WIDTH], F32, R + 112 * KB)
        tap_b = at("tap_b", [P, HY_WIDTH], F32, R + 114 * KB)
        tap_pm = at("tap_pm", [P, 2, HY_WIDTH], F32, R + 116 * KB)
        tap_sq = at("tap_sq", [P, 2, HY_WIDTH], F32, R + 120 * KB)
        energy = at("energy", [P, HY_WIDTH], F32, R + 126 * KB)
        half_spec = at("half_spec", [P, HY_WIDTH], F32, R + 126 * KB)
        prod = [at(f"prod{n}", [P, 2, HY_WIDTH], F32, R + (112 + 4 * n) * KB) for n in range(3)]
        yb_hi = at("yb_hi", [P, CT, SEQ], F32R, R + 112 * KB)
        yb_lo = at("yb_lo", [P, CT, SEQ], F32R, R + 120 * KB)
        vT = at("vT", [P, CT, SEQ], F32, R + 88 * KB)
        qT = at("qT", [P, CT, SEQ], F32, R + 48 * KB)
        kT = at("kT", [P, CT, SEQ], F32, R + 56 * KB)
        seg_sb = at("seg_sb", [P, HEADS, SEG], F32, R + 64 * KB)
        mask_sb = at("mask_sb", [P, 3, KEYS], F32, R + 72 * KB)
        bias_sb = at("bias_sb", [P, 2, 3, KEYS], F32, R + 16 * KB)
        v_sb = at("v_sb", [P, 4, HEADS * HEAD_DIM], F32, R + 80 * KB)
        ya_hi = at("ya_hi", [P, CT, SEQ], F32R, R + 24 * KB)
        ya_lo = at("ya_lo", [P, CT, SEQ], F32R, R + 32 * KB)
        probs = at("probs", [P, 3, BLOCKS, KEYS], F32, R + 96 * KB)
        probsT = at("probsT", [P, 2, 2 * KEYS], F32, R + 108 * KB)
        neg_max = at("neg_max", [P, HEADS, BLOCKS], F32, R + 75 * KB)
        row_sum = at("row_sum", [P, HEADS, BLOCKS], F32, R + 75 * KB + 128)
        row_inv = at("row_inv", [P, HEADS, BLOCKS], F32, R + 75 * KB + 256)
        m_hi = at("m_hi", [P, DT, SEQ], F32R, R + 48 * KB)
        m_lo = at("m_lo", [P, DT, SEQ], F32R, R + 64 * KB)
        gate_a = at("gate_a", [P, 2, SEQ], F32, R + 96 * KB)
        gate_b = at("gate_b", [P, 2, SEQ], F32, R + 100 * KB)

        ps = [ctx.enter_context(nc.psum_tensor(f"ps{n}", [P, SEQ], F32)) for n in range(8)]
        MEAN, VAR = ps[6], ps[7]

        raw_loaded = [sem("raw_loaded0"), sem("raw_loaded1")]
        x_loaded, small_loaded, filt_loaded = sem("x_loaded"), sem("small_loaded"), sem("filt_loaded")
        mixer_loaded, na_loaded, stored = sem("mixer_loaded"), sem("na_loaded"), sem("stored")
        unit_hi, unit_lo, ring_freed = sem("unit_hi"), sem("unit_lo"), sem("ring_freed")
        mean_set = sem("mean_set")
        x_hi_ready, x_ready = sem("x_hi_ready"), sem("x_ready")
        up_freed, gate_ready = sem("up_freed"), sem("gate_ready")
        h_hi_ready, h_ready = sem("h_hi_ready"), sem("h_ready")
        res_freed = sem("res_freed")
        y_summed, mean_ready, centred = sem("y_summed"), sem("mean_ready"), sem("centred")
        squared, var_step, var_eps, std_ready = sem("squared"), sem("var_step"), sem("var_eps"), sem("std_ready")
        scaled, final_ready = sem("scaled"), sem("final_ready")
        dve_step, pool_step, act_step = sem("dve_step"), sem("pool_step"), sem("act_step")
        hid_mm, arg_ready, hid_ready, ones_row = sem("hid_mm"), sem("arg_ready"), sem("hid_ready"), sem("ones_row")
        dft_ready = sem("dft_ready")
        proj_freed, pad_ready, conv_ready = sem("proj_freed"), sem("pad_ready"), sem("conv_ready")
        filt_mm, filt_freed, taps_made, taps_hi_ready, taps_ready = (
            sem("filt_mm"), sem("filt_freed"), sem("taps_made"), sem("taps_hi_ready"), sem("taps_ready"))
        energy_ready, energy_mm, energy_eps, energy_std, scale_ready = (
            sem("energy_ready"), sem("energy_mm"), sem("energy_eps"), sem("energy_std"), sem("scale_ready"))
        spec_mm, spec_half, spec_freed = sem("spec_mm"), sem("spec_half"), sem("spec_freed")
        zt_ready, z_hi_ready, z_ready = sem("zt_ready"), sem("z_hi_ready"), sem("z_ready")
        spec_made, spec_hi_ready, spec_ready = sem("spec_made"), sem("spec_hi_ready"), sem("spec_ready")
        inv_mm, inv_ready, gated = sem("inv_mm"), sem("inv_ready"), sem("gated")
        yb_hi_ready, yb_ready = sem("yb_hi_ready"), sem("yb_ready")
        qk_ready, vt_ready, v_mm, v_ready = sem("qk_ready"), sem("vt_ready"), sem("v_mm"), sem("v_ready")
        bias_ready, score_mm, scored, max_ready, exp_ready, prob_ready = (
            sem("bias_ready"), sem("score_mm"), sem("scored"), sem("max_ready"), sem("exp_ready"),
            sem("prob_ready"))
        pt_mm, pt_ready, pv_mm, ya_hi_ready, ya_ready = (
            sem("pt_mm"), sem("pt_ready"), sem("pv_mm"), sem("ya_hi_ready"), sem("ya_ready"))
        gates_ready, m_made, m_hi_ready, m_ready = (
            sem("gates_ready"), sem("m_made"), sem("m_hi_ready"), sem("m_ready"))

        UNIT0 = {"ffn1": 0, "mix": FFN_UNITS, "ffn2": FFN_UNITS + MIX_UNITS}
        SLOT0 = {"ffn1": 0, "mix": FFN_SLOTS, "ffn2": FFN_SLOTS + MIX_UNITS}

        def used(phase, slots):
            return SLOTS + SLOT0[phase] + slots

        block = ctx.enter_context(nc.Block())

        @block.sync
        def _(sp):
            sp.dma_start(feat_sb[:], feat).then_inc(filt_loaded, 16)
            sp.dma_start(w_f1[:], filt1).then_inc(filt_loaded, 16)
            sp.dma_start(w_f2[:], filt2).then_inc(filt_loaded, 16)
            sp.dma_start(f_cols[:], filt_cols).then_inc(filt_loaded, 16)
            sp.dma_start(par[:], params).then_inc(small_loaded, 16)
            sp.dma_start(eye[:], ident).then_inc(small_loaded, 16)
            for half in range(2):
                a = half * DT // 2
                sp.dma_start(y[:, a:a + DT // 2, :], xT[:, a:a + DT // 2, :]).then_inc(x_loaded, 16)

            def units(src, width, n, first):
                with sp.Fori(0, n // 2) as i:
                    for s in range(2):
                        sp.wait_ge(unit_lo, i * 2 + (first + s - 1))
                        sp.dma_start(raw[:, s, 0:width], src[i * 2 + s]).then_inc(raw_loaded[s], 16)

            def ffn(up, down, u0):
                skip = 2 if u0 == 0 else 0
                for u in range(skip):
                    sp.dma_start(raw[:, u, 0:UP_W], up[u]).then_inc(raw_loaded[u], 16)
                units(up[skip:], UP_W, UP_UNITS - skip, u0 + skip)
                units(down, DOWN_W, DOWN_UNITS, u0 + UP_UNITS)

            ffn(up1, down1, 0)
            u0 = UNIT0["mix"]
            units(mix_units[0:4], UP_W, 4, u0)
            sp.wait_ge(ring_freed, used("ffn1", FFN_SLOTS))
            sp.dma_start(dft_raw[:], dft).then_inc(mixer_loaded, 16)
            sp.dma_start(w_f3[:], filt3).then_inc(mixer_loaded, 16)
            sp.dma_start(decay_sb[:], decay).then_inc(mixer_loaded, 16)
            units(mix_units[4:U_MIX], UP_W, U_MIX - 4, u0 + 4)
            sp.wait_ge(spec_made, 4)
            sp.dma_start(seg_sb[:], rpb_seg).then_inc(na_loaded, 16)
            sp.dma_start(mask_sb[:], na_mask).then_inc(na_loaded, 16)
            units(mix_units[U_MIX:], UP_W, MIX_UNITS - U_MIX, u0 + U_MIX)
            ffn(up2, down2, UNIT0["ffn2"])
            for d in range(DT):
                sp.wait_ge(final_ready, d + 1)
                sp.dma_start(out[:, d, :], y[:, d, :]).then_inc(stored, 16)
            sp.wait_ge(stored, 16 * DT)

        @block.gpsimd
        def _(pool):
            pool.sem_inc(ring_freed, SLOTS)

            def split(slot, width, raw_slot, unit):
                hi = ring_hi[:, slot * UP_W:slot * UP_W + width]
                lo = ring_lo[:, slot * UP_W:slot * UP_W + width]
                pool.wait_ge(unit_hi, unit + 1)
                pool.tensor_tensor(lo, raw[:, raw_slot, 0:width], hi.bitcast(F32), ALU.subtract
                                   ).then_inc(unit_lo, 1)

            def up_units(n, unit0):
                with pool.Fori(0, n // SLOTS) as i:
                    for s in range(SLOTS):
                        split(s, UP_W, s % 2, i * SLOTS + (unit0 + s))

            def down_units(unit0):
                with pool.Fori(0, DOWN_UNITS // 2) as i:
                    for s in range(2):
                        split(2 * s, DOWN_W, s, i * 2 + (unit0 + s))

            up_units(UP_UNITS, 0)
            down_units(UP_UNITS)
            u0 = UNIT0["mix"]
            up_units(4, u0)
            pool.wait_ge(mixer_loaded, 48)
            pool.tensor_copy(dft_hi[:], dft_raw[:]).then_inc(pool_step, 1)
            pool.wait_ge(pool_step, 1)
            pool.tensor_tensor(dft_lo[:], dft_raw[:], dft_hi[:].bitcast(F32), ALU.subtract).then_inc(dft_ready, 1)
            up_units(U_MIX, u0 + 4)
            pool.wait_ge(na_loaded, 32)
            pool.wait_ge(gated, 2 * CT)
            for h in range(HEADS):
                if h >= 2:
                    pool.wait_ge(scored, 2 * (h - 1))
                pos = 0
                for c0, cols in ((8, 8), (8, 8), (16, 16), (0, 16), (16, 16), (0, 16), (16, 8), (16, 8)):
                    w = ROWS * cols
                    seg = bass.AP(seg_sb[:].tensor, seg_sb[:, h, c0:c0 + 1].offset,
                                  [list(seg_sb[:].ap[0]), [2 * KW - 1, ROWS], [1, cols]])
                    there = lambda t: t.rearrange("p a k -> p (a k)")[:, pos:pos + w].rearrange(
                        "p (r c) -> p r c", r=ROWS)
                    last = pool.tensor_tensor(there(bias_sb[:, h % 2]), seg, there(mask_sb[:]), ALU.add)
                    pos += w
                last.then_inc(bias_ready, 1)
            up_units(MIX_UNITS - U_MIX - 4, u0 + U_MIX + 4)
            up_units(UP_UNITS, UNIT0["ffn2"])
            down_units(UNIT0["ffn2"] + UP_UNITS)

        @block.tensor
        def _(pe):
            def mm3(out_ps, lhs_hi, lhs_lo, rhs_hi, rhs_lo, start, stop, **kw):
                pe.matmul(out_ps, lhs_hi, rhs_hi, start=start, stop=False, **kw)
                pe.matmul(out_ps, lhs_hi, rhs_lo, start=False, stop=False, **kw)
                return pe.matmul(out_ps, lhs_lo, rhs_hi, start=False, stop=stop, **kw)

            def tile_of(slot, k):
                a = slot * UP_W + k * P
                return ring_hi[:, a:a + P], ring_lo[:, a:a + P]

            def unit_times(slot, out_ps, mov_hi, mov_lo, tiles=DT, first=0, start=True, stop=True):
                for k in range(tiles):
                    w_hi, w_lo = tile_of(slot, k + first)
                    last = mm3(out_ps, w_hi, w_lo, mov_hi(k), mov_lo(k), start and k == 0,
                               stop and k == tiles - 1)
                return last

            x_tile = (lambda k: x_hi[:, k, :], lambda k: x_lo[:, k, :])

            def ffn_up(f, unit0, x_count):
                pe.wait_ge(x_ready, x_count)
                with pe.Fori(0, FT // 2) as i:
                    for p in range(2):
                        pe.wait_ge(up_freed, i * 2 + (f * FT + p + 1))
                        for m in range(2):
                            s = 2 * p + m
                            pe.wait_ge(unit_lo, i * SLOTS + (unit0 + s + 1))
                            unit_times(s, ps[s][:], *x_tile).then_inc(ring_freed, 1)

            def ffn_down(f, r0, unit0):
                pe.wait_ge(h_ready, (f + 1) * FT)
                with pe.Fori(0, DT // 2) as i:
                    for p in range(2):
                        pe.wait_ge(res_freed, i * 2 + (r0 + p + 1))
                        for half in range(2):
                            pe.wait_ge(unit_lo, i * 4 + (unit0 + 2 * p + half + 1))
                            k0 = half * DOWN_K
                            last = unit_times(2 * half, ps[4 + p][:], lambda k: h_hi[:, k0 + k, :],
                                              lambda k: h_lo[:, k0 + k, :], tiles=DOWN_K,
                                              start=half == 0, stop=half == 1)
                            last.then_inc(ring_freed, 2)

            def layer_norm(n):
                pe.wait_ge(y_summed, n + 1)
                pe.matmul(MEAN[:], mean_of[:], y_sum[:], start=True, stop=True).then_inc(mean_ready, 1)
                for d in range(DT):
                    pe.wait_ge(squared, n * DT + d + 1)
                    pe.matmul(VAR[:], mean_of[:], squares[:, d % 2, :], start=d == 0, stop=d == DT - 1
                              ).then_inc(var_step, 1)

            pe.wait_ge(filt_loaded, 64)
            pe.matmul(ps[7][0:HID, :], w_f1[:], feat_sb[:], start=True, stop=True).then_inc(hid_mm, 1)
            pe.wait_ge(hid_ready, 1)
            pe.matmul(ps[7][0:HID, :], w_f2[:], hid1[:], start=True, stop=True).then_inc(hid_mm, 1)

            pe.wait_ge(mean_set, 3)
            ffn_up(0, 0, DT)
            ffn_down(0, 0, UP_UNITS)
            layer_norm(0)

            u0 = UNIT0["mix"]
            pe.wait_ge(x_ready, 2 * DT)

            def project(n):
                pe.wait_ge(proj_freed, n + 1)
                pe.wait_ge(unit_lo, u0 + n + 1)
                unit_times(n % SLOTS, ps[n % 2][:], *x_tile).then_inc(ring_freed, 1)

            def filter_tile(n):
                o, t = n // TT, n % TT
                if n >= 2:
                    pe.wait_ge(filt_freed, n - 1)
                if n == TT:
                    pe.wait_ge(spec_freed, 4)
                tokens = hid[:, t * P:(t + 1) * P]
                for way in range(2):
                    col = (way * HY_ORDER + o) * HY_WIDTH
                    last = pe.matmul(ps[2 + 2 * (n % 2) + way][:], tokens, w_f3[:, col:col + HY_WIDTH],
                                     start=True, stop=True)
                last.then_inc(filt_mm, 1)

            def spectrum(v0, src, kinds):
                for kt in range(2):
                    for rs in range(2):
                        v = v0 + 2 * kt + rs
                        if v - v0 >= 2:
                            pe.wait_ge(spec_freed, v - 1)
                        for odd in range(2):
                            for t in range(2):
                                hi, lo = (w[:, 2 * rs + odd, t, kt * P:(kt + 1) * P] for w in (dft_hi, dft_lo))
                                s_hi, s_lo = src(rs, 2 * odd + t)
                                last = mm3(ps[2 + 2 * rs + odd][:], hi, lo, s_hi, s_lo, t == 0, t == 1)
                        last.then_inc(spec_mm, 1)

            taps = lambda rs, t: (taps_hi[:, rs, t, :], taps_lo[:, rs, t, :])
            z_of = lambda rs, t: (zy_hi[:, t, :], zy_lo[:, t, :])

            def energy_sum(o):
                pe.wait_ge(energy_ready, o + 1)
                for c in range(CT):
                    last = pe.matmul(ps[7][:, c:c + 1], energy[:, c * P:(c + 1) * P], mean_of[:, 0:1],
                                     start=True, stop=True)
                last.then_inc(energy_mm, 1)

            def turn_z(o):
                for t in range(TT):
                    if t >= 2:
                        pe.wait_ge(z_ready, o * TT + t - 1)
                    for c in range(CT):
                        last = pe.transpose(ps[6 + t % 2][:, c * P:(c + 1) * P],
                                            parts[o][:, c, t * P:(t + 1) * P], eye[:])
                    last.then_inc(zt_ready, 1)

            def inverse(o, kt):
                pe.wait_ge(spec_ready, 2 * o + kt + 1)
                for c in range(CT):
                    cols = slice(c * P, (c + 1) * P)
                    for odd, mats in ((0, (4, 5)), (1, (1, 3))):
                        for rs in range(2):
                            a = 2 * rs + odd
                            first = kt == 0 and odd == 0 and rs == 0
                            last = mm3(ps[2 + c][:, odd * HALF:(odd + 1) * HALF],
                                       zy_hi[:, a, cols], zy_lo[:, a, cols],
                                       dft_hi[:, mats[rs], kt, :], dft_lo[:, mats[rs], kt, :],
                                       first, kt == 1 and rs == 1, skip_group_check=True)
                    if kt == 1:
                        last.then_inc(inv_ready, 1)
                if kt == 0:
                    last.then_inc(inv_mm, 1)

            pe.wait_ge(mixer_loaded, 48)
            pe.wait_ge(ones_row, 1)
            pe.wait_ge(hid_ready, 2)
            pe.wait_ge(dft_ready, 1)
            for n in range(TT):
                project(n)
                filter_tile(n)
            project(TT)
            energy_sum(0)
            pe.wait_ge(taps_ready, TT)
            spectrum(0, taps, 2)
            filter_tile(TT)
            for n in range(TT + 1, 2 * TT):
                project(n)
                filter_tile(n)
            pe.wait_ge(conv_ready, CT)
            energy_sum(1)
            pe.wait_ge(taps_ready, 2 * TT)
            spectrum(4, taps, 2)
            for o in range(HY_ORDER):
                if o:
                    pe.wait_ge(gated, CT)
                turn_z(o)
                pe.wait_ge(z_ready, (o + 1) * TT)
                spectrum(8 + 4 * o, z_of, 1)
                for n in (range(2 * CT, 3 * CT) if o == 0 else range(3 * CT, 5 * CT)):
                    project(n)
                pe.wait_ge(spec_freed, 12 + 4 * o)
                inverse(o, 0)
                inverse(o, 1)

            for n in range(5 * CT, 6 * CT):
                project(n)
            for g in range(TT):
                pe.wait_ge(vt_ready, CT)
                if g >= 2:
                    pe.wait_ge(v_ready, g - 1)
                for c in range(CT):
                    last = pe.transpose(ps[6 + g % 2][:, c * P:(c + 1) * P], vT[:, c, g * P:(g + 1) * P], eye[:])
                last.then_inc(v_mm, 1)

            def score(h):
                if h >= 2:
                    pe.wait_ge(scored, 2 * (h - 1))
                row = slice((h % 2) * HEAD_DIM, (h % 2 + 1) * HEAD_DIM)
                for b in range(BLOCKS):
                    q = qT[row, h // 2, b * P:(b + 1) * P]
                    bank, col = ps[2 * (h % 2) + b // 2], (b % 2) * KEYS
                    if b < 3:
                        last = pe.matmul(bank[:, col:col + KEYS], q, kT[row, h // 2, b * P:(b + 2) * P],
                                         start=True, stop=True)
                    else:
                        pe.matmul(bank[:, col:col + P], q, kT[row, h // 2, 3 * P:4 * P], start=True, stop=True)
                        last = pe.matmul(bank[:, col + P:col + KEYS], q, kT[row, h // 2, 0:P],
                                         start=True, stop=True)
                    if b % 2:
                        last.then_inc(score_mm, 1)

            def turn_probs(h):
                for j in range(2):
                    pe.wait_ge(prob_ready, 2 * h + j + 1)
                    if h >= 1:
                        pe.wait_ge(pt_ready, 2 * (h - 1) + j + 1)
                    for n in range(4):
                        last = pe.transpose(ps[4 + j][:, n * P:(n + 1) * P],
                                            probs[:, h % 3, 2 * j + n // 2, (n % 2) * P:(n % 2 + 1) * P], eye[:])
                    last.then_inc(pt_mm, 1)

            def values(h):
                if h % 2 == 0 and h >= 4:
                    pe.wait_ge(ya_ready, h // 2 - 1)
                for b in range(BLOCKS):
                    if b % 2 == 0:
                        pe.wait_ge(pt_ready, 2 * h + b // 2 + 1)
                    out_ps = ps[6 + (h // 2) % 2][(h % 2) * HEAD_DIM:(h % 2 + 1) * HEAD_DIM, b * P:(b + 1) * P]
                    for n in range(2):
                        col = (b % 2) * KEYS + n * P
                        last = pe.matmul(out_ps, v_sb[:, (b + n) % 4, h * HEAD_DIM:(h + 1) * HEAD_DIM],
                                         probsT[:, b // 2, col:col + P], start=n == 0, stop=n == 1)
                    if b % 2:
                        last.then_inc(pv_mm, 1)

            pe.wait_ge(v_ready, 4)
            pe.wait_ge(qk_ready, 2 * CT)
            score(0)
            score(1)
            for h in range(HEADS):
                turn_probs(h)
                if h + 2 < HEADS:
                    score(h + 2)
                values(h)

            pe.wait_ge(ya_ready, CT)
            pe.wait_ge(yb_ready, CT)
            ya_t = (lambda k: ya_hi[:, k, :], lambda k: ya_lo[:, k, :])
            yb_t = (lambda k: yb_hi[:, k, :], lambda k: yb_lo[:, k, :])
            with pe.Fori(0, 2) as i:
                for d in range(4):
                    b0 = 4 * (d % 2)
                    pe.wait_ge(m_made, i * 4 + (d + 1))
                    for m in range(3):
                        n = 3 * d + m
                        pe.wait_ge(unit_lo, i * 12 + (u0 + U_MIX + n + 1))
                        if m < 2:
                            last = unit_times(n % SLOTS, ps[b0 + m][:], *x_tile)
                        else:
                            unit_times(n % SLOTS, ps[b0 + 2][:], *ya_t, tiles=CT)
                            last = unit_times(n % SLOTS, ps[b0 + 3][:], *yb_t, tiles=CT, first=CT)
                        last.then_inc(ring_freed, 1)
            pe.wait_ge(m_ready, DT)
            m_t = (lambda k: m_hi[:, k, :], lambda k: m_lo[:, k, :])
            with pe.Fori(0, DT // 4) as i:
                for s in range(4):
                    pe.wait_ge(res_freed, i * 4 + (RESIDUAL_TILES + s + 1))
                    pe.wait_ge(unit_lo, i * 4 + (u0 + U_OUT + s + 1))
                    unit_times(s, ps[4 + s % 2][:], *m_t).then_inc(ring_freed, 1)
            layer_norm(1)

            ffn_up(1, UNIT0["ffn2"], 3 * DT)
            ffn_down(1, 2 * RESIDUAL_TILES, UNIT0["ffn2"] + UP_UNITS)
            layer_norm(2)

        @block.scalar
        def _(act):
            def split_x():
                act.wait_ge(x_loaded, 32)
                for d in range(DT):
                    act.activation(x_hi[:, d, :], y[:, d, :], ACT.Copy).then_inc(x_hi_ready, 1)

            def unit_hi_of(width, slot, raw_slot, nth_load, slots_taken):
                act.wait_ge(raw_loaded[raw_slot], nth_load * 16)
                act.wait_ge(ring_freed, slots_taken)
                act.activation(ring_hi[:, slot * UP_W:slot * UP_W + width], raw[:, raw_slot, 0:width],
                               ACT.Copy).then_inc(unit_hi, 1)

            def up_hi(phase, n, i=0):
                unit_hi_of(UP_W, n % SLOTS, n % 2, i * 2 + (UNIT0[phase] // 2 + n // 2 + 1),
                           i * 4 + (SLOT0[phase] + n + 1))

            def down_hi(phase, n, i=0):
                unit_hi_of(DOWN_W, 2 * (n % 2), n % 2, i + ((UNIT0[phase] + UP_UNITS) // 2 + n // 2 + 1),
                           i * 4 + (SLOT0[phase] + UP_UNITS + 2 * (n + 1)))

            AHEAD = 3
            mix_hi_done = [0]

            def mix_hi(n):
                while mix_hi_done[0] <= min(n, MIX_UNITS - 1):
                    up_hi("mix", mix_hi_done[0])
                    mix_hi_done[0] += 1

            def ffn_up(f):
                phase = ("ffn1", "ffn2")[f]

                def tile(j, p, i):
                    act.wait_ge(ring_freed, i * 4 + used(phase, 2 * j + 2))
                    act.activation(act_gate[p], ps[2 * p][:], ACT.Silu).then_inc(gate_ready, 1)
                    act.wait_ge(up_freed, i * 2 + (2 + f * FT + j + 1))
                    act.activation(h_hi[:, i * 2 + j, :], h_prod[p], ACT.Copy).then_inc(h_hi_ready, 1)

                with act.Fori(0, FT // 2 - 1) as i:
                    for p in range(2):
                        up_hi(phase, 2 * p + AHEAD, i)
                        up_hi(phase, 2 * p + AHEAD + 1, i)
                        tile(p, p, i)
                up_hi(phase, UP_UNITS - 1)
                tile(FT - 2, 0, 0)
                down_hi(phase, 0)
                tile(FT - 1, 1, 0)
                down_hi(phase, 1)
                with act.Fori(0, DOWN_UNITS // 2 - 1) as i:
                    for s in range(2):
                        down_hi(phase, 2 + s, i)

            def layer_norm(n, last):
                for d in range(DT):
                    act.wait_ge(centred, n * DT + d + 1)
                    if d >= 2:
                        act.wait_ge(var_step, n * DT + d - 1)
                    act.activation(squares[:, d % 2, :], y[:, d, :], ACT.Square).then_inc(squared, 1)
                act.wait_ge(var_eps, n + 1)
                act.activation(rstd[:], rstd[:], ACT.Sqrt).then_inc(std_ready, 1)
                for d in range(DT):
                    b = par[:, (2 * n + 1) * DT + d:(2 * n + 1) * DT + d + 1]
                    act.wait_ge(scaled, n * DT + d + 1)
                    if last:
                        act.activation(y[:, d, :], y[:, d, :], ACT.Identity, bias=b).then_inc(final_ready, 1)
                    else:
                        act.activation(x_hi[:, d, :], y[:, d, :], ACT.Identity, bias=b).then_inc(x_hi_ready, 1)

            act.wait_ge(small_loaded, 32)
            for n in range(2):
                act.wait_ge(arg_ready, n + 1)
                act.activation((hid1, hid)[n][0:HID, :], arg[:], ACT.Sin).then_inc(hid_ready, 1)
            for n in range(2):
                up_hi("ffn1", n)
            split_x()
            up_hi("ffn1", 2)
            ffn_up(0)
            mix_hi(3)
            layer_norm(0, False)

            act.sem_inc(proj_freed, 2)
            act.wait_ge(mean_set, 3)

            def pad_part(n):
                part, c = n // CT, n % CT
                mix_hi(n + AHEAD)
                if n >= 1:
                    act.wait_ge(conv_ready, n)
                act.wait_ge(ring_freed, used("mix", n + 1))
                act.activation(u_pad[:, 1:SEQ + 1], ps[n % 2][:], ACT.Copy).then_inc(pad_ready, 1)
                act.activation(parts[part][:, c, :].rearrange("p (two s) -> p s two", two=2),
                               ps[n % 2][:].rearrange("p (s two) -> p s two", two=2), ACT.Identity,
                               scale=par[:, C_SW + 3 * CT + n:C_SW + 3 * CT + n + 1],
                               bias=par[:, C_SB + n:C_SB + n + 1]).then_inc(pad_ready, 1)
                act.wait_ge(pad_ready, 2 * n + 2)
                act.sem_inc(proj_freed, 1)

            def by_group(dst, bank):
                act.activation(dst[:, 0:P].rearrange("p (s r w) -> p s r w", s=2, w=8),
                               bank.rearrange("p (r s w) -> p s r w", s=8, w=8)[:, 0:8:7], ACT.Copy)
                return act.activation(dst[:, P:].rearrange("p (g r w) -> p g r w", g=3, w=KW),
                                      bank.rearrange("p (r w) -> p r w", w=GRID_W)[:, :, 8:56].rearrange(
                                          "p r (g w) -> p g r w", w=KW), ACT.Copy)

            def tap_hi(n):
                act.wait_ge(taps_made, n + 1)
                if n == TT:
                    act.wait_ge(spec_mm, 4)
                t = n % TT
                act.activation(taps_hi[:, :, t, :], tap_pm[:], ACT.Copy).then_inc(taps_hi_ready, 1)
                act.activation(tap_sq[:], tap_pm[:], ACT.Square).then_inc(taps_hi_ready, 1)

            def spec_evac(v0):
                for v in range(v0, v0 + 4):
                    act.wait_ge(spec_mm, v + 1)
                    if v >= 1:
                        act.wait_ge(spec_freed, v)
                    act.activation(half_spec[:], ps[2 + 2 * (v % 2)][:], ACT.Copy).then_inc(spec_half, 1)

            def energy_sqrt(o):
                act.wait_ge(energy_eps, o + 1)
                act.activation(kernel_scale[:, o, :], kernel_scale[:, o, :], ACT.Sqrt).then_inc(energy_std, 1)

            for n in range(TT):
                pad_part(n)
                tap_hi(n)
            pad_part(TT)
            energy_sqrt(0)
            spec_evac(0)
            tap_hi(TT)
            for n in range(TT + 1, 2 * TT):
                pad_part(n)
                tap_hi(n)
            energy_sqrt(1)
            spec_evac(4)
            for o in range(HY_ORDER):
                for t in range(TT):
                    act.wait_ge(zt_ready, o * TT + t + 1)
                    act.activation(zy_hi[:, t, :], ps[6 + t % 2][:], ACT.Copy).then_inc(z_hi_ready, 1)
                spec_evac(8 + 4 * o)

                def product_hi(kt):
                    act.wait_ge(spec_made, 2 * o + kt + 1)
                    if kt:
                        act.wait_ge(inv_mm, o + 1)
                    act.activation(zy_hi[:], spec_z[:, kt].rearrange("p a b c -> p (a b) c"), ACT.Copy
                                   ).then_inc(spec_hi_ready, 1)

                if o == 0:
                    pad_part(2 * CT)
                    pad_part(2 * CT + 1)
                    product_hi(0)
                    pad_part(2 * CT + 2)
                    pad_part(2 * CT + 3)
                    product_hi(1)
                else:
                    for n in range(2 * CT):
                        if n == 4:
                            product_hi(0)
                        mix_hi(3 * CT + n + AHEAD)
                        act.wait_ge(ring_freed, used("mix", 3 * CT + n + 1))
                        if n < CT:
                            act.activation(qT[:, n, :].rearrange("p (b r w) -> p b r w", r=ROWS, w=KW),
                                           ps[n % 2][:].rearrange("p (r b w) -> p b r w", r=ROWS, w=KW),
                                           ACT.Copy).then_inc(qk_ready, 1)
                        else:
                            by_group(kT[:, n - CT, :], ps[n % 2][:]).then_inc(qk_ready, 1)
                        act.wait_ge(qk_ready, n + 1)
                        act.sem_inc(proj_freed, 1)
                    product_hi(1)
            for c in range(CT):
                act.wait_ge(gated, CT + c + 1)
                act.activation(yb_hi[:, c, :], z0[:, c, :], ACT.Copy).then_inc(yb_hi_ready, 1)
            act.wait_ge(inv_ready, 2 * CT)
            for n in range(CT):
                bank, vt = ps[n % 2][:], vT[:, n, :]
                mix_hi(U_V + n + AHEAD)
                act.wait_ge(ring_freed, used("mix", U_V + n + 1))
                by_group(vt, bank).then_inc(vt_ready, 1)
                act.wait_ge(vt_ready, n + 1)
                act.sem_inc(proj_freed, 1)
            mix_hi(U_MIX + 3)
            for g in range(TT):
                act.wait_ge(v_mm, g + 1)
                act.activation(v_sb[:, g, :], ps[6 + g % 2][:], ACT.Copy).then_inc(v_ready, 1)

            def exp_scores(h):
                act.wait_ge(max_ready, h + 1)
                for b in range(BLOCKS):
                    last = act.activation(probs[:, h % 3, b, :], probs[:, h % 3, b, :], ACT.Exp,
                                          bias=neg_max[:, h, b:b + 1], accum_out=row_sum[:, h, b:b + 1])
                    last.then_inc(exp_ready, 1)

            by_block = lambda t, c: t[:, c, :].rearrange("p (r b w) -> p b r w", b=BLOCKS, w=KW)
            exp_scores(0)
            exp_scores(1)
            for h in range(HEADS):
                for j in range(2):
                    act.wait_ge(pt_mm, 2 * h + j + 1)
                    if h >= 1:
                        act.wait_ge(pv_mm, 2 * (h - 1) + j + 1)
                    act.activation(probsT[:, j, :], ps[4 + j][:], ACT.Copy).then_inc(pt_ready, 1)
                if h + 2 < HEADS:
                    exp_scores(h + 2)
                if h % 2:
                    c = h // 2
                    act.wait_ge(pv_mm, 2 * (h + 1))
                    act.activation(by_block(ya_hi, c), ps[6 + c % 2][:].rearrange(
                        "p (b r w) -> p b r w", b=BLOCKS, w=KW), ACT.Copy).then_inc(ya_hi_ready, 1)

            for d in range(DT):
                mix_hi(U_MIX + 3 * d + 2 + AHEAD)
                act.wait_ge(ring_freed, used("mix", U_MIX + 3 * (d + 1)))
                b0 = 4 * (d % 2)
                for br, dst in ((0, gate_a), (1, gate_b)):
                    col = C_GATE + br * DT + d
                    last = act.activation(dst[:, d % 2, :], ps[b0 + br][:], ACT.Sigmoid, bias=par[:, col:col + 1])
                last.then_inc(gates_ready, 1)
                act.wait_ge(m_made, 2 + d + 1)
                act.activation(m_hi[:, d, :], gate_a[:, d % 2, :], ACT.Copy).then_inc(m_hi_ready, 1)
            mix_hi(MIX_UNITS - 1)
            for n in range(AHEAD):
                up_hi("ffn2", n)
            layer_norm(1, False)
            ffn_up(1)
            layer_norm(2, True)

        @block.vector
        def _(dve):
            step = Steps(dve, dve_step)
            dve.memset(mean_of[:], 1.0 / D_MODEL).then_inc(mean_set, 1)
            dve.memset(hid[HID:HID + 1, :], 1.0).then_inc(ones_row, 1)
            dve.memset(u_pad[:, 0:1], 0.0).then_inc(mean_set, 1)
            dve.memset(u_pad[:, SEQ + 1:SEQ + 2], 0.0).then_inc(mean_set, 1)
            dve.sem_inc(up_freed, 2)
            dve.sem_inc(res_freed, 2)
            dve.sem_inc(m_made, 2)

            def ffn_up(f):
                with dve.Fori(0, FT // 2) as i:
                    for p in range(2):
                        dve.wait_ge(gate_ready, i * 2 + (f * FT + p + 1))
                        dve.tensor_tensor(h_prod[p], act_gate[p], ps[2 * p + 1][:], ALU.mult
                                          ).then_inc(up_freed, 1)
                        dve.wait_ge(h_hi_ready, i * 2 + (f * FT + p + 1))
                        dve.tensor_tensor(h_lo[:, i * 2 + p, :], h_prod[p], h_hi[:, i * 2 + p, :].bitcast(F32),
                                          ALU.subtract).then_inc(h_ready, 1)

            def residual(r0, scale, phase, slot0, slots):
                for d in range(DT):
                    dve.wait_ge(ring_freed, used(phase, slot0 + (d + 1) * slots))
                    dve.scalar_tensor_tensor(y[:, d, :], x_hi[:, d, :].bitcast(F32), scale,
                                             ps[4 + d % 2][:], ALU.mult, ALU.add).then_inc(res_freed, 1)
                    dve.wait_ge(res_freed, 2 + r0 + d + 1)
                    step.then(dve.scalar_tensor_tensor(y[:, d, :], x_lo[:, d, :].bitcast(F32), scale,
                                                       y[:, d, :], ALU.mult, ALU.add))
                    if d == 0:
                        step.then(dve.tensor_copy(y_sum[:], y[:, 0, :]))
                    else:
                        last = dve.tensor_tensor(y_sum[:], y_sum[:], y[:, d, :], ALU.add)
                        if d == DT - 1:
                            last.then_inc(y_summed, 1)
                        else:
                            step.then(last)

            def layer_norm(n, eps, last):
                dve.wait_ge(mean_ready, n + 1)
                for d in range(DT):
                    dve.tensor_tensor(y[:, d, :], y[:, d, :], MEAN[:], ALU.subtract).then_inc(centred, 1)
                dve.wait_ge(var_step, (n + 1) * DT)
                dve.tensor_scalar(rstd[:], VAR[:], eps, None, ALU.add).then_inc(var_eps, 1)
                dve.wait_ge(std_ready, n + 1)
                step.then(dve.reciprocal(rstd[:], rstd[:]))

                def low(d):
                    dve.wait_ge(x_hi_ready, (n + 1) * DT + d + 1)
                    b = par[:, (2 * n + 1) * DT + d:(2 * n + 1) * DT + d + 1]
                    dve.scalar_tensor_tensor(x_lo[:, d, :], y[:, d, :], b, x_hi[:, d, :].bitcast(F32),
                                             ALU.add, ALU.subtract).then_inc(x_ready, 1)

                for d in range(DT):
                    g = par[:, 2 * n * DT + d:2 * n * DT + d + 1]
                    dve.scalar_tensor_tensor(y[:, d, :], y[:, d, :], g, rstd[:], ALU.mult, ALU.mult
                                             ).then_inc(scaled, 1)
                    if d >= 1 and not last:
                        low(d - 1)
                if not last:
                    low(DT - 1)

            dve.wait_ge(filt_loaded, 64)
            for n in range(2):
                dve.wait_ge(hid_mm, n + 1)
                step.then(dve.tensor_scalar(arg[:], ps[7][0:HID, :], f_cols[:, n:n + 1], f_cols[:, 2:3],
                                            ALU.add, ALU.mult))
                step.then(dve.tensor_scalar(turns[:], arg[:], float(1 / (2 * np.pi)), MAGIC, ALU.mult, ALU.add))
                step.then(dve.tensor_scalar(turns[:], turns[:], MAGIC, None, ALU.subtract))
                for part in TWO_PI_PARTS:
                    step.then(dve.scalar_tensor_tensor(arg[:], turns[:], -part, arg[:], ALU.mult, ALU.add))
                pi = 3.1415925
                dve.tensor_scalar(arg[:], arg[:], pi, -pi, ALU.min, ALU.max).then_inc(arg_ready, 1)
            for d in range(DT):
                dve.wait_ge(x_hi_ready, d + 1)
                dve.tensor_tensor(x_lo[:, d, :], y[:, d, :], x_hi[:, d, :].bitcast(F32), ALU.subtract
                                  ).then_inc(x_ready, 1)
            ffn_up(0)
            residual(0, 2 * ALPHA, "ffn1", UP_UNITS, 4)
            layer_norm(0, 4 * LN_EPS, False)

            def short_conv(n):
                part, c = n // CT, n % CT
                dst = parts[part][:, c, :].rearrange("p (two s) -> p s two", two=2)
                dve.wait_ge(pad_ready, 2 * n + 2)
                for tap in (0, 2):
                    col = C_SW + tap * 3 * CT + n
                    src = u_pad[:, tap:tap + SEQ].rearrange("p (s two) -> p s two", two=2)
                    last = dve.scalar_tensor_tensor(dst, src, par[:, col:col + 1], dst, ALU.mult, ALU.add)
                    if tap == 0:
                        step.then(last)
                last.then_inc(conv_ready, 1)

            def tap_tile(n):
                o, t = n // TT, n % TT
                dve.wait_ge(filt_mm, n + 1)
                b0 = 2 + 2 * (n % 2)
                if n >= 1:
                    dve.wait_ge(taps_hi_ready, 2 * n)
                step.then(dve.tensor_tensor(tap_f[:], decay_sb[:, t, :], ps[b0][:], ALU.mult))
                dve.tensor_tensor(tap_b[:], decay_sb[:, t, :], ps[b0 + 1][:], ALU.mult).then_inc(filt_freed, 1)
                dve.wait_ge(filt_freed, n + 1)
                if t == 0:
                    step.then(dve.memset(tap_b[0:1, :], 0.0))
                dve.tensor_tensor(tap_pm[:, 0, :], tap_f[:], tap_b[:], ALU.add)
                dve.tensor_tensor(tap_pm[:, 1, :], tap_f[:], tap_b[:], ALU.subtract).then_inc(taps_made, 1)
                dve.wait_ge(taps_hi_ready, 2 * n + 2)
                dve.tensor_tensor(taps_lo[:, :, t, :], tap_pm[:], taps_hi[:, :, t, :].bitcast(F32),
                                  ALU.subtract).then_inc(taps_ready, 1)
                if t == 0:
                    if o == 1:
                        dve.wait_ge(spec_half, 4)
                    step.then(dve.tensor_tensor(energy[:], tap_sq[:, 0, :], tap_sq[:, 1, :], ALU.add))
                else:
                    step.then(dve.tensor_tensor(energy[:], energy[:], tap_sq[:, 0, :], ALU.add))
                    last = dve.tensor_tensor(energy[:], energy[:], tap_sq[:, 1, :], ALU.add)
                    if t == TT - 1:
                        last.then_inc(energy_ready, 1)
                    else:
                        step.then(last)

            def kernel_norm(o):
                dve.wait_ge(energy_mm, o + 1)
                dve.tensor_scalar(kernel_scale[:, o, :], ps[7][:, 0:CT], float(D_MODEL / 2 * SEQ ** 2),
                                  1e-12 * SEQ ** 2, ALU.mult, ALU.add).then_inc(energy_eps, 1)
                dve.wait_ge(energy_std, o + 1)
                step.then(dve.reciprocal(kernel_scale[:, o, :], kernel_scale[:, o, :]))

            def spec_evac(v0, dst):
                for v in range(v0, v0 + 4):
                    kt, rs = (v - v0) // 2, v % 2
                    dve.wait_ge(spec_half, v + 1)
                    odd = ps[3 + 2 * rs][:]
                    dve.tensor_tensor(dst[:, kt, rs, 0, :], half_spec[:], odd, ALU.add)
                    if rs == 0:
                        last = dve.tensor_tensor(dst[:, kt, rs, 1, :], half_spec[:], odd, ALU.subtract)
                    else:
                        last = dve.tensor_tensor(dst[:, kt, rs, 1, :], odd, half_spec[:], ALU.subtract)
                    last.then_inc(spec_freed, 1)

            def product(o, kt):
                zr, zs = spec_z[:, kt, 0], spec_z[:, kt, 1]
                kr, ks = spec_k[o][:, kt, 0], spec_k[o][:, kt, 1]
                if kt == 0:
                    dve.wait_ge(spec_freed, 12 + 4 * o)
                dve.tensor_tensor(prod[0][:], zr, kr, ALU.mult)
                dve.tensor_tensor(prod[1][:], zs, ks, ALU.mult)
                step.then(dve.tensor_tensor(prod[2][:], zr, ks, ALU.mult))
                step.then(dve.tensor_tensor(zs, zs, kr, ALU.mult))
                dve.tensor_tensor(prod[0][:], prod[0][:], prod[1][:], ALU.subtract)
                step.then(dve.tensor_tensor(prod[2][:], prod[2][:], zs, ALU.add))
                for rs, src in ((0, prod[0]), (1, prod[2])):
                    for odd in range(2):
                        op = ALU.add if odd == rs else ALU.subtract
                        last = dve.tensor_tensor(spec_z[:, kt, rs, odd, :], src[:, 0, :], src[:, 1, :], op)
                last.then_inc(spec_made, 1)

            def product_lo(o, kt):
                dve.wait_ge(spec_hi_ready, 2 * o + kt + 1)
                dve.tensor_tensor(zy_lo[:], spec_z[:, kt].rearrange("p a b c -> p (a b) c"),
                                  zy_hi[:].bitcast(F32), ALU.subtract).then_inc(spec_ready, 1)

            def gate(o, c):
                z = parts[o][:, c, :]
                col = C_HB + o * CT + c
                step.then(dve.tensor_scalar(z, z, par[:, col:col + 1], None, ALU.mult))
                dve.wait_ge(inv_ready, o * CT + c + 1)
                step.then(dve.scalar_tensor_tensor(z, ps[2 + c][:], kernel_scale[:, o, c:c + 1], z,
                                                   ALU.mult, ALU.add))
                if o == 0:
                    dve.tensor_tensor(z1[:, c, :], z, z1[:, c, :], ALU.mult).then_inc(gated, 1)
                else:
                    last = dve.tensor_tensor(z0[:, c, :].rearrange("p (s two) -> p two s", two=2),
                                             z.rearrange("p (two s) -> p two s", two=2),
                                             part2[:, c, :].rearrange("p (two s) -> p two s", two=2), ALU.mult)
                    last.then_inc(gated, 1)

            for n in range(TT):
                short_conv(n)
                tap_tile(n)
            short_conv(TT)
            kernel_norm(0)
            spec_evac(0, spec_k[0])
            tap_tile(TT)
            for n in range(TT + 1, 2 * TT):
                short_conv(n)
                tap_tile(n)
            kernel_norm(1)
            spec_evac(4, spec_k[1])
            for o in range(HY_ORDER):
                for t in range(TT):
                    dve.wait_ge(z_hi_ready, o * TT + t + 1)
                    dve.tensor_tensor(zy_lo[:, t, :], ps[6 + t % 2][:], zy_hi[:, t, :].bitcast(F32),
                                      ALU.subtract).then_inc(z_ready, 1)
                spec_evac(8 + 4 * o, spec_z)
                product(o, 0)
                if o == 0:
                    short_conv(2 * CT)
                    short_conv(2 * CT + 1)
                product_lo(o, 0)
                product(o, 1)
                if o == 0:
                    short_conv(2 * CT + 2)
                    short_conv(2 * CT + 3)
                product_lo(o, 1)
                for c in range(CT):
                    gate(o, c)
            for c in range(CT):
                dve.wait_ge(yb_hi_ready, c + 1)
                dve.tensor_tensor(yb_lo[:, c, :], z0[:, c, :], yb_hi[:, c, :].bitcast(F32), ALU.subtract
                                  ).then_inc(yb_ready, 1)

            by_block = lambda t, c: t[:, c, :].rearrange("p (r b w) -> p b r w", b=BLOCKS, w=KW)

            def softmax_front(h):
                dve.wait_ge(bias_ready, h + 1)
                if h >= 3:
                    dve.wait_ge(pt_mm, 2 * (h - 2))
                for j in range(2):
                    dve.wait_ge(score_mm, 2 * h + j + 1)
                    dve.scalar_tensor_tensor(probs[:, h % 3, 2 * j:2 * j + 2, :].rearrange("p a k -> p (a k)"),
                                             ps[2 * (h % 2) + j][:], HEAD_DIM ** -0.5,
                                             bias_sb[:, h % 2, j:j + 2, :].rearrange("p a k -> p (a k)"),
                                             ALU.mult, ALU.add).then_inc(scored, 1)
                dve.wait_ge(scored, 2 * h + 2)
                dve.tensor_reduce(neg_max[:, h, :], probs[:, h % 3], AX.X, ALU.max, negate=True
                                  ).then_inc(max_ready, 1)

            def softmax_back(h):
                dve.wait_ge(exp_ready, BLOCKS * (h + 1))
                step.then(dve.reciprocal(row_inv[:, h, :], row_sum[:, h, :]))
                for b in range(BLOCKS):
                    last = dve.tensor_scalar(probs[:, h % 3, b, :], probs[:, h % 3, b, :],
                                             row_inv[:, h, b:b + 1], None, ALU.mult)
                    if b % 2:
                        last.then_inc(prob_ready, 1)

            def ya_low(c):
                dve.wait_ge(ya_hi_ready, c + 1)
                dve.tensor_tensor(by_block(ya_lo, c), ps[6 + c % 2][:].rearrange(
                    "p (b r w) -> p b r w", b=BLOCKS, w=KW), by_block(ya_hi, c).bitcast(F32),
                    ALU.subtract).then_inc(ya_ready, 1)

            softmax_front(0)
            softmax_front(1)
            for h in range(HEADS):
                softmax_back(h)
                if h % 2 == 0 and h >= 2:
                    ya_low(h // 2 - 1)
                if h + 2 < HEADS:
                    softmax_front(h + 2)
            ya_low(CT - 1)

            for d in range(DT):
                s, b0 = d % 2, 4 * (d % 2)
                dve.wait_ge(gates_ready, d + 1)
                dve.tensor_tensor(gate_a[:, s, :], gate_a[:, s, :], ps[b0 + 2][:], ALU.mult)
                step.then(dve.tensor_tensor(gate_b[:, s, :], gate_b[:, s, :], ps[b0 + 3][:], ALU.mult))
                dve.tensor_tensor(gate_a[:, s, :], gate_a[:, s, :], gate_b[:, s, :], ALU.add).then_inc(m_made, 1)
                dve.wait_ge(m_hi_ready, d + 1)
                dve.tensor_tensor(m_lo[:, d, :], gate_a[:, s, :], m_hi[:, d, :].bitcast(F32), ALU.subtract
                                  ).then_inc(m_ready, 1)
            residual(RESIDUAL_TILES, ALPHA, "mix", U_OUT, 1)
            layer_norm(1, LN_EPS, False)
            ffn_up(1)
            residual(2 * RESIDUAL_TILES, 2 * ALPHA, "ffn2", UP_UNITS, 4)
            layer_norm(2, 4 * LN_EPS, True)


def _dft_tables():
    k = np.arange(HALF)[None, :]
    s = np.arange(HALF)[:, None]
    def angle(t):
        return np.pi * (((2 * k + 1) * t) % (4 * SEQ)) / (2 * SEQ)
    ce, se = np.cos(angle(2 * s)), np.sin(angle(2 * s))
    co, so = np.cos(angle(2 * s + 1)), np.sin(angle(2 * s + 1))
    tables = np.stack([ce, co, se, so, ce.T, se.T]).astype(np.float32)
    return np.ascontiguousarray(tables.reshape(6, 2, P, HALF).transpose(2, 0, 1, 3))


def _split_tokens():
    return np.concatenate([np.arange(0, SEQ, 2), np.arange(1, SEQ, 2)])


def _filter_features():
    t = np.linspace(0.0, 1.0, SEQ, dtype=np.float32)[:, None]
    bands = (EMB - 1) // 2
    w = (np.float32(2.0 * np.pi / SEQ) * np.arange(SEQ, dtype=np.float32))[:, None]
    f = np.linspace(1e-4, bands - 1, bands, dtype=np.float32)[None, :]
    z = np.concatenate([t, np.cos(f * w), -np.sin(f * w)], axis=-1).astype(np.float32)
    return np.ascontiguousarray(z[_split_tokens()].T)


def _decay():
    t = np.linspace(0.0, 1.0, SEQ, dtype=np.float32)[:, None]
    lo, hi = np.log(1e-2) / 1.5, np.log(1e-2) / 0.3
    deltas = np.abs(np.linspace(lo, hi, HY_WIDTH, dtype=np.float32))
    d = np.exp(-t * deltas).astype(np.float32)[_split_tokens()]
    return np.ascontiguousarray(d.reshape(TT, P, HY_WIDTH).transpose(1, 0, 2))


def _window_mask():
    cq = np.arange(P) % KW
    out = []
    for b, first, second in ((0, (0, 56), (8, 16)), (1, (8, 16), (24, 32)), (3, (40, 48), (0, 56))):
        start = np.clip(KW * b + cq - KW // 2, 0, GRID_W - KW)[:, None, None]
        for halves in (first, second):
            cols = np.concatenate([c0 + np.arange(8) for c0 in halves])
            if halves == (0, 56):
                cols = np.stack([np.broadcast_to(cols[i:i + 8], (ROWS, 8)) for i in (0, 8)])[None]
                cols = cols.reshape(1, 2 * ROWS, 8)
            else:
                cols = np.broadcast_to(cols, (1, ROWS, KW))
            ok = (cols >= start) & (cols < start + KW)
            out.append(np.where(ok, 0.0, MASKED).reshape(P, 1, P))
    return np.ascontiguousarray(np.concatenate(out, axis=1).reshape(P, 3, KEYS).astype(np.float32))


def _col_tiles(w, first, n):
    kt = w.shape[0] // P
    t = w[:, first:first + n * P].reshape(kt, P, n, P)
    return np.ascontiguousarray(t.transpose(2, 1, 0, 3)).reshape(n, P, kt * P)


def _up_units(w1, w3):
    return np.ascontiguousarray(np.stack([_col_tiles(w1, 0, FT), _col_tiles(w3, 0, FT)], axis=1)
                                ).reshape(UP_UNITS, P, UP_W)


def _down_units(w2):
    t = w2.reshape(2, DOWN_K, P, DT, P).transpose(3, 0, 2, 1, 4)
    return np.ascontiguousarray(t).reshape(DOWN_UNITS, P, DOWN_W)


def _mixer_units(w_in, w_pa, w_pb, w_out):
    a_w, h_w = 3 * HEADS * HEAD_DIM, 3 * HY_WIDTH
    ga, gb = _col_tiles(w_in, a_w + h_w, DT), _col_tiles(w_in, a_w + h_w + D_MODEL, DT)
    pab = np.concatenate([_col_tiles(w_pa, 0, DT), _col_tiles(w_pb, 0, DT)], axis=2)
    gates = np.stack([ga, gb, pab], axis=1).reshape(3 * DT, P, UP_W)
    return np.ascontiguousarray(np.concatenate([
        _col_tiles(w_in, a_w, 3 * CT), _col_tiles(w_in, 0, CT), _col_tiles(w_in, 512, CT),
        _col_tiles(w_in, 1024, CT), gates,
        _col_tiles(w_out, 0, DT)], axis=0))


def _bias_segments(rpb):
    flat = np.pad(rpb.reshape(HEADS, -1), ((0, 0), (8, 8)))
    out = np.empty((P, HEADS, SEG), np.float32)
    for rq in range(ROWS):
        for cq in range(KW):
            a = 8 + (KH - 1 - rq) * (2 * KW - 1) + (7 - cq)
            out[rq * KW + cq] = flat[:, a:a + SEG]
    return out


def _columns(v):
    return np.asarray(v).reshape(-1, P).T


def kernel(**inputs):
    import concourse.bacc as bacc
    from concourse.bass_utils import run_bass_kernel_spmd

    a = {k: np.asarray(v)[0] for k, v in inputs.items()}
    xT = np.ascontiguousarray(a["x"].T.reshape(DT, P, SEQ).transpose(1, 0, 2))
    arrays = {
        "in_xT": xT,
        "in_params": np.ascontiguousarray(np.concatenate(
            [_columns(a[n]) for n in ("ln1_g", "ln1_b", "ln2_g", "ln2_b", "ln3_g", "ln3_b", "b_gate",
                                      "hy_short_w", "hy_short_b", "hy_bias")], axis=1)),
        "in_up1": _up_units(a["ffn1_w1"], a["ffn1_w3"]),
        "in_down1": _down_units(a["ffn1_w2"]),
        "in_mix": _mixer_units(a["w_in"], a["w_pa"], a["w_pb"], a["w_out"]),
        "in_up2": _up_units(a["ffn2_w1"], a["ffn2_w3"]),
        "in_down2": _down_units(a["ffn2_w2"]),
        "in_eye": np.eye(P, dtype=np.float32),
        "in_dft": _dft_tables(),
        "in_feat": _filter_features(),
        "in_filt1": np.ascontiguousarray(a["hy_filt_w1"]),
        "in_filt2": np.ascontiguousarray(a["hy_filt_w2"]),
        "in_filt_cols": np.ascontiguousarray(np.stack([a["hy_filt_b1"], a["hy_filt_b2"], a["hy_filt_freq"]], 1)),
        "in_filt3": np.concatenate([a["hy_filt_w3"], a["hy_filt_b3"][None]], axis=0),
        "in_decay": _decay(),
        "in_seg": _bias_segments(a["na_rpb"]),
        "in_mask": _window_mask(),
    }
    nc = bacc.Bacc("TRN2", target_bir_lowering=False, num_devices=1)
    args = [nc.dram_tensor(n, v.shape, mybir.dt.from_np(v.dtype), kind="ExternalInput").ap()
            for n, v in arrays.items()]
    args.append(nc.dram_tensor("out_yT", (P, DT, SEQ), F32, kind="ExternalOutput").ap())
    build(nc, *args)
    got = run_bass_kernel_spmd(nc, [arrays], core_ids=[0]).results[0]["out_yT"]
    return np.ascontiguousarray(np.asarray(got).transpose(1, 0, 2).reshape(D_MODEL, SEQ).T)[None]
```

```python
from contextlib import ExitStack

import numpy as np

import concourse.bass as bass
from concourse import mybir

F32 = mybir.dt.float32
F32R = mybir.dt.float32r
ALU = mybir.AluOpType
ACT = mybir.ActivationFunctionType
AX = mybir.AxisListType

P = 128
D_MODEL, SEQ, D_FF = 1024, 512, 2816
GRID_W, KW, KH = 64, 16, 8
ROWS = SEQ // GRID_W
HEADS, HEAD_DIM = 8, 64
HY_WIDTH, HY_ORDER, EMB, HID = 512, 2, 33, 64
DEPTH = 1
ALPHA = (2 * DEPTH) ** 0.25
LN_EPS = 1e-5

DT = D_MODEL // P
FT = D_FF // P
CT = HY_WIDTH // P
TT = SEQ // P
HALF = SEQ // 2

UP_W = DT * P
DOWN_K = FT // 2
DOWN_W = DOWN_K * P
SLOTS = 4
UP_UNITS, DOWN_UNITS = 2 * FT, 2 * DT
FFN_UNITS = UP_UNITS + DOWN_UNITS
FFN_SLOTS = UP_UNITS + 2 * DOWN_UNITS
U_HYENA, U_Q, U_K, U_V, U_MIX, U_OUT = 0, 3 * CT, 4 * CT, 5 * CT, 6 * CT, 6 * CT + 3 * DT
MIX_UNITS = U_OUT + DT
RESIDUAL_TILES = DT

C_LN = 0
C_GATE = C_LN + 6 * DT
C_SW = C_GATE + 2 * DT
C_SB = C_SW + 9 * CT
C_HB = C_SB + 3 * CT
N_PARAM = C_HB + HY_ORDER * CT

SEG = (KH - 1) * (2 * KW - 1) + 2 * KW
BLOCKS = GRID_W // KW
KEYS = 2 * P
MASKED = -1e30

MAGIC = 1.5 * 2 ** 23
TWO_PI_PARTS = (6.28125, 0.0019350051879882812, 3.019916050561733e-07)


class Steps:

    def __init__(self, eng, sem):
        self.eng, self.sem, self.n = eng, sem, 0

    def then(self, ins):
        ins.then_inc(self.sem, 1)
        self.n += 1
        self.eng.wait_ge(self.sem, self.n)


def build(nc, xT, params, up1, down1, mix_units, up2, down2, ident, dft, feat, filt1, filt2, filt_cols,
          filt3, decay, rpb_seg, na_mask, out):
    with ExitStack() as ctx:
        base = (nc.sbuf_base + 63) // 64 * 64
        KB = 1024

        def at(name, shape, dt, offset):
            return nc.alloc_sbuf_tensor_at(name, shape, dt, offset=base + offset)

        def sem(name):
            return ctx.enter_context(nc.semaphore(name))

        x_hi = at("x_hi", [P, DT, SEQ], F32R, 0)
        x_lo = at("x_lo", [P, DT, SEQ], F32R, 16 * KB)
        ring_hi = at("ring_hi", [P, SLOTS * UP_W], F32R, 32 * KB)
        ring_lo = at("ring_lo", [P, SLOTS * UP_W], F32R, 48 * KB)
        raw = at("raw", [P, 2, DOWN_W], F32, 64 * KB)
        fixed = 64 * KB + 2 * DOWN_W * 4
        par = at("par", [P, N_PARAM], F32, fixed)
        mean_of = at("mean_of", [P, P], F32, fixed + 512)
        eye = at("eye", [P, P], F32, fixed + 1024)
        u_pad = at("u_pad", [P, SEQ + 2], F32, fixed + 1536)
        kernel_scale = at("kernel_scale", [P, HY_ORDER, CT], F32, fixed + 1536 + 2112)
        w_f1 = at("w_f1", [EMB, HID], F32, fixed + 3712)
        w_f2 = at("w_f2", [HID, HID], F32, fixed + 3712 + 256)
        f_cols = at("f_cols", [HID, 3], F32, fixed + 3712 + 512)
        one = at("one", [P, 1], F32, fixed + 3712 + 544)
        mean_col = at("mean_col", [P, TT], F32, fixed + 3712 + 576)
        deviation = at("deviation", [P, TT], F32, fixed + 3712 + 608)
        mean_sq = at("mean_sq", [P, TT], F32, fixed + 3712 + 640)
        R = fixed + 3712 + 704
        y = at("y", [P, DT, SEQ], F32, R)
        act_gate = [y[:, p, :] for p in range(2)]
        h_prod = [y[:, 2 + p, :] for p in range(2)]
        h_hi = at("h_hi", [P, FT, SEQ], F32R, R + 16 * KB)
        h_lo = at("h_lo", [P, FT, SEQ], F32R, R + 60 * KB)
        squares = at("squares", [P, 2, SEQ], F32, R + 104 * KB)
        rstd_diag = at("rstd_diag", [P, TT, P], F32, R + 108 * KB)
        y_sum = at("y_sum", [P, SEQ], F32, R + 110 * KB)
        shift = at("shift", [P, SEQ], F32, R + 112 * KB)
        square_sum = at("square_sum", [P, SEQ], F32, R + 114 * KB)
        mean_left = shift
        mean_diag = at("mean_diag", [P, TT, P], F32, R + 116 * KB)
        feat_sb = at("feat_sb", [EMB, SEQ], F32, R + 118 * KB)
        hid1 = at("hid1", [HID, SEQ], F32, R + 120 * KB)
        arg = at("arg", [HID, SEQ], F32, R + 122 * KB)
        hid = at("hid", [HID + 1, SEQ], F32, R + 124 * KB)
        turns = at("turns", [HID, SEQ], F32, R + 126 * KB)
        z0 = at("z0", [P, CT, SEQ], F32, R)
        z1 = at("z1", [P, CT, SEQ], F32, R + 8 * KB)
        part2 = at("part2", [P, CT, SEQ], F32, R + 16 * KB)
        parts = [z0, z1, part2]
        w_f3 = at("w_f3", [HID + 1, 2 * HY_ORDER * HY_WIDTH], F32, R + 16 * KB)
        dft_hi = at("dft_hi", [P, 6, 2, HALF], F32R, R + 24 * KB)
        dft_lo = at("dft_lo", [P, 6, 2, HALF], F32R, R + 36 * KB)
        spec_k = [at(f"spec_k{o}", [P, 2, 2, 2, HY_WIDTH], F32, R + (48 + 16 * o) * KB) for o in range(2)]
        decay_sb = at("decay_sb", [P, TT, HY_WIDTH], F32, R + 64 * KB)
        taps_hi = at("taps_hi", [P, 2, TT, HY_WIDTH], F32R, R + 80 * KB)
        taps_lo = at("taps_lo", [P, 2, TT, HY_WIDTH], F32R, R + 96 * KB)
        dft_raw = at("dft_raw", [P, 6, 2, HALF], F32, R + 48 * KB)
        zy_hi = at("zy_hi", [P, TT, HY_WIDTH], F32R, R + 80 * KB)
        zy_lo = at("zy_lo", [P, TT, HY_WIDTH], F32R, R + 88 * KB)
        spec_z = at("spec_z", [P, 2, 2, 2, HY_WIDTH], F32, R + 96 * KB)
        tap_pm = [at(f"tap_pm{n}", [P, 2, HY_WIDTH], F32, R + (112, 72)[n] * KB) for n in range(2)]
        tap_sq = [at(f"tap_sq{n}", [P, 2, HY_WIDTH], F32, R + (116, 76)[n] * KB) for n in range(2)]
        energy = at("energy", [P, HY_WIDTH], F32, R + 120 * KB)
        half_spec = at("half_spec", [P, HY_WIDTH], F32, R + 126 * KB + 64)
        u_pad1 = at("u_pad1", [P, SEQ + 2], F32, R + 124 * KB)
        prod = [at(f"prod{n}", [P, 2, HY_WIDTH], F32, R + (112 + 4 * n) * KB) for n in range(3)]
        yb = at("yb", [P, CT, SEQ], F32, R + 96 * KB)
        yb_hi = at("yb_hi", [P, CT, SEQ], F32R, R + 112 * KB)
        yb_lo = at("yb_lo", [P, CT, SEQ], F32R, R + 120 * KB)
        vT = at("vT", [P, CT, SEQ], F32, R)
        qT = at("qT", [P, CT, SEQ], F32, R + 48 * KB)
        kT = at("kT", [P, CT, SEQ], F32, R + 56 * KB)
        seg_sb = at("seg_sb", [P, HEADS, SEG], F32, R + 64 * KB)
        mask_sb = at("mask_sb", [P, 3, KEYS], F32, R + 72 * KB)
        bias_sb = at("bias_sb", [P, 2, 3, KEYS], F32, R + 16 * KB)
        v_sb = at("v_sb", [P, 4, HEADS * HEAD_DIM], F32, R + 80 * KB)
        ya_hi = at("ya_hi", [P, CT, SEQ], F32R, R + 24 * KB)
        ya_lo = at("ya_lo", [P, CT, SEQ], F32R, R + 32 * KB)
        probs = at("probs", [P, 3, BLOCKS, KEYS], F32, R + 96 * KB)
        probsT = at("probsT", [P, 2, 2 * KEYS], F32, R + 108 * KB)
        neg_max = at("neg_max", [P, HEADS, BLOCKS], F32, R + 75 * KB)
        row_sum = at("row_sum", [P, HEADS, BLOCKS], F32, R + 75 * KB + 128)
        row_inv = at("row_inv", [P, HEADS, BLOCKS], F32, R + 75 * KB + 256)
        m_hi = at("m_hi", [P, DT, SEQ], F32R, R + 48 * KB)
        m_lo = at("m_lo", [P, DT, SEQ], F32R, R + 64 * KB)
        gate_a = at("gate_a", [P, 2, SEQ], F32, R + 96 * KB)
        gate_b = at("gate_b", [P, 2, SEQ], F32, R + 100 * KB)

        ps = [ctx.enter_context(nc.psum_tensor(f"ps{n}", [P, SEQ], F32)) for n in range(8)]
        MEAN, RSTD = ps[6], ps[7]
        MEAN_COL, SQUARE_COL = ps[3], ps[2]

        raw_loaded = [sem("raw_loaded0"), sem("raw_loaded1")]
        x_loaded = [sem(f"x_loaded{n}") for n in range(4)]
        small_loaded, filt_loaded = sem("small_loaded"), sem("filt_loaded")
        mixer_loaded, na_loaded, stored = sem("mixer_loaded"), sem("na_loaded"), sem("stored")
        unit_hi, unit_lo, ring_freed = sem("unit_hi"), sem("unit_lo"), sem("ring_freed")
        mean_set = sem("mean_set")
        x_hi_ready, x_ready = sem("x_hi_ready"), sem("x_ready")
        up_freed, gate_ready = sem("up_freed"), sem("gate_ready")
        h_hi_ready, h_ready = sem("h_hi_ready"), sem("h_ready")
        res_freed = sem("res_freed")
        y_summed, shift_mm, shifted, c_summed = sem("y_summed"), sem("shift_mm"), sem("shifted"), sem("c_summed")
        squared, square_added, mean_col_ready, square_col_ready = (
            sem("squared"), sem("square_added"), sem("mean_col_ready"), sem("square_col_ready"))
        centred = sem("centred")
        mean_diag_ready, mean_mm, mean_copied = sem("mean_diag_ready"), sem("mean_mm"), sem("mean_copied")
        var_eps, std_ready = sem("var_eps"), sem("std_ready")
        rstd_diag_ready, rstd_mm = sem("rstd_diag_ready"), sem("rstd_mm")
        scaled, final_ready = sem("scaled"), sem("final_ready")
        dve_step = sem("dve_step")
        hid_mm, arg_ready, hid_ready, ones_row = sem("hid_mm"), sem("arg_ready"), sem("hid_ready"), sem("ones_row")
        dft_hi_ready, dft_ready = sem("dft_hi_ready"), sem("dft_ready")
        proj_freed, pad_ready, conv_ready = sem("proj_freed"), sem("pad_ready"), sem("conv_ready")
        w_f3_ready, filt_mm, taps_made, taps_hi_ready, taps_ready = (
            sem("w_f3_ready"), sem("filt_mm"), sem("taps_made"), sem("taps_hi_ready"), sem("taps_ready"))
        energy_ready, energy_mm, energy_eps, energy_std = (
            sem("energy_ready"), sem("energy_mm"), sem("energy_eps"), sem("energy_std"))
        spec_mm, spec_half, spec_freed = sem("spec_mm"), sem("spec_half"), sem("spec_freed")
        zt_ready, z_hi_ready, z_ready = sem("zt_ready"), sem("z_hi_ready"), sem("z_ready")
        sin_products, spec_made, spec_hi_ready, spec_ready = (
            sem("sin_products"), sem("spec_made"), sem("spec_hi_ready"), sem("spec_ready"))
        inv_mm, inv_ready, gated = sem("inv_mm"), sem("inv_ready"), sem("gated")
        yb_hi_ready, yb_ready = sem("yb_hi_ready"), sem("yb_ready")
        qk_ready, vt_ready, v_mm, v_ready = sem("qk_ready"), sem("vt_ready"), sem("v_mm"), sem("v_ready")
        bias_ready, score_mm, scored, max_ready, exp_ready, prob_ready = (
            sem("bias_ready"), sem("score_mm"), sem("scored"), sem("max_ready"), sem("exp_ready"),
            sem("prob_ready"))
        pt_mm, pt_ready, pv_mm, ya_hi_ready, ya_ready = (
            sem("pt_mm"), sem("pt_ready"), sem("pv_mm"), sem("ya_hi_ready"), sem("ya_ready"))
        gates_ready, m_made, m_hi_ready, m_ready = (
            sem("gates_ready"), sem("m_made"), sem("m_hi_ready"), sem("m_ready"))

        SHIFT_TILES = 4
        SHIFT_AFTER = (5, 5, 5)
        DVE_CENTRES = (2, 2, 3)

        UNIT0 = {"ffn1": 0, "mix": FFN_UNITS, "ffn2": FFN_UNITS + MIX_UNITS}
        SLOT0 = {"ffn1": 0, "mix": FFN_SLOTS, "ffn2": FFN_SLOTS + MIX_UNITS}

        def pad_of(n):
            return u_pad1 if n >= 8 and n % 2 == 0 else u_pad

        AHEAD = 3

        V_BANK = (0, 6, 7, 1)

        def used(phase, slots):
            return SLOTS + SLOT0[phase] + slots

        FILL = (((8,), (9,), (10, 11), (12, 13), (14,)),
                ((15,), (16,), (17, 18), (19, 20), (21,)))
        assert [n for o in FILL for part in o for n in part] == list(range(2 * CT, 6 * CT - 2))

        block = ctx.enter_context(nc.Block())

        @block.sync
        def _(sp):
            for q in range(4):
                if q < 2:
                    sp.dma_start(raw[:, q, 0:UP_W], up1[q]).then_inc(raw_loaded[q], 16)
                sp.dma_start(y[:, 2 * q:2 * q + 2, :], xT[:, 2 * q:2 * q + 2, :]).then_inc(x_loaded[q], 16)
            sp.dma_start(par[:], params).then_inc(small_loaded, 16)
            sp.dma_start(eye[:], ident).then_inc(small_loaded, 16)
            sp.dma_start(feat_sb[:], feat).then_inc(filt_loaded, 16)
            sp.dma_start(w_f1[:], filt1).then_inc(filt_loaded, 16)
            sp.dma_start(w_f2[:], filt2).then_inc(filt_loaded, 16)
            sp.dma_start(f_cols[:], filt_cols).then_inc(filt_loaded, 16)

            def units(src, width, n, first):
                with sp.Fori(0, n // 2) as i:
                    for s in range(2):
                        sp.wait_ge(unit_lo, i * 2 + (first + s - 1))
                        sp.dma_start(raw[:, s, 0:width], src[i * 2 + s]).then_inc(raw_loaded[s], 16)

            def ffn(up, down, u0):
                skip = 2 if u0 == 0 else 0
                units(up[skip:], UP_W, UP_UNITS - skip, u0 + skip)
                units(down, DOWN_W, DOWN_UNITS, u0 + UP_UNITS)

            ffn(up1, down1, 0)
            u0 = UNIT0["mix"]
            units(mix_units[0:4], UP_W, 4, u0)
            sp.wait_ge(ring_freed, used("ffn1", FFN_SLOTS))
            sp.dma_start(dft_raw[:], dft).then_inc(mixer_loaded, 16)
            sp.dma_start(w_f3[:], filt3).then_inc(mixer_loaded, 16)
            sp.dma_start(decay_sb[:], decay).then_inc(mixer_loaded, 16)
            units(mix_units[4:U_MIX], UP_W, U_MIX - 4, u0 + 4)
            sp.wait_ge(spec_made, 8)
            sp.dma_start(seg_sb[:], rpb_seg).then_inc(na_loaded, 16)
            sp.dma_start(mask_sb[:], na_mask).then_inc(na_loaded, 16)
            units(mix_units[U_MIX:], UP_W, MIX_UNITS - U_MIX, u0 + U_MIX)
            ffn(up2, down2, UNIT0["ffn2"])
            for d in range(DT):
                sp.wait_ge(final_ready, d + 1)
                sp.dma_start(out[:, d, :], y[:, d, :]).then_inc(stored, 16)
            sp.wait_ge(stored, 16 * DT)

        @block.gpsimd
        def _(pool):
            pool.sem_inc(ring_freed, SLOTS)

            def split(slot, width, raw_slot, unit):
                hi = ring_hi[:, slot * UP_W:slot * UP_W + width]
                lo = ring_lo[:, slot * UP_W:slot * UP_W + width]
                pool.wait_ge(unit_hi, unit + 1)
                pool.tensor_tensor(lo, raw[:, raw_slot, 0:width], hi.bitcast(F32), ALU.subtract
                                   ).then_inc(unit_lo, 1)

            def square_adds(n, tiles):
                for d in tiles:
                    pool.wait_ge(squared, n * DT + d + 1)
                    other = squares[:, 0, :] if d == 1 else square_sum[:]
                    if d > 1:
                        pool.wait_ge(square_added, n * (DT - 2) + d - 1)
                    pool.tensor_tensor(square_sum[:], other, squares[:, d % 2, :], ALU.add
                                       ).then_inc(square_added, 1)

            def centre(n):
                pool.wait_ge(mean_copied, n + 1)
                pool.wait_ge(squared, (n + 1) * DT)
                for d in range(DVE_CENTRES[n], DT):
                    pool.tensor_tensor(y[:, d, :], y[:, d, :], mean_left[:], ALU.subtract).then_inc(centred, 1)

            def up_units(n, unit0, first=0):
                with pool.Fori(first, n // SLOTS) as i:
                    for s in range(SLOTS):
                        split(s, UP_W, s % 2, i * SLOTS + (unit0 + s))

            def down_units(n, unit0):
                with pool.Fori(0, DOWN_UNITS // 2 - 1) as i:
                    for s in range(2):
                        split(2 * s, DOWN_W, s, i * 2 + (unit0 + s))
                S = SHIFT_AFTER[n]
                square_adds(n, range(1, S))
                split(0, DOWN_W, 0, unit0 + DOWN_UNITS - 2)
                square_adds(n, range(S, DT - 2))
                split(2, DOWN_W, 1, unit0 + DOWN_UNITS - 1)
                square_adds(n, (DT - 2,))

            pool.wait_ge(unit_lo, 2)
            split(2, UP_W, 0, 2)
            split(3, UP_W, 1, 3)
            up_units(UP_UNITS, 0, first=1)
            down_units(0, UP_UNITS)
            u0 = UNIT0["mix"]
            mix_lo_done = [0]

            def mix_lo(n):
                while mix_lo_done[0] <= n:
                    m = mix_lo_done[0]
                    split(m % SLOTS, UP_W, m % 2, u0 + m)
                    mix_lo_done[0] += 1

            def energy_tile(n):
                t, sq = n % TT, tap_sq[n % 2]
                pool.wait_ge(taps_hi_ready, 2 * n + 2)
                if t == 0 and n:
                    pool.wait_ge(energy_mm, 1)
                for way in range(2):
                    if t == 0 and way == 0:
                        continue
                    first = sq[:, 0, :] if t == 0 else energy[:]
                    if not (n == 0 and way == 1):
                        pool.wait_ge(energy_ready, 2 * n + way - 1 - (n // TT))
                    pool.tensor_tensor(energy[:], first, sq[:, way, :], ALU.add).then_inc(energy_ready, 1)

            def sin_terms(o, kt):
                zs = spec_z[:, kt, 1]
                if kt == 0:
                    pool.wait_ge(spec_freed, 12 + 4 * o)
                if o or kt:
                    pool.wait_ge(spec_made, 2 * (2 * o + kt))
                pool.tensor_tensor(prod[1][:], zs, spec_k[o][:, kt, 1], ALU.mult).then_inc(sin_products, 1)
                pool.tensor_tensor(zs, zs, spec_k[o][:, kt, 0], ALU.mult).then_inc(sin_products, 1)

            mix_lo(1)
            centre(0)
            mix_lo(3)
            pool.wait_ge(mixer_loaded, 48)
            pool.wait_ge(dft_hi_ready, 1)
            pool.tensor_tensor(dft_lo[:], dft_raw[:], dft_hi[:].bitcast(F32), ALU.subtract).then_inc(dft_ready, 1)
            for n, units in enumerate((1, 1, 2, 3, TT + 1, TT + 1, TT + 2, TT + 2)):
                mix_lo(AHEAD + units)
                energy_tile(n)
            mix_lo(AHEAD + FILL[0][1][0])
            for o in range(HY_ORDER):
                sin_terms(o, 0)
                mix_lo(AHEAD + FILL[o][2][0])
                sin_terms(o, 1)
                mix_lo(AHEAD + (FILL[1][1][0] if o == 0 else 6 * CT - 3))
            pool.wait_ge(na_loaded, 32)
            pool.wait_ge(gated, 2 * CT)
            for h in range(HEADS):
                if h == 3:
                    mix_lo(U_MIX + 3)
                if h >= 2:
                    pool.wait_ge(scored, 2 * (h - 1))
                pos = 0
                for c0, cols in ((8, 8), (8, 8), (16, 16), (0, 16), (16, 16), (0, 16), (16, 8), (16, 8)):
                    w = ROWS * cols
                    seg = bass.AP(seg_sb[:].tensor, seg_sb[:, h, c0:c0 + 1].offset,
                                  [list(seg_sb[:].ap[0]), [2 * KW - 1, ROWS], [1, cols]])
                    there = lambda t: t.rearrange("p a k -> p (a k)")[:, pos:pos + w].rearrange(
                        "p (r c) -> p r c", r=ROWS)
                    last = pool.tensor_tensor(there(bias_sb[:, h % 2]), seg, there(mask_sb[:]), ALU.add)
                    pos += w
                last.then_inc(bias_ready, 1)
            up_units(MIX_UNITS - U_MIX - 4, u0 + U_MIX + 4)
            square_adds(1, range(1, DT - 1))
            for n in range(SLOTS):
                if n == 2:
                    centre(1)
                split(n, UP_W, n % 2, UNIT0["ffn2"] + n)
            up_units(UP_UNITS, UNIT0["ffn2"], first=1)
            down_units(2, UNIT0["ffn2"] + UP_UNITS)
            centre(2)

        @block.tensor
        def _(pe):
            def mm3(out_ps, lhs_hi, lhs_lo, rhs_hi, rhs_lo, start, stop, **kw):
                pe.matmul(out_ps, lhs_hi, rhs_hi, start=start, stop=False, **kw)
                pe.matmul(out_ps, lhs_hi, rhs_lo, start=False, stop=False, **kw)
                return pe.matmul(out_ps, lhs_lo, rhs_hi, start=False, stop=stop, **kw)

            def tile_of(slot, k):
                a = slot * UP_W + k * P
                return ring_hi[:, a:a + P], ring_lo[:, a:a + P]

            def unit_times(slot, out_ps, mov_hi, mov_lo, tiles=DT, first=0, start=True, stop=True):
                for k in range(tiles):
                    w_hi, w_lo = tile_of(slot, k + first)
                    last = mm3(out_ps, w_hi, w_lo, mov_hi(k), mov_lo(k), start and k == 0,
                               stop and k == tiles - 1)
                return last

            x_tile = (lambda k: x_hi[:, k, :], lambda k: x_lo[:, k, :])

            def first_pair(unit0, x_count):
                for k0 in range(0, DT, 2):
                    for s in range(2):
                        if k0 == 0:
                            pe.wait_ge(unit_lo, unit0 + s + 1)
                        for k in (k0, k0 + 1):
                            if s == 0:
                                pe.wait_ge(x_ready, x_count + k + 1)
                            w_hi, w_lo = tile_of(s, k)
                            last = mm3(ps[s][:], w_hi, w_lo, x_hi[:, k, :], x_lo[:, k, :], k == 0, k == DT - 1)
                        if k == DT - 1:
                            last.then_inc(ring_freed, 1)

            def ffn_up(f, unit0, x_count):
                def turn(i, parts_of_turn):
                    for s in parts_of_turn:
                        if s % 2 == 0:
                            pe.wait_ge(up_freed, i * 2 + (f * FT + s // 2 + 1))
                        pe.wait_ge(unit_lo, i * SLOTS + (unit0 + s + 1))
                        unit_times(s, ps[s][:], *x_tile).then_inc(ring_freed, 1)

                pe.wait_ge(up_freed, f * FT + 1)
                first_pair(unit0, x_count)
                turn(0, (2, 3))
                with pe.Fori(1, FT // 2) as i:
                    turn(i, range(SLOTS))

            def ffn_down(f, r0, unit0):
                def out_tile(p, i=0):
                    pe.wait_ge(res_freed, i * 2 + (r0 + p + 1))
                    for half in range(2):
                        if p == DT - 1 and half:
                            early_sums(2 * f)
                        pe.wait_ge(unit_lo, i * 4 + (unit0 + 2 * p + half + 1))
                        for k in range(DOWN_K):
                            j = half * DOWN_K + k
                            if j == FT - 1:
                                pe.wait_ge(h_ready, (f + 1) * FT)
                            w_hi, w_lo = tile_of(2 * half, k)
                            last = mm3(ps[4 + p % 2][:], w_hi, w_lo, h_hi[:, j, :], h_lo[:, j, :],
                                       j == 0, j == FT - 1)
                        last.then_inc(ring_freed, 2)

                pe.wait_ge(h_ready, (f + 1) * FT - 1)
                with pe.Fori(0, DT // 4) as i:
                    for p in range(2):
                        out_tile(p, i)
                out_tile(DT // 2)
                shift_sum(2 * f)
                if f == 0:
                    pe.wait_ge(hid_ready, 1)
                    pe.matmul(ps[7][0:HID, :], w_f2[:], hid1[:], start=True, stop=True).then_inc(hid_mm, 1)
                for d in range(DT // 2 + 1, DT):
                    out_tile(d)

            def shift_sum(n):
                pe.wait_ge(y_summed, n + 1)
                pe.matmul(MEAN[:], mean_of[:], y_sum[:], start=True, stop=True).then_inc(shift_mm, 1)

            def sum_channels(bank, src, first, last):
                for j in range(TT):
                    mm = pe.matmul(bank[:, j:j + 1], src[:, j * P:(j + 1) * P], mean_of[:, 0:1],
                                   start=first and j == 0, stop=last and j == TT - 1, skip_group_check=True)
                return mm

            def early_sums(n):
                pe.wait_ge(c_summed, n + 1)
                sum_channels(MEAN_COL, y_sum, True, False)
                pe.wait_ge(square_added, (n + 1) * (DT - 2))
                sum_channels(SQUARE_COL, square_sum, True, False)

            def spread(n, bank, diag, diag_ready):
                for j in range(TT):
                    pe.wait_ge(diag_ready, n * TT + j + 1)
                    mm = pe.matmul(bank[:, j * P:(j + 1) * P], mean_of[:], diag[:, j, :], start=True, stop=True)
                return mm

            def layer_norm(n):
                pe.wait_ge(res_freed, 2 + (n + 1) * DT)
                sum_channels(MEAN_COL, y[:, DT - 1, :], False, True).then_inc(mean_col_ready, 1)
                pe.wait_ge(squared, (n + 1) * DT)
                sum_channels(SQUARE_COL, squares[:, 1, :], False, True).then_inc(square_col_ready, 1)
                spread(n, MEAN, mean_diag, mean_diag_ready).then_inc(mean_mm, 1)
                spread(n, RSTD, rstd_diag, rstd_diag_ready).then_inc(rstd_mm, 1)

            pe.wait_ge(mean_set, 3)
            ffn_up(0, 0, 0)
            pe.wait_ge(filt_loaded, 64)
            pe.matmul(ps[7][0:HID, :], w_f1[:], feat_sb[:], start=True, stop=True).then_inc(hid_mm, 1)
            ffn_down(0, 0, UP_UNITS)
            layer_norm(0)

            u0 = UNIT0["mix"]
            def project(n):
                pe.wait_ge(proj_freed, n + 1)
                pe.wait_ge(unit_lo, u0 + n + 1)
                unit_times(n % SLOTS, ps[n % 2][:], *x_tile).then_inc(ring_freed, 1)

            def filter_tile(n):
                o, t = n // TT, n % TT
                if n >= 2:
                    pe.wait_ge(taps_made, n - 1)
                if n == TT:
                    pe.wait_ge(spec_freed, 4)
                tokens = hid[:, t * P:(t + 1) * P]
                for way in range(2):
                    col = (way * HY_ORDER + o) * HY_WIDTH
                    last = pe.matmul(ps[2 + 2 * (n % 2) + way][:], tokens, w_f3[:, col:col + HY_WIDTH],
                                     start=True, stop=True)
                last.then_inc(filt_mm, 1)

            def spectrum(v0, src):
                for kt in range(2):
                    for rs in range(2):
                        v = v0 + 2 * kt + rs
                        if v - v0 >= 2:
                            pe.wait_ge(spec_freed, v - 1)
                        for odd in range(2):
                            for t in range(2):
                                hi, lo = (w[:, 2 * rs + odd, t, kt * P:(kt + 1) * P] for w in (dft_hi, dft_lo))
                                s_hi, s_lo = src(rs, 2 * odd + t)
                                last = mm3(ps[2 + 2 * rs + odd][:], hi, lo, s_hi, s_lo, t == 0, t == 1)
                        last.then_inc(spec_mm, 1)

            taps = lambda rs, t: (taps_hi[:, rs, t, :], taps_lo[:, rs, t, :])
            z_of = lambda rs, t: (zy_hi[:, t, :], zy_lo[:, t, :])

            def energy_sum(o):
                pe.wait_ge(energy_ready, (2 * TT - 1) * (o + 1))
                for c in range(CT):
                    last = pe.matmul(ps[7][:, o * CT + c:o * CT + c + 1], energy[:, c * P:(c + 1) * P], mean_of[:, 0:1],
                                     start=True, stop=True)
                last.then_inc(energy_mm, 1)

            def turn_z(o, tiles):
                for t in tiles:
                    if t >= 2:
                        pe.wait_ge(z_ready, o * TT + t - 1)
                    if o == 0 and t == 1:
                        pe.wait_ge(energy_eps, 1)
                    for c in range(CT):
                        last = pe.transpose(ps[6 + t % 2][:, c * P:(c + 1) * P],
                                            parts[o][:, c, t * P:(t + 1) * P], eye[:])
                    last.then_inc(zt_ready, 1)

            def inverse(o, kt):
                for rs in range(2):
                    pe.wait_ge(spec_ready, 4 * o + 2 * kt + rs + 1)
                    for c in range(CT):
                        cols = slice(c * P, (c + 1) * P)
                        for odd, mat in ((0, 4 + rs), (1, 1 + 2 * rs)):
                            a = 2 * rs + odd
                            first = kt == 0 and odd == 0 and rs == 0
                            last = mm3(ps[2 + c][:, odd * HALF:(odd + 1) * HALF],
                                       zy_hi[:, a, cols], zy_lo[:, a, cols],
                                       dft_hi[:, mat, kt, :], dft_lo[:, mat, kt, :],
                                       first, kt == 1 and rs == 1, skip_group_check=True)
                        if kt == 1 and rs == 1:
                            last.then_inc(inv_ready, 1)
                    if kt == 0:
                        last.then_inc(inv_mm, 1)

            pe.wait_ge(proj_freed, 2)
            first_pair(u0, DT)
            pe.wait_ge(ones_row, 1)
            pe.wait_ge(hid_ready, 2)
            pe.wait_ge(w_f3_ready, 1)
            filter_tile(0)
            filter_tile(1)
            for n in range(2, TT):
                project(n)
                filter_tile(n)
            project(TT)
            pe.wait_ge(dft_ready, 1)
            pe.wait_ge(taps_ready, TT)
            spectrum(0, taps)
            energy_sum(0)
            project(TT + 1)
            filter_tile(TT)
            filter_tile(TT + 1)
            project(TT + 2)
            filter_tile(TT + 2)
            filter_tile(TT + 3)
            project(TT + 3)
            pe.wait_ge(conv_ready, CT)
            pe.wait_ge(taps_ready, 2 * TT)
            spectrum(4, taps)
            energy_sum(1)

            def fill(o, part):
                for n in FILL[o][part]:
                    project(n)

            for o in range(HY_ORDER):
                if o:
                    pe.wait_ge(gated, CT)
                turn_z(o, (0, 1))
                fill(o, 0)
                turn_z(o, (2, 3))
                fill(o, 1)
                pe.wait_ge(z_ready, (o + 1) * TT)
                spectrum(8 + 4 * o, z_of)
                fill(o, 2)
                pe.wait_ge(spec_freed, 12 + 4 * o)
                inverse(o, 0)
                fill(o, 3)
                inverse(o, 1)
                fill(o, 4)

            def score(h):
                if h >= 2:
                    pe.wait_ge(scored, 2 * (h - 1))
                row = slice((h % 2) * HEAD_DIM, (h % 2 + 1) * HEAD_DIM)
                for b in range(BLOCKS):
                    q = qT[row, h // 2, b * P:(b + 1) * P]
                    bank, col = ps[(6, 2)[h % 2] + b // 2], (b % 2) * KEYS
                    if b < 3:
                        last = pe.matmul(bank[:, col:col + KEYS], q, kT[row, h // 2, b * P:(b + 2) * P],
                                         start=True, stop=True)
                    else:
                        pe.matmul(bank[:, col:col + P], q, kT[row, h // 2, 3 * P:4 * P], start=True, stop=True)
                        last = pe.matmul(bank[:, col + P:col + KEYS], q, kT[row, h // 2, 0:P],
                                         start=True, stop=True)
                    if b % 2:
                        last.then_inc(score_mm, 1)

            def turn_probs(h):
                for j in range(2):
                    pe.wait_ge(prob_ready, 2 * h + j + 1)
                    if h >= 1:
                        pe.wait_ge(pt_ready, 2 * (h - 1) + j + 1)
                    for n in range(4):
                        last = pe.transpose(ps[4 + j][:, n * P:(n + 1) * P],
                                            probs[:, h % 3, 2 * j + n // 2, (n % 2) * P:(n % 2 + 1) * P], eye[:])
                    last.then_inc(pt_mm, 1)

            def values(h):
                if h % 2 == 0 and h >= 4:
                    pe.wait_ge(ya_ready, h // 2 - 1)
                for b in range(BLOCKS):
                    if b % 2 == 0:
                        pe.wait_ge(pt_ready, 2 * h + b // 2 + 1)
                    out_ps = ps[(h // 2) % 2][(h % 2) * HEAD_DIM:(h % 2 + 1) * HEAD_DIM, b * P:(b + 1) * P]
                    for n in range(2):
                        col = (b % 2) * KEYS + n * P
                        last = pe.matmul(out_ps, v_sb[:, (b + n) % 4, h * HEAD_DIM:(h + 1) * HEAD_DIM],
                                         probsT[:, b // 2, col:col + P], start=n == 0, stop=n == 1)
                    if b % 2:
                        last.then_inc(pv_mm, 1)

            pe.wait_ge(qk_ready, CT + 1)
            score(0)
            project(6 * CT - 2)
            project(6 * CT - 1)
            pe.wait_ge(gated, 2 * CT)
            score(1)
            pe.wait_ge(vt_ready, CT)
            pe.wait_ge(scored, 2)
            pe.wait_ge(proj_freed, 6 * CT + 2)
            for g in range(TT):
                for c in range(CT):
                    last = pe.transpose(ps[V_BANK[g]][:, c * P:(c + 1) * P], vT[:, c, g * P:(g + 1) * P], eye[:])
                last.then_inc(v_mm, 1)
            pe.wait_ge(v_ready, TT - 1)
            for h in range(HEADS):
                if h + 2 < HEADS:
                    score(h + 2)
                turn_probs(h)
                if h == 0:
                    pe.wait_ge(v_ready, TT)
                values(h)

            ya_t = (lambda k: ya_hi[:, k, :], lambda k: ya_lo[:, k, :])
            yb_t = (lambda k: yb_hi[:, k, :], lambda k: yb_lo[:, k, :])
            with pe.Fori(0, 2) as i:
                for d in range(4):
                    b0 = 4 - 4 * (d % 2)
                    pe.wait_ge(m_made, i * 4 + (d + 1))
                    for m in range(3):
                        n = 3 * d + m
                        pe.wait_ge(unit_lo, i * 12 + (u0 + U_MIX + n + 1))
                        if m < 2:
                            last = unit_times(n % SLOTS, ps[b0 + m][:], *x_tile)
                        else:
                            pe.wait_ge(ya_ready, CT)
                            pe.wait_ge(yb_ready, CT)
                            unit_times(n % SLOTS, ps[b0 + 2][:], *ya_t, tiles=CT)
                            last = unit_times(n % SLOTS, ps[b0 + 3][:], *yb_t, tiles=CT, first=CT)
                        last.then_inc(ring_freed, 1)
            for d in range(DT):
                if d == 0:
                    pe.wait_ge(m_made, 2 + DT - 1)
                pe.wait_ge(res_freed, RESIDUAL_TILES + d + 1)
                pe.wait_ge(unit_lo, u0 + U_OUT + d + 1)
                for k in range(DT):
                    if d == 0:
                        pe.wait_ge(m_ready, k + 1)
                    if d == DT - 1 and k == 6:
                        early_sums(1)
                    w_hi, w_lo = tile_of(d % SLOTS, k)
                    last = mm3(ps[4 + d % 2][:], w_hi, w_lo, m_hi[:, k, :], m_lo[:, k, :], k == 0, k == DT - 1)
                last.then_inc(ring_freed, 1)
                if d == SHIFT_AFTER[1] - 1:
                    shift_sum(1)
            layer_norm(1)

            ffn_up(1, UNIT0["ffn2"], 2 * DT)
            ffn_down(1, 2 * RESIDUAL_TILES, UNIT0["ffn2"] + UP_UNITS)
            layer_norm(2)

        @block.scalar
        def _(act):
            def split_x(pairs):
                for q in pairs:
                    act.wait_ge(x_loaded[q], 16)
                    for d in (2 * q, 2 * q + 1):
                        act.activation(x_hi[:, d, :], y[:, d, :], ACT.Copy).then_inc(x_hi_ready, 1)

            def unit_hi_of(width, slot, raw_slot, nth_load, slots_taken):
                act.wait_ge(raw_loaded[raw_slot], nth_load * 16)
                act.wait_ge(ring_freed, slots_taken)
                act.activation(ring_hi[:, slot * UP_W:slot * UP_W + width], raw[:, raw_slot, 0:width],
                               ACT.Copy).then_inc(unit_hi, 1)

            def up_hi(phase, n, i=0):
                unit_hi_of(UP_W, n % SLOTS, n % 2, i * 2 + (UNIT0[phase] // 2 + n // 2 + 1),
                           i * 4 + (SLOT0[phase] + n + 1))

            def down_hi(phase, n, i=0):
                unit_hi_of(DOWN_W, 2 * (n % 2), n % 2, i + ((UNIT0[phase] + UP_UNITS) // 2 + n // 2 + 1),
                           i * 4 + (SLOT0[phase] + UP_UNITS + 2 * (n + 1)))

            mix_hi_done = [0]

            def mix_hi(n):
                while mix_hi_done[0] <= min(n, MIX_UNITS - 1):
                    up_hi("mix", mix_hi_done[0])
                    mix_hi_done[0] += 1

            def ffn_up(f):
                phase = ("ffn1", "ffn2")[f]

                def tile(j, p, i):
                    act.wait_ge(ring_freed, i * 4 + used(phase, 2 * j + 2))
                    act.activation(act_gate[p], ps[2 * p][:], ACT.Silu).then_inc(gate_ready, 1)
                    act.wait_ge(up_freed, i * 2 + (2 + f * FT + j + 1))
                    act.activation(h_hi[:, i * 2 + j, :], h_prod[p], ACT.Copy).then_inc(h_hi_ready, 1)

                with act.Fori(0, FT // 2 - 1) as i:
                    for p in range(2):
                        up_hi(phase, 2 * p + AHEAD, i)
                        up_hi(phase, 2 * p + AHEAD + 1, i)
                        tile(p, p, i)
                up_hi(phase, UP_UNITS - 1)
                tile(FT - 2, 0, 0)
                down_hi(phase, 0)
                tile(FT - 1, 1, 0)
                down_hi(phase, 1)
                if f == 0:
                    act.wait_ge(arg_ready, 1)
                    act.activation(hid1[:], arg[:], ACT.Sin).then_inc(hid_ready, 1)
                with act.Fori(0, DOWN_UNITS // 2 - 2) as i:
                    for s in range(2):
                        down_hi(phase, 2 + s, i)

            def layer_norm(n, last):
                for d in range(DT):
                    if d < SHIFT_AFTER[n]:
                        act.wait_ge(shifted, sum(SHIFT_AFTER[:n]) + d + 1)
                    else:
                        act.wait_ge(res_freed, 2 + n * DT + d + 1)
                    if d >= 2:
                        act.wait_ge(square_added, n * (DT - 2) + max(d - 2, 1))
                    act.activation(squares[:, d % 2, :], y[:, d, :], ACT.Square).then_inc(squared, 1)
                    if n == 0 and d == SHIFT_AFTER[n] - 1:
                        act.wait_ge(arg_ready, 2)
                        act.activation(hid[0:HID, :], arg[:], ACT.Sin).then_inc(hid_ready, 1)
                    if n != 1 and d in (SHIFT_AFTER[n] - 1, DT - 3):
                        down_hi(("ffn1", "ffn2")[n // 2], DOWN_UNITS - (2 if d < DT - 3 else 1))
                    if d == DT - 2:
                        act.activation(one[:], mean_of[:, 0:1], ACT.Sqrt)
                        if n == 0:
                            mix_hi(1)
                        if n == 1:
                            up_hi("ffn2", 0)
                            up_hi("ffn2", 1)
                act.wait_ge(var_eps, n + 1)
                act.activation(deviation[:], deviation[:], ACT.Sqrt, scale=1.0 / D_MODEL ** 2
                               ).then_inc(std_ready, 1)
                act.wait_ge(mean_mm, n + 1)
                act.activation(mean_left[:], MEAN[:], ACT.Copy).then_inc(mean_copied, 1)
                if n == 0:
                    mix_hi(2)
                if n == 1:
                    up_hi("ffn2", 2)
                for d in range(DT):
                    if n == 0 and d == 2:
                        mix_hi(3)
                    b = par[:, (2 * n + 1) * DT + d:(2 * n + 1) * DT + d + 1]
                    act.wait_ge(scaled, n * DT + d + 1)
                    if last:
                        act.activation(y[:, d, :], y[:, d, :], ACT.Identity, bias=b).then_inc(final_ready, 1)
                    else:
                        act.activation(x_hi[:, d, :], y[:, d, :], ACT.Identity, bias=b).then_inc(x_hi_ready, 1)

            up_hi("ffn1", 0)
            split_x((0,))
            up_hi("ffn1", 1)
            split_x((1, 2, 3))
            up_hi("ffn1", 2)
            ffn_up(0)
            act.wait_ge(small_loaded, 32)
            layer_norm(0, False)
            act.wait_ge(mixer_loaded, 48)
            act.activation(dft_hi[:], dft_raw[:], ACT.Copy).then_inc(dft_hi_ready, 1)

            act.wait_ge(mean_set, 3)

            def pad_part(n):
                part, c = n // CT, n % CT
                if n > 8:
                    act.wait_ge(conv_ready, n - 1)
                elif n >= 1:
                    act.wait_ge(conv_ready, n)
                act.wait_ge(ring_freed, used("mix", n + 1))
                act.activation(pad_of(n)[:, 1:SEQ + 1], ps[n % 2][:], ACT.Copy).then_inc(pad_ready, 1)
                act.activation(parts[part][:, c, :].rearrange("p (two s) -> p s two", two=2),
                               ps[n % 2][:].rearrange("p (s two) -> p s two", two=2), ACT.Identity,
                               scale=par[:, C_SW + 3 * CT + n:C_SW + 3 * CT + n + 1],
                               bias=par[:, C_SB + n:C_SB + n + 1]).then_inc(pad_ready, 1)
                mix_hi(n + AHEAD)
                act.wait_ge(pad_ready, 2 * n + 2)
                act.sem_inc(proj_freed, 1)

            def by_group(dst, bank):
                act.activation(dst[:, 0:P].rearrange("p (s r w) -> p s r w", s=2, w=8),
                               bank.rearrange("p (r s w) -> p s r w", s=8, w=8)[:, 0:8:7], ACT.Copy)
                return act.activation(dst[:, P:].rearrange("p (g r w) -> p g r w", g=3, w=KW),
                                      bank.rearrange("p (r w) -> p r w", w=GRID_W)[:, :, 8:56].rearrange(
                                          "p r (g w) -> p g r w", w=KW), ACT.Copy)

            def tap_hi(n):
                act.wait_ge(taps_made, n + 1)
                if n == TT:
                    act.wait_ge(spec_mm, 4)
                if n >= 2:
                    act.wait_ge(energy_ready, 2 * (n - 1) - 1 - (n - 2) // TT)
                act.activation(taps_hi[:, :, n % TT, :], tap_pm[n % 2][:], ACT.Copy).then_inc(taps_hi_ready, 1)
                act.activation(tap_sq[n % 2][:], tap_pm[n % 2][:], ACT.Square).then_inc(taps_hi_ready, 1)

            def spec_evac(v0):
                for v in range(v0, v0 + 4):
                    act.wait_ge(spec_mm, v + 1)
                    if v >= 1:
                        act.wait_ge(spec_freed, v)
                    act.activation(half_spec[:], ps[2 + 2 * (v % 2)][:], ACT.Copy).then_inc(spec_half, 1)

            for n in (0, 1):
                pad_part(n)
            for n in (0, 1):
                tap_hi(n)
            for n in (2, 3):
                pad_part(n)
                tap_hi(n)
            pad_part(TT)
            spec_evac(0)
            pad_part(TT + 1)
            tap_hi(TT)
            tap_hi(TT + 1)
            pad_part(TT + 2)
            tap_hi(TT + 2)
            tap_hi(TT + 3)
            pad_part(TT + 3)
            spec_evac(4)

            def product_hi(o, kt):
                for rs in range(2):
                    act.wait_ge(spec_made, 4 * o + 2 * kt + rs + 1)
                    if kt:
                        act.wait_ge(inv_mm, 2 * o + rs + 1)
                    act.activation(zy_hi[:, 2 * rs:2 * rs + 2, :], spec_z[:, kt, rs], ACT.Copy
                                   ).then_inc(spec_hi_ready, 1)

            def take_qk(n):
                m = n - 3 * CT
                mix_hi(n + AHEAD)
                act.wait_ge(ring_freed, used("mix", n + 1))
                if m < CT:
                    act.activation(qT[:, m, :].rearrange("p (b r w) -> p b r w", r=ROWS, w=KW),
                                   ps[n % 2][:].rearrange("p (r b w) -> p b r w", r=ROWS, w=KW),
                                   ACT.Copy).then_inc(qk_ready, 1)
                else:
                    by_group(kT[:, m - CT, :], ps[n % 2][:]).then_inc(qk_ready, 1)
                act.wait_ge(qk_ready, m + 1)
                act.sem_inc(proj_freed, 1)

            def take_v(n):
                c = n - 5 * CT
                mix_hi(n + AHEAD)
                act.wait_ge(ring_freed, used("mix", n + 1))
                by_group(vT[:, c, :], ps[n % 2][:]).then_inc(vt_ready, 1)
                act.wait_ge(vt_ready, c + 1)
                act.sem_inc(proj_freed, 1)

            def take(n):
                (pad_part if n < 3 * CT else take_qk if n < 5 * CT else take_v)(n)

            def z_hi(o, tiles):
                for t in tiles:
                    act.wait_ge(zt_ready, o * TT + t + 1)
                    act.activation(zy_hi[:, t, :], ps[6 + t % 2][:], ACT.Copy).then_inc(z_hi_ready, 1)

            for o in range(HY_ORDER):
                z_hi(o, (0, 1))
                take(FILL[o][0][0])
                z_hi(o, (2, 3))
                if o == 0:
                    act.wait_ge(energy_eps, 1)
                    act.activation(kernel_scale[:], kernel_scale[:], ACT.Sqrt).then_inc(energy_std, 1)
                take(FILL[o][1][0])
                spec_evac(8 + 4 * o)
                take(FILL[o][2][0])
                product_hi(o, 0)
                take(FILL[o][2][1])
                product_hi(o, 1)
                for n in FILL[o][3] + FILL[o][4]:
                    take(n)
            for c in range(CT):
                act.wait_ge(gated, CT + c + 1)
                act.activation(yb_hi[:, c, :], yb[:, c, :], ACT.Copy).then_inc(yb_hi_ready, 1)

            def exp_scores(h):
                act.wait_ge(max_ready, h + 1)
                for b in range(BLOCKS):
                    last = act.activation(probs[:, h % 3, b, :], probs[:, h % 3, b, :], ACT.Exp,
                                          bias=neg_max[:, h, b:b + 1], accum_out=row_sum[:, h, b:b + 1])
                    last.then_inc(exp_ready, 1)

            def turned_probs(h):
                for j in range(2):
                    act.wait_ge(pt_mm, 2 * h + j + 1)
                    if h >= 1:
                        act.wait_ge(pv_mm, 2 * (h - 1) + j + 1)
                    act.activation(probsT[:, j, :], ps[4 + j][:], ACT.Copy).then_inc(pt_ready, 1)

            by_block = lambda t, c: t[:, c, :].rearrange("p (r b w) -> p b r w", b=BLOCKS, w=KW)
            exp_scores(0)
            take(6 * CT - 2)
            take(6 * CT - 1)
            for g in range(TT):
                act.wait_ge(v_mm, g + 1)
                act.activation(v_sb[:, g, :], ps[V_BANK[g]][:], ACT.Copy).then_inc(v_ready, 1)
            exp_scores(1)
            mix_hi(U_MIX + 3)
            def ya_high(c):
                act.wait_ge(pv_mm, 4 * (c + 1))
                act.activation(by_block(ya_hi, c), ps[c % 2][:].rearrange(
                    "p (b r w) -> p b r w", b=BLOCKS, w=KW), ACT.Copy).then_inc(ya_hi_ready, 1)

            for h in range(HEADS):
                turned_probs(h)
                if h % 2 == 0 and h >= 2:
                    ya_high(h // 2 - 1)
                if h + 2 < HEADS:
                    exp_scores(h + 2)
            ya_high(CT - 1)

            for d in range(DT):
                mix_hi(U_MIX + 3 * d + 2 + AHEAD)
                act.wait_ge(ring_freed, used("mix", U_MIX + 3 * (d + 1)))
                b0 = 4 - 4 * (d % 2)
                for br, dst in ((0, gate_a), (1, gate_b)):
                    col = C_GATE + br * DT + d
                    last = act.activation(dst[:, d % 2, :], ps[b0 + br][:], ACT.Sigmoid, bias=par[:, col:col + 1])
                last.then_inc(gates_ready, 1)
                act.wait_ge(m_made, 2 + d + 1)
                act.activation(m_hi[:, d, :], gate_a[:, d % 2, :], ACT.Copy).then_inc(m_hi_ready, 1)
            mix_hi(MIX_UNITS - 1)
            layer_norm(1, False)
            ffn_up(1)
            layer_norm(2, True)

        @block.vector
        def _(dve):
            step = Steps(dve, dve_step)
            dve.memset(mean_of[:], 1.0 / D_MODEL).then_inc(mean_set, 1)
            dve.memset(hid[HID:HID + 1, :], 1.0).then_inc(ones_row, 1)
            dve.memset(u_pad[:, 0:1], 0.0).then_inc(mean_set, 1)
            dve.memset(u_pad[:, SEQ + 1:SEQ + 2], 0.0).then_inc(mean_set, 1)
            dve.sem_inc(up_freed, 2)
            dve.sem_inc(res_freed, 2)
            dve.sem_inc(m_made, 2)
            dve.sem_inc(proj_freed, 2)

            def ffn_up(f):
                with dve.Fori(0, FT // 2) as i:
                    for p in range(2):
                        dve.wait_ge(gate_ready, i * 2 + (f * FT + p + 1))
                        dve.tensor_tensor(h_prod[p], act_gate[p], ps[2 * p + 1][:], ALU.mult
                                          ).then_inc(up_freed, 1)
                        dve.wait_ge(h_hi_ready, i * 2 + (f * FT + p + 1))
                        dve.tensor_tensor(h_lo[:, i * 2 + p, :], h_prod[p], h_hi[:, i * 2 + p, :].bitcast(F32),
                                          ALU.subtract).then_inc(h_ready, 1)

            def residual(r0, scale, phase, slot0, slots):
                n = r0 // RESIDUAL_TILES
                S = SHIFT_AFTER[n]
                for d in range(DT):
                    if d < S:
                        dve.wait_ge(ring_freed, used(phase, slot0 + (d + 1) * slots))
                        dve.scalar_tensor_tensor(y[:, d, :], x_hi[:, d, :].bitcast(F32), scale,
                                                 ps[4 + d % 2][:], ALU.mult, ALU.add).then_inc(res_freed, 1)
                        dve.wait_ge(res_freed, 2 + r0 + d + 1)
                        step.then(dve.scalar_tensor_tensor(y[:, d, :], x_lo[:, d, :].bitcast(F32), scale,
                                                           y[:, d, :], ALU.mult, ALU.add))
                        if d == 1:
                            step.then(dve.tensor_tensor(y_sum[:], y[:, 0, :], y[:, 1, :], ALU.add))
                        elif 1 < d < SHIFT_TILES:
                            last = dve.tensor_tensor(y_sum[:], y_sum[:], y[:, d, :], ALU.add)
                            if d < SHIFT_TILES - 1:
                                step.then(last)
                            else:
                                last.then_inc(y_summed, 1)
                    if d == S - 1:
                        dve.wait_ge(shift_mm, n + 1)
                        step.then(dve.tensor_scalar(shift[:], MEAN[:], DT / SHIFT_TILES, None, ALU.mult))
                        for e in range(S, DT):
                            dve.scalar_tensor_tensor(y[:, e, :], x_hi[:, e, :].bitcast(F32), scale, shift[:],
                                                     ALU.mult, ALU.subtract)
                        for e in range(S):
                            dve.tensor_tensor(y[:, e, :], y[:, e, :], shift[:], ALU.subtract).then_inc(shifted, 1)
                        dve.wait_ge(shifted, sum(SHIFT_AFTER[:n + 1]))
                        for e in range(S, DT):
                            last = dve.scalar_tensor_tensor(y[:, e, :], x_lo[:, e, :].bitcast(F32), scale,
                                                            y[:, e, :], ALU.mult, ALU.add)
                        step.then(last)
                        if n == 0:
                            sin_argument(1)
                    if d >= S:
                        dve.wait_ge(ring_freed, used(phase, slot0 + (d + 1) * slots))
                        dve.tensor_tensor(y[:, d, :], y[:, d, :], ps[4 + d % 2][:], ALU.add).then_inc(res_freed, 1)
                        if d == S:
                            step.then(dve.tensor_tensor(y_sum[:], y[:, 0, :], y[:, 1, :], ALU.add))
                            for e in range(2, S):
                                step.then(dve.tensor_tensor(y_sum[:], y_sum[:], y[:, e, :], ALU.add))
                        if d < DT - 1:
                            dve.wait_ge(res_freed, 2 + r0 + d + 1)
                            last = dve.tensor_tensor(y_sum[:], y_sum[:], y[:, d, :], ALU.add)
                            if d == DT - 2:
                                last.then_inc(c_summed, 1)
                            else:
                                step.then(last)

            def layer_norm(n, eps, last):
                def centre(d):
                    step.then(dve.tensor_tensor(y[:, d, :], y[:, d, :], mean_left[:], ALU.subtract))

                def diagonal(dst, col, ready):
                    for j in range(TT):
                        dve.tensor_scalar(dst[:, j, :], eye[:], col[:, j:j + 1], None, ALU.mult
                                          ).then_inc(ready, 1)

                dve.wait_ge(mean_col_ready, n + 1)
                step.then(dve.tensor_scalar(mean_col[:], MEAN_COL[:, 0:TT], float(D_MODEL), None, ALU.mult))
                diagonal(mean_diag, mean_col, mean_diag_ready)
                step.then(dve.scalar_tensor_tensor(mean_sq[:], mean_col[:], 1.0 / D_MODEL ** 2, mean_col[:],
                                                   ALU.mult, ALU.mult))
                dve.wait_ge(square_col_ready, n + 1)
                dve.scalar_tensor_tensor(deviation[:], SQUARE_COL[:, 0:TT], eps, mean_sq[:], ALU.add, ALU.subtract
                                         ).then_inc(var_eps, 1)
                dve.wait_ge(std_ready, n + 1)
                step.then(dve.reciprocal(deviation[:], deviation[:]))
                diagonal(rstd_diag, deviation, rstd_diag_ready)
                dve.wait_ge(mean_copied, n + 1)

                def low(d):
                    dve.wait_ge(x_hi_ready, (n + 1) * DT + d + 1)
                    b = par[:, (2 * n + 1) * DT + d:(2 * n + 1) * DT + d + 1]
                    dve.scalar_tensor_tensor(x_lo[:, d, :], y[:, d, :], b, x_hi[:, d, :].bitcast(F32),
                                             ALU.add, ALU.subtract).then_inc(x_ready, 1)

                for d in range(DVE_CENTRES[n]):
                    centre(d)
                for d in range(DT):
                    if d >= DVE_CENTRES[n]:
                        dve.wait_ge(centred, n * DT - sum(DVE_CENTRES[:n + 1]) + d + 1)
                    if d == 0:
                        dve.wait_ge(rstd_mm, n + 1)
                    g = par[:, 2 * n * DT + d:2 * n * DT + d + 1]
                    dve.scalar_tensor_tensor(y[:, d, :], y[:, d, :], g, RSTD[:], ALU.mult, ALU.mult
                                             ).then_inc(scaled, 1)
                    if d >= 1 and not last:
                        low(d - 1)
                if not last:
                    low(DT - 1)

            def sin_argument(n):
                dve.wait_ge(filt_loaded, 64)
                dve.wait_ge(hid_mm, n + 1)
                step.then(dve.tensor_scalar(arg[:], ps[7][0:HID, :], f_cols[:, n:n + 1], f_cols[:, 2:3],
                                            ALU.add, ALU.mult))
                step.then(dve.tensor_scalar(turns[:], arg[:], float(1 / (2 * np.pi)), MAGIC, ALU.mult, ALU.add))
                step.then(dve.tensor_scalar(turns[:], turns[:], MAGIC, None, ALU.subtract))
                for part in TWO_PI_PARTS:
                    step.then(dve.scalar_tensor_tensor(arg[:], turns[:], -part, arg[:], ALU.mult, ALU.add))
                pi = 3.1415925
                dve.tensor_scalar(arg[:], arg[:], pi, -pi, ALU.min, ALU.max).then_inc(arg_ready, 1)

            for d in range(DT):
                if d in (0, 2):
                    n = d // 2
                    there = slice(n * UP_W, (n + 1) * UP_W)
                    dve.wait_ge(unit_hi, n + 1)
                    dve.tensor_tensor(ring_lo[:, there], raw[:, n, 0:UP_W], ring_hi[:, there].bitcast(F32),
                                      ALU.subtract).then_inc(unit_lo, 1)
                dve.wait_ge(x_hi_ready, d + 1)
                dve.tensor_tensor(x_lo[:, d, :], y[:, d, :], x_hi[:, d, :].bitcast(F32), ALU.subtract
                                  ).then_inc(x_ready, 1)
            ffn_up(0)
            sin_argument(0)
            residual(0, 2 * ALPHA, "ffn1", UP_UNITS, 4)
            layer_norm(0, 4 * LN_EPS, False)

            def short_conv(n):
                part, c = n // CT, n % CT
                dst = parts[part][:, c, :].rearrange("p (two s) -> p s two", two=2)
                dve.wait_ge(pad_ready, 2 * n + 2)
                for tap in (0, 2):
                    col = C_SW + tap * 3 * CT + n
                    src = pad_of(n)[:, tap:tap + SEQ].rearrange("p (s two) -> p s two", two=2)
                    last = dve.scalar_tensor_tensor(dst, src, par[:, col:col + 1], dst, ALU.mult, ALU.add)
                    if tap == 0:
                        step.then(last)
                last.then_inc(conv_ready, 1)

            def sum_filters():
                dve.wait_ge(mixer_loaded, 48)
                w = HY_ORDER * HY_WIDTH
                step.then(dve.tensor_tensor(w_f3[:, 0:w], w_f3[:, 0:w], w_f3[:, w:], ALU.add))
                dve.scalar_tensor_tensor(w_f3[:, w:], w_f3[:, w:], -2.0, w_f3[:, 0:w], ALU.mult, ALU.add
                                         ).then_inc(w_f3_ready, 1)

            def tap_tile(n):
                t, pm = n % TT, tap_pm[n % 2]
                dve.wait_ge(filt_mm, n + 1)
                b0 = 2 + 2 * (n % 2)
                if n >= 2:
                    dve.wait_ge(taps_ready, n - 1)
                    dve.wait_ge(taps_hi_ready, 2 * (n - 1))
                dve.tensor_tensor(pm[:, 0, :], decay_sb[:, t, :], ps[b0][:], ALU.mult)
                last = dve.tensor_tensor(pm[:, 1, :], decay_sb[:, t, :], ps[b0 + 1][:], ALU.mult)
                if t == 0:
                    step.then(last)
                    step.then(dve.tensor_tensor(pm[0:1, 0, :], pm[0:1, 0, :], pm[0:1, 1, :], ALU.add))
                    step.then(dve.tensor_scalar(pm[0:1, 1, :], pm[0:1, 0, :], 0.5, None, ALU.mult))
                    last = dve.tensor_scalar(pm[0:1, 0, :], pm[0:1, 0, :], 0.5, None, ALU.mult)
                last.then_inc(taps_made, 1)

            def tap_low(n):
                dve.wait_ge(taps_hi_ready, 2 * n + 1)
                dve.tensor_tensor(taps_lo[:, :, n % TT, :], tap_pm[n % 2][:],
                                  taps_hi[:, :, n % TT, :].bitcast(F32), ALU.subtract).then_inc(taps_ready, 1)

            def kernel_energy():
                dve.wait_ge(energy_mm, 2)
                dve.tensor_scalar(kernel_scale[:].rearrange("p o c -> p (o c)"), ps[7][:, 0:HY_ORDER * CT],
                                  float(D_MODEL / 2 * SEQ ** 2), 1e-12 * SEQ ** 2, ALU.mult, ALU.add
                                  ).then_inc(energy_eps, 1)

            def spec_evac(v0, dst, steps=range(4)):
                for v in (v0 + n for n in steps):
                    kt, rs = (v - v0) // 2, v % 2
                    dve.wait_ge(spec_half, v + 1)
                    odd = ps[3 + 2 * rs][:]
                    dve.tensor_tensor(dst[:, kt, rs, 0, :], half_spec[:], odd, ALU.add)
                    if rs == 0:
                        last = dve.tensor_tensor(dst[:, kt, rs, 1, :], half_spec[:], odd, ALU.subtract)
                    else:
                        last = dve.tensor_tensor(dst[:, kt, rs, 1, :], odd, half_spec[:], ALU.subtract)
                    last.then_inc(spec_freed, 1)

            def product(o, kt):
                def low(rs):
                    dve.wait_ge(spec_hi_ready, 4 * o + 2 * kt + rs + 1)
                    part = slice(2 * rs, 2 * rs + 2)
                    dve.tensor_tensor(zy_lo[:, part, :], spec_z[:, kt, rs], zy_hi[:, part, :].bitcast(F32),
                                      ALU.subtract).then_inc(spec_ready, 1)

                zr, zs = spec_z[:, kt, 0], spec_z[:, kt, 1]
                kr, ks = spec_k[o][:, kt, 0], spec_k[o][:, kt, 1]
                if kt == 0:
                    dve.wait_ge(spec_freed, 12 + 4 * o)
                step.then(dve.tensor_tensor(prod[0][:], zr, kr, ALU.mult))
                step.then(dve.tensor_tensor(prod[2][:], zr, ks, ALU.mult))
                for rs, src in ((0, prod[0]), (1, prod[2])):
                    dve.wait_ge(sin_products, 4 * o + 2 * kt + rs + 1)
                    if rs == 0:
                        step.then(dve.tensor_tensor(prod[0][:], prod[0][:], prod[1][:], ALU.subtract))
                    else:
                        step.then(dve.tensor_tensor(prod[2][:], prod[2][:], zs, ALU.add))
                    if rs == 1:
                        low(0)
                    for odd in range(2):
                        op = ALU.add if odd == rs else ALU.subtract
                        last = dve.tensor_tensor(spec_z[:, kt, rs, odd, :], src[:, 0, :], src[:, 1, :], op)
                    last.then_inc(spec_made, 1)
                low(1)

            def gate(o, c):
                z = parts[o][:, c, :]
                col = C_HB + o * CT + c
                step.then(dve.tensor_scalar(z, z, par[:, col:col + 1], None, ALU.mult))
                dve.wait_ge(inv_ready, o * CT + c + 1)
                step.then(dve.scalar_tensor_tensor(z, ps[2 + c][:], kernel_scale[:, o, c:c + 1], z,
                                                   ALU.mult, ALU.add))
                if o == 0:
                    dve.tensor_tensor(z1[:, c, :], z, z1[:, c, :], ALU.mult).then_inc(gated, 1)
                else:
                    last = dve.tensor_tensor(yb[:, c, :].rearrange("p (s two) -> p two s", two=2),
                                             z.rearrange("p (two s) -> p two s", two=2),
                                             part2[:, c, :].rearrange("p (two s) -> p two s", two=2), ALU.mult)
                    last.then_inc(gated, 1)

            sum_filters()
            for n in (0, 1):
                short_conv(n)
                tap_tile(n)
            for n in (0, 1):
                tap_low(n)
            for n in (2, 3):
                tap_tile(n)
                short_conv(n)
                tap_low(n)
            short_conv(TT)
            spec_evac(0, spec_k[0])
            short_conv(TT + 1)
            tap_tile(TT)
            tap_tile(TT + 1)
            tap_low(TT)
            tap_low(TT + 1)
            tap_tile(TT + 2)
            short_conv(TT + 2)
            tap_tile(TT + 3)
            dve.memset(u_pad1[:, 0:1], 0.0)
            step.then(dve.memset(u_pad1[:, SEQ + 1:SEQ + 2], 0.0))
            tap_low(TT + 2)
            tap_low(TT + 3)
            short_conv(TT + 3)
            dve.wait_ge(energy_ready, HY_ORDER * (2 * TT - 1))
            spec_evac(4, spec_k[1], range(3))
            kernel_energy()
            spec_evac(4, spec_k[1], (3,))

            def z_low(o, tiles):
                for t in tiles:
                    dve.wait_ge(z_hi_ready, o * TT + t + 1)
                    dve.tensor_tensor(zy_lo[:, t, :], ps[6 + t % 2][:], zy_hi[:, t, :].bitcast(F32),
                                      ALU.subtract).then_inc(z_ready, 1)

            for o in range(HY_ORDER):
                z_low(o, (0, 1))
                if o == 0:
                    short_conv(8)
                z_low(o, (2, 3))
                if o == 0:
                    short_conv(9)
                    dve.wait_ge(energy_std, 1)
                    step.then(dve.reciprocal(kernel_scale[:], kernel_scale[:]))
                spec_evac(8 + 4 * o, spec_z)
                product(o, 0)
                product(o, 1)
                if o == 0:
                    short_conv(10)
                    short_conv(11)
                for c in range(CT):
                    gate(o, c)

            by_block = lambda t, c: t[:, c, :].rearrange("p (r b w) -> p b r w", b=BLOCKS, w=KW)

            def softmax_front(h):
                dve.wait_ge(bias_ready, h + 1)
                if h >= 3:
                    dve.wait_ge(pt_mm, 2 * (h - 2))
                for j in range(2):
                    dve.wait_ge(score_mm, 2 * h + j + 1)
                    dve.scalar_tensor_tensor(probs[:, h % 3, 2 * j:2 * j + 2, :].rearrange("p a k -> p (a k)"),
                                             ps[(6, 2)[h % 2] + j][:], HEAD_DIM ** -0.5,
                                             bias_sb[:, h % 2, j:j + 2, :].rearrange("p a k -> p (a k)"),
                                             ALU.mult, ALU.add).then_inc(scored, 1)
                dve.wait_ge(scored, 2 * h + 2)
                dve.tensor_reduce(neg_max[:, h, :], probs[:, h % 3], AX.X, ALU.max, negate=True
                                  ).then_inc(max_ready, 1)

            def softmax_back(h):
                dve.wait_ge(exp_ready, BLOCKS * (h + 1))
                step.then(dve.reciprocal(row_inv[:, h, :], row_sum[:, h, :]))
                for b in range(BLOCKS):
                    last = dve.tensor_scalar(probs[:, h % 3, b, :], probs[:, h % 3, b, :],
                                             row_inv[:, h, b:b + 1], None, ALU.mult)
                    if b % 2:
                        last.then_inc(prob_ready, 1)

            def ya_low(c):
                dve.wait_ge(ya_hi_ready, c + 1)
                dve.tensor_tensor(by_block(ya_lo, c), ps[c % 2][:].rearrange(
                    "p (b r w) -> p b r w", b=BLOCKS, w=KW), by_block(ya_hi, c).bitcast(F32),
                    ALU.subtract).then_inc(ya_ready, 1)

            for c in range(CT):
                dve.wait_ge(yb_hi_ready, c + 1)
                dve.tensor_tensor(yb_lo[:, c, :], yb[:, c, :], yb_hi[:, c, :].bitcast(F32), ALU.subtract
                                  ).then_inc(yb_ready, 1)
            dve.wait_ge(yb_ready, CT)
            softmax_front(0)
            softmax_front(1)
            softmax_back(0)
            for h in range(HEADS):
                if h + 2 < HEADS:
                    softmax_front(h + 2)
                if h + 1 < HEADS:
                    softmax_back(h + 1)
                if h % 2 == 0 and h >= 2:
                    ya_low(h // 2 - 1)
            ya_low(CT - 1)

            for d in range(DT):
                s, b0 = d % 2, 4 - 4 * (d % 2)
                dve.wait_ge(gates_ready, d + 1)
                dve.tensor_tensor(gate_a[:, s, :], gate_a[:, s, :], ps[b0 + 2][:], ALU.mult)
                step.then(dve.tensor_tensor(gate_b[:, s, :], gate_b[:, s, :], ps[b0 + 3][:], ALU.mult))
                dve.tensor_tensor(gate_a[:, s, :], gate_a[:, s, :], gate_b[:, s, :], ALU.add).then_inc(m_made, 1)
                dve.wait_ge(m_hi_ready, d + 1)
                dve.tensor_tensor(m_lo[:, d, :], gate_a[:, s, :], m_hi[:, d, :].bitcast(F32), ALU.subtract
                                  ).then_inc(m_ready, 1)
            residual(RESIDUAL_TILES, ALPHA, "mix", U_OUT, 1)
            layer_norm(1, LN_EPS, False)
            ffn_up(1)
            residual(2 * RESIDUAL_TILES, 2 * ALPHA, "ffn2", UP_UNITS, 4)
            layer_norm(2, 4 * LN_EPS, True)


def _dft_tables():
    k = np.arange(HALF)[None, :]
    s = np.arange(HALF)[:, None]
    def angle(t):
        return np.pi * (((2 * k + 1) * t) % (4 * SEQ)) / (2 * SEQ)
    ce, se = np.cos(angle(2 * s)), np.sin(angle(2 * s))
    co, so = np.cos(angle(2 * s + 1)), np.sin(angle(2 * s + 1))
    tables = np.stack([ce, co, se, so, ce.T, se.T]).astype(np.float32)
    return np.ascontiguousarray(tables.reshape(6, 2, P, HALF).transpose(2, 0, 1, 3))


def _split_tokens():
    return np.concatenate([np.arange(0, SEQ, 2), np.arange(1, SEQ, 2)])


def _filter_features():
    t = np.linspace(0.0, 1.0, SEQ, dtype=np.float32)[:, None]
    bands = (EMB - 1) // 2
    w = (np.float32(2.0 * np.pi / SEQ) * np.arange(SEQ, dtype=np.float32))[:, None]
    f = np.linspace(1e-4, bands - 1, bands, dtype=np.float32)[None, :]
    z = np.concatenate([t, np.cos(f * w), -np.sin(f * w)], axis=-1).astype(np.float32)
    return np.ascontiguousarray(z[_split_tokens()].T)


def _decay():
    t = np.linspace(0.0, 1.0, SEQ, dtype=np.float32)[:, None]
    lo, hi = np.log(1e-2) / 1.5, np.log(1e-2) / 0.3
    deltas = np.abs(np.linspace(lo, hi, HY_WIDTH, dtype=np.float32))
    d = np.exp(-t * deltas).astype(np.float32)[_split_tokens()]
    return np.ascontiguousarray(d.reshape(TT, P, HY_WIDTH).transpose(1, 0, 2))


def _window_mask():
    cq = np.arange(P) % KW
    out = []
    for b, first, second in ((0, (0, 56), (8, 16)), (1, (8, 16), (24, 32)), (3, (40, 48), (0, 56))):
        start = np.clip(KW * b + cq - KW // 2, 0, GRID_W - KW)[:, None, None]
        for halves in (first, second):
            cols = np.concatenate([c0 + np.arange(8) for c0 in halves])
            if halves == (0, 56):
                cols = np.stack([np.broadcast_to(cols[i:i + 8], (ROWS, 8)) for i in (0, 8)])[None]
                cols = cols.reshape(1, 2 * ROWS, 8)
            else:
                cols = np.broadcast_to(cols, (1, ROWS, KW))
            ok = (cols >= start) & (cols < start + KW)
            out.append(np.where(ok, 0.0, MASKED).reshape(P, 1, P))
    return np.ascontiguousarray(np.concatenate(out, axis=1).reshape(P, 3, KEYS).astype(np.float32))


def _col_tiles(w, first, n):
    kt = w.shape[0] // P
    t = w[:, first:first + n * P].reshape(kt, P, n, P)
    return np.ascontiguousarray(t.transpose(2, 1, 0, 3)).reshape(n, P, kt * P)


def _up_units(w1, w3):
    return np.ascontiguousarray(np.stack([_col_tiles(w1, 0, FT), _col_tiles(w3, 0, FT)], axis=1)
                                ).reshape(UP_UNITS, P, UP_W)


def _down_units(w2):
    t = w2.reshape(2, DOWN_K, P, DT, P).transpose(3, 0, 2, 1, 4)
    return np.ascontiguousarray(t).reshape(DOWN_UNITS, P, DOWN_W)


def _mixer_units(w_in, w_pa, w_pb, w_out):
    a_w, h_w = 3 * HEADS * HEAD_DIM, 3 * HY_WIDTH
    ga, gb = _col_tiles(w_in, a_w + h_w, DT), _col_tiles(w_in, a_w + h_w + D_MODEL, DT)
    pab = np.concatenate([_col_tiles(w_pa, 0, DT), _col_tiles(w_pb, 0, DT)], axis=2)
    gates = np.stack([ga, gb, pab], axis=1).reshape(3 * DT, P, UP_W)
    return np.ascontiguousarray(np.concatenate([
        _col_tiles(w_in, a_w, 3 * CT), _col_tiles(w_in, 0, CT), _col_tiles(w_in, 512, CT),
        _col_tiles(w_in, 1024, CT), gates,
        _col_tiles(w_out, 0, DT)], axis=0))


def _bias_segments(rpb):
    flat = np.pad(rpb.reshape(HEADS, -1), ((0, 0), (8, 8)))
    out = np.empty((P, HEADS, SEG), np.float32)
    for rq in range(ROWS):
        for cq in range(KW):
            a = 8 + (KH - 1 - rq) * (2 * KW - 1) + (7 - cq)
            out[rq * KW + cq] = flat[:, a:a + SEG]
    return out


def _columns(v):
    return np.asarray(v).reshape(-1, P).T


def kernel(**inputs):
    import concourse.bacc as bacc
    from concourse.bass_utils import run_bass_kernel_spmd

    a = {k: np.asarray(v)[0] for k, v in inputs.items()}
    xT = np.ascontiguousarray(a["x"].T.reshape(DT, P, SEQ).transpose(1, 0, 2))
    arrays = {
        "in_xT": xT,
        "in_params": np.ascontiguousarray(np.concatenate(
            [_columns(a[n]) for n in ("ln1_g", "ln1_b", "ln2_g", "ln2_b", "ln3_g", "ln3_b", "b_gate",
                                      "hy_short_w", "hy_short_b", "hy_bias")], axis=1)),
        "in_up1": _up_units(a["ffn1_w1"], a["ffn1_w3"]),
        "in_down1": _down_units(a["ffn1_w2"]),
        "in_mix": _mixer_units(a["w_in"], a["w_pa"], a["w_pb"], a["w_out"]),
        "in_up2": _up_units(a["ffn2_w1"], a["ffn2_w3"]),
        "in_down2": _down_units(a["ffn2_w2"]),
        "in_eye": np.eye(P, dtype=np.float32),
        "in_dft": _dft_tables(),
        "in_feat": _filter_features(),
        "in_filt1": np.ascontiguousarray(a["hy_filt_w1"]),
        "in_filt2": np.ascontiguousarray(a["hy_filt_w2"]),
        "in_filt_cols": np.ascontiguousarray(np.stack([a["hy_filt_b1"], a["hy_filt_b2"], a["hy_filt_freq"]], 1)),
        "in_filt3": np.concatenate([a["hy_filt_w3"], a["hy_filt_b3"][None]], axis=0),
        "in_decay": _decay(),
        "in_seg": _bias_segments(a["na_rpb"]),
        "in_mask": _window_mask(),
    }
    nc = bacc.Bacc("TRN2", target_bir_lowering=False, num_devices=1)
    args = [nc.dram_tensor(n, v.shape, mybir.dt.from_np(v.dtype), kind="ExternalInput").ap()
            for n, v in arrays.items()]
    args.append(nc.dram_tensor("out_yT", (P, DT, SEQ), F32, kind="ExternalOutput").ap())
    build(nc, *args)
    got = run_bass_kernel_spmd(nc, [arrays], core_ids=[0]).results[0]["out_yT"]
    return np.ascontiguousarray(np.asarray(got).transpose(1, 0, 2).reshape(D_MODEL, SEQ).T)[None]
```
